# Optimizing a Trainium2 kernel written in Bass

```python
import math
import jax, jax.numpy as jnp
from jax import lax
import numpy as np

D_MODEL = 2048
BATCH = 1
SEQ = 256
DEPTH = 1

MIX_WIDTH = D_MODEL
ATTN_WIDTH = MIX_WIDTH // 2
SSM_WIDTH = MIX_WIDTH - ATTN_WIDTH
ATTN_HEAD_DIM = 128
ATTN_HEADS = ATTN_WIDTH // ATTN_HEAD_DIM
MOBA_BLOCK = 256
MOBA_TOPK = 3
Q_CHUNK = 32
SSM_HEAD_DIM = 64
SSM_HEADS = SSM_WIDTH // SSM_HEAD_DIM
SSM_GROUPS = 2
SSM_HEADS_PER_GROUP = SSM_HEADS // SSM_GROUPS
SSM_STATE = 128
SSM_CONV = 4
SSD_CHUNK = 128
XBC_WIDTH = SSM_WIDTH + 2 * SSM_GROUPS * SSM_STATE
IN_COLS = 3 * ATTN_WIDTH + SSM_WIDTH + XBC_WIDTH + SSM_HEADS
SPLIT_POINTS = (ATTN_WIDTH, 2 * ATTN_WIDTH, 3 * ATTN_WIDTH,
                3 * ATTN_WIDTH + SSM_WIDTH, 3 * ATTN_WIDTH + SSM_WIDTH + XBC_WIDTH)
D_FF = 5632
FFN_CONV = 3
EPS = 1e-6


def rms_norm(x, w):
    xf = x.astype(jnp.float32)
    y = xf * lax.rsqrt(jnp.mean(xf * xf, axis=-1, keepdims=True) + EPS)
    return (y * w.astype(jnp.float32)).astype(x.dtype)

def causal_dwconv(u, w, bias):
    k_width = w.shape[0]
    s = u.shape[1]
    up = jnp.pad(u, ((0, 0), (k_width - 1, 0), (0, 0)))
    out = bias + up[:, 0:s] * w[0]
    for j in range(1, k_width):
        out = out + up[:, j:j + s] * w[j]
    return out

def moba_attention(q, k, v):
    b, h, s, dh = q.shape
    nb = -(-s // MOBA_BLOCK)
    pad = nb * MOBA_BLOCK - s
    kb = jnp.pad(k, ((0, 0), (0, 0), (0, pad), (0, 0))).reshape(b, h, nb, MOBA_BLOCK, dh)
    vb = jnp.pad(v, ((0, 0), (0, 0), (0, pad), (0, 0))).reshape(b, h, nb, MOBA_BLOCK, dh)
    k_mean = jnp.mean(kb, axis=3)
    n_sel = min(MOBA_TOPK, nb - 1)
    scale = dh ** -0.5
    blk_ids = jnp.arange(nb, dtype=jnp.int32)
    key_off = jnp.arange(MOBA_BLOCK, dtype=jnp.int32)
    gather_blocks = jax.vmap(jax.vmap(lambda blocks, idx: blocks[idx]))
    nq = s // Q_CHUNK
    q_chunks = q.reshape(b, h, nq, Q_CHUNK, dh).transpose(2, 0, 1, 3, 4)

    def chunk_attend(args):
        qc, c = args
        q_pos = c * Q_CHUNK + jnp.arange(Q_CHUNK, dtype=jnp.int32)
        own = (c * Q_CHUNK) // MOBA_BLOCK
        k_own = lax.dynamic_index_in_dim(kb, own, axis=2, keepdims=False)
        v_own = lax.dynamic_index_in_dim(vb, own, axis=2, keepdims=False)
        k_pos = own * MOBA_BLOCK + key_off
        s_own = jnp.einsum('bhqd,bhkd->bhqk', qc, k_own).astype(jnp.float32) * scale
        s_own = jnp.where(k_pos[None, :] <= q_pos[:, None], s_own, -jnp.inf)
        if n_sel == 0:
            p_own = jax.nn.softmax(s_own, axis=-1).astype(v.dtype)
            return jnp.einsum('bhqk,bhkd->bhqd', p_own, v_own)
        gate = jnp.einsum('bhqd,bhnd->bhqn', qc, k_mean).astype(jnp.float32)
        gate = jnp.where(blk_ids < own, gate, -jnp.inf)
        _, sel = lax.top_k(gate, n_sel)
        valid = sel < own
        k_sel = gather_blocks(kb, sel)
        v_sel = gather_blocks(vb, sel)
        s_sel = jnp.einsum('bhqd,bhqjkd->bhqjk', qc, k_sel).astype(jnp.float32) * scale
        s_sel = jnp.where(valid[..., None], s_sel, -jnp.inf).reshape(b, h, Q_CHUNK, n_sel * MOBA_BLOCK)
        p = jax.nn.softmax(jnp.concatenate([s_sel, s_own], axis=-1), axis=-1).astype(v.dtype)
        p_sel = p[..., :n_sel * MOBA_BLOCK].reshape(b, h, Q_CHUNK, n_sel, MOBA_BLOCK)
        p_own = p[..., n_sel * MOBA_BLOCK:]
        return (jnp.einsum('bhqjk,bhqjkd->bhqd', p_sel, v_sel)
                + jnp.einsum('bhqk,bhkd->bhqd', p_own, v_own))

    out = lax.map(chunk_attend, (q_chunks, jnp.arange(nq, dtype=jnp.int32)))
    return out.transpose(1, 2, 0, 3, 4).reshape(b, h, s, dh)

def ssd_chunked_scan(xs, dt, a, bm, cm):
    b, s, g, r, p = xs.shape
    n = bm.shape[-1]
    nc = s // SSD_CHUNK
    L = SSD_CHUNK
    log_a = (dt * a).reshape(b, nc, L, g, r).transpose(0, 3, 4, 1, 2)
    xdt = (xs * dt[..., None]).reshape(b, nc, L, g, r, p)
    bc = bm.reshape(b, nc, L, g, n)
    cc = cm.reshape(b, nc, L, g, n)
    a_cum = jnp.cumsum(log_a, axis=-1)
    tril = jnp.tril(jnp.ones((L, L), dtype=bool))
    seg = a_cum[..., :, None] - a_cum[..., None, :]
    decay = jnp.where(tril, jnp.exp(jnp.where(tril, seg, 0.0)), 0.0)
    cb = jnp.einsum('bclgn,bcsgn->bgcls', cc, bc)
    y_diag = jnp.einsum('bgrcls,bcsgrp->bclgrp', cb[:, :, None] * decay, xdt)
    decay_to_end = jnp.exp(a_cum[..., -1:] - a_cum)
    chunk_states = jnp.einsum('bclgn,bgrcl,bclgrp->cbgrpn', bc, decay_to_end, xdt)
    chunk_decay = jnp.exp(a_cum[..., -1]).transpose(3, 0, 1, 2)

    def carry_state(h, inputs):
        st, dec = inputs
        return h * dec[..., None, None] + st, h

    h0 = jnp.zeros((b, g, r, p, n), xs.dtype)
    _, h_in = lax.scan(carry_state, h0, (chunk_states, chunk_decay))
    y_off = jnp.einsum('bclgn,cbgrpn,bgrcl->bclgrp', cc, h_in, jnp.exp(a_cum))
    return (y_diag + y_off).reshape(b, s, g, r, p)

def hybrid_layer(x, norm1_w, w_in, q_norm_w, k_norm_w, ssm_conv_w, ssm_conv_b, dt_bias, a_log,
                 d_skip, ssm_norm_w, w_out, norm2_w, w_up, ffn_conv_w, ffn_conv_b, w_down):
    b, s, _ = x.shape
    h = rms_norm(x, norm1_w)
    proj = h @ w_in
    q, k, v, z, xbc, dt_raw = jnp.split(proj, SPLIT_POINTS, axis=-1)

    q = rms_norm(q.reshape(b, s, ATTN_HEADS, ATTN_HEAD_DIM), q_norm_w).transpose(0, 2, 1, 3)
    k = rms_norm(k.reshape(b, s, ATTN_HEADS, ATTN_HEAD_DIM), k_norm_w).transpose(0, 2, 1, 3)
    v = v.reshape(b, s, ATTN_HEADS, ATTN_HEAD_DIM).transpose(0, 2, 1, 3)
    attn = moba_attention(q, k, v).transpose(0, 2, 1, 3).reshape(b, s, ATTN_WIDTH)

    xbc = jax.nn.silu(causal_dwconv(xbc, ssm_conv_w, ssm_conv_b))
    xs, bm, cm = jnp.split(xbc, (SSM_WIDTH, SSM_WIDTH + SSM_GROUPS * SSM_STATE), axis=-1)
    xs = xs.astype(jnp.float32).reshape(b, s, SSM_GROUPS, SSM_HEADS_PER_GROUP, SSM_HEAD_DIM)
    bm = bm.astype(jnp.float32).reshape(b, s, SSM_GROUPS, SSM_STATE)
    cm = cm.astype(jnp.float32).reshape(b, s, SSM_GROUPS, SSM_STATE)
    dt = jax.nn.softplus(dt_raw.astype(jnp.float32) + dt_bias.astype(jnp.float32))
    dt = dt.reshape(b, s, SSM_GROUPS, SSM_HEADS_PER_GROUP)
    a = -jnp.exp(a_log.astype(jnp.float32)).reshape(SSM_GROUPS, SSM_HEADS_PER_GROUP)
    y = ssd_chunked_scan(xs, dt, a, bm, cm)
    y = y + d_skip.astype(jnp.float32).reshape(SSM_GROUPS, SSM_HEADS_PER_GROUP)[:, :, None] * xs
    gate = jax.nn.silu(z.astype(jnp.float32)).reshape(b, s, SSM_GROUPS, SSM_HEADS_PER_GROUP * SSM_HEAD_DIM)
    y = y.reshape(b, s, SSM_GROUPS, SSM_HEADS_PER_GROUP * SSM_HEAD_DIM) * gate
    y = rms_norm(y, ssm_norm_w.reshape(SSM_GROUPS, SSM_HEADS_PER_GROUP * SSM_HEAD_DIM))
    ssm = y.reshape(b, s, SSM_WIDTH).astype(x.dtype)

    x = x + jnp.concatenate([attn, ssm], axis=-1) @ w_out

    h = rms_norm(x, norm2_w)
    u = causal_dwconv(h @ w_up, ffn_conv_w, ffn_conv_b)
    u_gate, u_val = jnp.split(u, 2, axis=-1)
    return x + (jax.nn.silu(u_gate) * u_val) @ w_down

def first_inputs(seed: int = 0) -> dict:
    key = jax.random.key(seed)
    ks = jax.random.split(key, 17)

    def nrm(k, shape, scale):
        return jax.random.normal(k, shape, jnp.float32) * scale

    x = nrm(ks[0], (BATCH, SEQ, D_MODEL), 1.0)
    norm1_w = 1.0 + nrm(ks[1], (DEPTH, D_MODEL), 0.02)
    w_in = nrm(ks[2], (DEPTH, D_MODEL, IN_COLS), D_MODEL ** -0.5)
    q_norm_w = 1.0 + nrm(ks[3], (DEPTH, ATTN_HEAD_DIM), 0.02)
    k_norm_w = 1.0 + nrm(ks[4], (DEPTH, ATTN_HEAD_DIM), 0.02)
    ssm_conv_w = nrm(ks[5], (DEPTH, SSM_CONV, XBC_WIDTH), SSM_CONV ** -0.5)
    ssm_conv_b = nrm(ks[6], (DEPTH, XBC_WIDTH), 0.02)
    dt0 = jnp.exp(jax.random.uniform(ks[7], (DEPTH, SSM_HEADS), jnp.float32,
                                     minval=math.log(1e-3), maxval=math.log(1e-1)))
    dt_bias = dt0 + jnp.log(-jnp.expm1(-dt0))
    a_log = jnp.log(jax.random.uniform(ks[8], (DEPTH, SSM_HEADS), jnp.float32, minval=1.0, maxval=16.0))
    d_skip = 1.0 + nrm(ks[9], (DEPTH, SSM_HEADS), 0.1)
    ssm_norm_w = 1.0 + nrm(ks[10], (DEPTH, SSM_WIDTH), 0.02)
    w_out = nrm(ks[11], (DEPTH, MIX_WIDTH, D_MODEL), MIX_WIDTH ** -0.5)
    norm2_w = 1.0 + nrm(ks[12], (DEPTH, D_MODEL), 0.02)
    w_up = nrm(ks[13], (DEPTH, D_MODEL, 2 * D_FF), D_MODEL ** -0.5)
    ffn_conv_w = nrm(ks[14], (DEPTH, FFN_CONV, 2 * D_FF), FFN_CONV ** -0.5)
    ffn_conv_b = nrm(ks[15], (DEPTH, 2 * D_FF), 0.02)
    w_down = nrm(ks[16], (DEPTH, D_FF, D_MODEL), D_FF ** -0.5)
    return {"x": x, "norm1_w": norm1_w, "w_in": w_in, "q_norm_w": q_norm_w, "k_norm_w": k_norm_w,
            "ssm_conv_w": ssm_conv_w, "ssm_conv_b": ssm_conv_b, "dt_bias": dt_bias, "a_log": a_log,
            "d_skip": d_skip, "ssm_norm_w": ssm_norm_w, "w_out": w_out, "norm2_w": norm2_w,
            "w_up": w_up, "ffn_conv_w": ffn_conv_w, "ffn_conv_b": ffn_conv_b, "w_down": w_down}

def first_block(x, norm1_w, w_in, q_norm_w, k_norm_w, ssm_conv_w, ssm_conv_b, dt_bias, a_log,
              d_skip, ssm_norm_w, w_out, norm2_w, w_up, ffn_conv_w, ffn_conv_b, w_down):
    for i in range(DEPTH):
        x = hybrid_layer(x, norm1_w[i], w_in[i], q_norm_w[i], k_norm_w[i], ssm_conv_w[i],
                         ssm_conv_b[i], dt_bias[i], a_log[i], d_skip[i], ssm_norm_w[i], w_out[i],
                         norm2_w[i], w_up[i], ffn_conv_w[i], ffn_conv_b[i], w_down[i])
    return x


N_META = 16
CONV_W = D_MODEL // 2
N_CONV_GROUPS = 16
CONV_K = 3
RWKV_W = D_MODEL // 2
HEAD_N = 64
N_RWKV_HEADS = RWKV_W // HEAD_N
DECAY_LORA = 96
AAA_LORA = 96
GATE_LORA = 256
FFN_K = 3
RMS_EPS = 1e-6
GN_EPS = 64e-5
DECAY_SCALE = math.exp(-0.5)

CONV_COLS = 3 * CONV_W
RWKV_COLS = 3 * RWKV_W + DECAY_LORA + AAA_LORA + GATE_LORA
IN_COLS_2 = CONV_COLS + RWKV_COLS


def rmsnorm(x, g):
    xf = x.astype(jnp.float32)
    y = xf * lax.rsqrt(jnp.mean(xf * xf, axis=-1, keepdims=True) + RMS_EPS)
    return (y * g.astype(jnp.float32)).astype(x.dtype)

def causal_dwconv_2(x, w):
    k = w.shape[0]
    seq_len = x.shape[1]
    xp = jnp.pad(x, ((0, 0), (k - 1, 0), (0, 0)))
    y = xp[:, 0:seq_len] * w[0]
    for i in range(1, k):
        y = y + xp[:, i:i + seq_len] * w[i]
    return y

def token_shift(z, mu):
    z_prev = jnp.pad(z, ((0, 0), (1, 0), (0, 0)))[:, :-1]
    return z + (z_prev - z) * mu

def rwkv7_scan(r, w, k, v, a_vec, b_vec):
    bsz, _, h, n = r.shape
    xs = tuple(jnp.swapaxes(t, 0, 1) for t in (r, w, k, v, a_vec, b_vec))

    def step(s, inp):
        r_t, w_t, k_t, v_t, a_t, b_t = inp
        sa = jnp.einsum('bhvk,bhk->bhv', s, a_t)
        s = s * w_t[:, :, None, :] + sa[..., None] * b_t[:, :, None, :] + v_t[..., None] * k_t[:, :, None, :]
        y_t = jnp.einsum('bhvk,bhk->bhv', s, r_t)
        return s, y_t

    s0 = jnp.zeros((bsz, h, n, n), jnp.float32)
    _, ys = lax.scan(step, s0, xs)
    return jnp.swapaxes(ys, 0, 1)

def short_conv_group(zc, conv_w):
    gate_b, gate_c, hx = jnp.split(zc, 3, axis=-1)
    return gate_b * causal_dwconv_2(gate_c * hx, conv_w)

def rwkv7_group(zr, mu_rwkv, w_decay_up, w0, a_up, a0, g_up, k_k, k_a, r_k, ln_x_w, ln_x_b):
    bsz, seq_len, _ = zr.shape
    zr = token_shift(zr, mu_rwkv)
    o1 = RWKV_W; o2 = 2 * RWKV_W; o3 = 3 * RWKV_W
    o4 = o3 + DECAY_LORA; o5 = o4 + AAA_LORA
    r = zr[..., :o1]
    k = zr[..., o1:o2]
    v = zr[..., o2:o3]
    wd = zr[..., o3:o4]
    ad = zr[..., o4:o5]
    gd = zr[..., o5:]

    f32 = jnp.float32
    log_w = -DECAY_SCALE * jax.nn.sigmoid((w0 + jnp.tanh(wd) @ w_decay_up).astype(f32))
    a = jax.nn.sigmoid(a0 + ad @ a_up)
    g = jax.nn.sigmoid(gd) @ g_up

    hs = (bsz, seq_len, N_RWKV_HEADS, HEAD_N)
    kk = (k * k_k).astype(f32).reshape(hs)
    kk = kk / jnp.maximum(jnp.sqrt(jnp.sum(kk * kk, axis=-1, keepdims=True)), 1e-12)
    k = k * (1.0 + (a - 1.0) * k_a)

    r_h = r.astype(f32).reshape(hs)
    k_h = k.astype(f32).reshape(hs)
    v_h = v.astype(f32).reshape(hs)
    a_h = a.astype(f32).reshape(hs)
    y = rwkv7_scan(r_h, jnp.exp(log_w).reshape(hs), k_h, v_h, -kk, kk * a_h)

    mean = jnp.mean(y, axis=-1, keepdims=True)
    var = jnp.mean(jnp.square(y - mean), axis=-1, keepdims=True)
    y = (y - mean) * lax.rsqrt(var + GN_EPS)
    y = y.reshape(bsz, seq_len, RWKV_W) * ln_x_w.astype(f32) + ln_x_b.astype(f32)
    bonus = jnp.sum(r_h * k_h * r_k.astype(f32), axis=-1, keepdims=True) * v_h
    y = y + bonus.reshape(bsz, seq_len, RWKV_W)
    return (y * g.astype(f32)).astype(zr.dtype)

def conv_glu(x, w_gate_up, conv_ffn, w_down):
    gu = x @ w_gate_up
    gate, up = jnp.split(gu, 2, axis=-1)
    gate = causal_dwconv_2(gate, conv_ffn)
    return (jax.nn.silu(gate) * up) @ w_down

def second_inputs(seed: int = 0) -> dict:
    key = jax.random.key(seed)
    ks = jax.random.split(key, 24)
    f32 = jnp.float32
    nrm = lambda k, shape, s: jax.random.normal(k, shape, f32) * s
    d = D_MODEL
    return {
        "x": nrm(ks[0], (BATCH, SEQ, d), 1.0),
        "meta_tokens": nrm(ks[1], (N_META, d), 1.0),
        "g_pre_mix": 1.0 + nrm(ks[2], (d,), 0.05),
        "w_in": nrm(ks[3], (d, IN_COLS_2), d ** -0.5),
        "conv_w": nrm(ks[4], (CONV_K, CONV_W), CONV_K ** -0.5),
        "mu_rwkv": jax.random.uniform(ks[5], (RWKV_COLS,), f32, 0.1, 0.9),
        "w_decay_up": nrm(ks[6], (DECAY_LORA, RWKV_W), 0.1 * DECAY_LORA ** -0.5),
        "w0": nrm(ks[7], (RWKV_W,), 0.5) - 0.5,
        "a_up": nrm(ks[8], (AAA_LORA, RWKV_W), 0.1 * AAA_LORA ** -0.5),
        "a0": nrm(ks[9], (RWKV_W,), 0.1),
        "g_up": nrm(ks[10], (GATE_LORA, RWKV_W), GATE_LORA ** -0.5),
        "k_k": 0.85 + nrm(ks[11], (RWKV_W,), 0.05),
        "k_a": 1.0 + nrm(ks[12], (RWKV_W,), 0.05),
        "r_k": nrm(ks[13], (N_RWKV_HEADS, HEAD_N), 0.1),
        "ln_x_w": 1.0 + nrm(ks[14], (RWKV_W,), 0.05),
        "ln_x_b": nrm(ks[15], (RWKV_W,), 0.02),
        "w_out": nrm(ks[16], (CONV_W + RWKV_W, d), (CONV_W + RWKV_W) ** -0.5),
        "g_post_mix": 1.0 + nrm(ks[17], (d,), 0.05),
        "g_pre_ffn": 1.0 + nrm(ks[18], (d,), 0.05),
        "w_gate_up": nrm(ks[19], (d, 2 * D_FF), d ** -0.5),
        "conv_ffn": nrm(ks[20], (FFN_K, D_FF), FFN_K ** -0.5),
        "w_down": nrm(ks[21], (D_FF, d), D_FF ** -0.5),
        "g_post_ffn": 1.0 + nrm(ks[22], (d,), 0.05),
    }

def second_block(x, meta_tokens, g_pre_mix, w_in, conv_w, mu_rwkv, w_decay_up, w0, a_up, a0,
              g_up, k_k, k_a, r_k, ln_x_w, ln_x_b, w_out, g_post_mix, g_pre_ffn,
              w_gate_up, conv_ffn, w_down, g_post_ffn):
    bsz = x.shape[0]
    meta = jnp.broadcast_to(meta_tokens.astype(x.dtype)[None], (bsz, N_META, x.shape[-1]))
    h = jnp.concatenate([meta, x], axis=1)

    for _ in range(DEPTH):
        n = rmsnorm(h, g_pre_mix)
        z = n @ w_in
        y_conv = short_conv_group(z[..., :CONV_COLS], conv_w)
        y_rwkv = rwkv7_group(z[..., CONV_COLS:], mu_rwkv, w_decay_up, w0, a_up, a0, g_up,
                             k_k, k_a, r_k, ln_x_w, ln_x_b)
        mix = jnp.concatenate([y_conv, y_rwkv], axis=-1) @ w_out
        h = h + rmsnorm(mix, g_post_mix)
        f = conv_glu(rmsnorm(h, g_pre_ffn), w_gate_up, conv_ffn, w_down)
        h = h + rmsnorm(f, g_post_ffn)

    return h[:, N_META:]


def setup_inputs(seed=0):
    out = dict(first_inputs(seed))
    for name, value in second_inputs(seed + 1).items():
        if name != "x":
            out[name + "_2"] = value
    return out


def reference(
    x, norm1_w, w_in, q_norm_w, k_norm_w, ssm_conv_w, ssm_conv_b, dt_bias, a_log, d_skip,
    ssm_norm_w, w_out, norm2_w, w_up, ffn_conv_w, ffn_conv_b, w_down, meta_tokens_2,
    g_pre_mix_2, w_in_2, conv_w_2, mu_rwkv_2, w_decay_up_2, w0_2, a_up_2, a0_2, g_up_2, k_k_2,
    k_a_2, r_k_2, ln_x_w_2, ln_x_b_2, w_out_2, g_post_mix_2, g_pre_ffn_2, w_gate_up_2,
    conv_ffn_2, w_down_2, g_post_ffn_2,
):
    x = first_block(
        x, norm1_w, w_in, q_norm_w, k_norm_w, ssm_conv_w, ssm_conv_b, dt_bias, a_log, d_skip,
        ssm_norm_w, w_out, norm2_w, w_up, ffn_conv_w, ffn_conv_b, w_down,
    )
    return second_block(
        x, meta_tokens_2, g_pre_mix_2, w_in_2, conv_w_2, mu_rwkv_2, w_decay_up_2, w0_2, a_up_2,
        a0_2, g_up_2, k_k_2, k_a_2, r_k_2, ln_x_w_2, ln_x_b_2, w_out_2, g_post_mix_2,
        g_pre_ffn_2, w_gate_up_2, conv_ffn_2, w_down_2, g_post_ffn_2,
    )


_drawn_inputs = setup_inputs


def setup_inputs(seed=0):
    import zlib

    import numpy as np

    out = dict(_drawn_inputs(seed))
    spreads = {}
    factors = {'q_norm_w': 8.0,
     'k_norm_w': 8.0,
     'ssm_norm_w': 3.129,
     'norm2_w': 3.046,
     'ffn_conv_b': 3.011,
     'w_decay_up_2': 126.365,
     'a_up_2': 4.12,
     'a0_2': 3.118,
     'k_k_2': 200.0,
     'k_a_2': 8.184,
     'ln_x_w_2': 200.0,
     'ln_x_b_2': 200.0,
     'meta_tokens_2': 3.142,
     'g_pre_mix_2': 4.021,
     'r_k_2': 7.415,
     'g_post_mix_2': 7.663,
     'g_pre_ffn_2': 5.379,
     'g_post_ffn_2': 7.916,
     'w0_2': 8.0}
    for name, (base, spread) in spreads.items():
        noise = np.random.default_rng([zlib.crc32(name.encode()), seed]).standard_normal(out[name].shape)
        drawn = base * np.exp(spread * noise) if base else spread * noise
        out[name] = __import__('jax').numpy.asarray(drawn.astype(out[name].dtype))
    for name, factor in factors.items():
        out[name] = (out[name] * factor).astype(out[name].dtype)
    return out
```

```python
import math
from contextlib import ExitStack

import concourse.bass as bass
from concourse import mybir

ALU = mybir.AluOpType
ACT = mybir.ActivationFunctionType
F32 = mybir.dt.float32
F32R = mybir.dt.float32r
AX_X = mybir.AxisListType.X

P = 128
BIG = 1.0e30


class Semaphores:

    def __init__(self, nc):
        self.nc, self.made = nc, {}

    def __getitem__(self, name):
        if name not in self.made:
            self.made[name] = self.nc.alloc_semaphore(name)
        return self.made[name]


class Tally:

    def __init__(self, sem, names):
        self.sem, self.names = sem, names.split()

    def at(self, name, again=0):
        return self.sem, again * len(self.names) + self.names.index(name) + 1


class Stream:

    def __init__(self):
        self.units = self.groups = 0
        self.unit0, self.group0 = {}, {}

    def phase(self, name, groups, units):
        self.unit0[name], self.group0[name] = self.units, self.groups
        self.units += units
        self.groups += groups


def two_blocks(
    nc, x, norm1_w, w_in, q_norm_w, k_norm_w, ssm_conv_w, ssm_conv_b, dt_bias, a_log, d_skip,
    ssm_norm_w, w_out, norm2_w, w_up, ffn_conv_w, ffn_conv_b, w_down, meta_tokens_2,
    g_pre_mix_2, w_in_2, conv_w_2, mu_rwkv_2, w_decay_up_2, w0_2, a_up_2, a0_2, g_up_2, k_k_2,
    k_a_2, r_k_2, ln_x_w_2, ln_x_b_2, w_out_2, g_post_mix_2, g_pre_ffn_2, w_gate_up_2,
    conv_ffn_2, w_down_2, g_post_ffn_2, out,
):
    _, SEQ, D = x.shape
    META = meta_tokens_2.shape[0]
    T1, T2 = SEQ, SEQ + META
    T0 = META
    KD = D // P
    AH = 8
    SH = dt_bias.shape[1]
    SG, SN, SPD = 2, 128, 64
    CH = 128
    DFF = w_down.shape[1]
    FCH = DFF // 512
    assert D == 2048 and SEQ == 256 and META == 16 and DFF == FCH * 512
    RK = 4
    NSLOT = 4
    RT = 288
    PAD = RT - T2
    RB = 96
    RC = 32
    RW = 8

    EPS = 1e-6
    GN_EPS = 64e-5
    DECAY = math.exp(-0.5)

    stream = Stream()
    G_IN1 = 22
    stream.phase("in1", G_IN1 + 1, 4 * (G_IN1 + 1))
    stream.phase("out1", 8, 32)
    stream.phase("ffn1", 4 * FCH + 8 * FCH, 24 * FCH)
    stream.phase("in2", 26, 104)
    stream.phase("out2", 8, 32)
    stream.phase("ffn2", 4 * FCH + 8 * FCH, 24 * FCH)

    chunks_before = {"ffn1": 0, "ffn2": FCH}

    S = Semaphores(nc)
    landed = [S[f"raw_landed_{j}"] for j in range(NSLOT)]

    rw_pe = Tally(S["rw_tensor"], "lt ak l tab tkv l2 l2t akv l4 l4t p2m l8 p3m p4m y1 zm xm rum "
                                  "mtm step0 step1 step2")
    rw_dve = Tally(S["rw_vector"], "ldt lot rbt akt rkt p1 ld l2_out l4t_out p2 p3 p4 z u ru mt0 "
                                   "mt1")
    rw_act = Tally(S["rw_scalar"], "rhs_a b_tok kv l2t_out rhs_v l4_out l8_out y1_out")
    ssd_pe = Tally(S["ssd_tensor"], "dt_turned cb_made b_turned")
    ssd_dve = Tally(S["ssd_vector"], "dt_w dt_rows cb_masked b_placed")
    MADE_CONSTS = 6
    MADE_CAUSAL = MADE_CONSTS + 3
    MADE_UPTO = MADE_CAUSAL + 2
    MADE_SCAN = MADE_UPTO + 2
    MADE_RWKV = MADE_SCAN + 5 + 2 + 2 + 2 + 2 + 4 + 1
    NORM_SIGNALS = dict(sq=4, add=5, ss=1, ms=1, inv=1, rstd=1, hi=16, lo=16)
    HI_NORMS = ("n0", "n1", "n2", "n4")

    def norm_at(name, what, n):
        before = HI_NORMS.index(name) if what in ("hi", "lo") else int(name[1])
        return S["norm_" + what], NORM_SIGNALS[what] * before + n

    def sb(name, shape, dtype=F32):
        return nc.alloc_sbuf_tensor(name, shape, dtype)

    raw = sb("raw", [P, NSLOT, RK * 256])
    w_hi = sb("w_hi", [P, NSLOT, RK * 256], F32R)
    w_lo = sb("w_lo", [P, NSLOT, RK * 256], F32R)
    resid = sb("resid", [P, KD, T2])
    act_hi = sb("act_hi", [P, KD, T2], F32R)
    act_lo = sb("act_lo", [P, KD, T2], F32R)
    ident = sb("ident", [P, P])
    ones = sb("ones", [P, P])
    halves = sb("halves", [P, P])
    rstd = sb("rstd", [P, T2])
    ss_part = sb("ss_part", [P, T2])
    head_par = sb("head_par", [P, 6])

    rows = []

    def rows_of(ap, n):
        at = sum(r[1] for r in rows)
        rows.append((ap, n, at))
        return at

    def flat(ap):
        return ap.rearrange("a d -> (a d)")

    def tiles(ap1, n):
        return ap1.rearrange("(k p) -> k p", p=P), n

    c_dskip = rows_of(None, 8)
    c_norm1 = rows_of(*tiles(flat(norm1_w), 16))
    c_qn = rows_of(q_norm_w, 1)
    c_kn = rows_of(k_norm_w, 1)
    c_sconv = rows_of(ssm_conv_w.rearrange("a j (k p) -> (a j k) p", p=P), 48)
    c_sconvb = rows_of(*tiles(flat(ssm_conv_b), 12))
    c_snorm = rows_of(*tiles(flat(ssm_norm_w), 8))
    c_norm2 = rows_of(*tiles(flat(norm2_w), 16))
    fconv = ffn_conv_w.rearrange("a j (k p) -> (a j) k p", p=P)
    c_fconv = [rows_of(fconv[j], 88) for j in range(3)]
    c_fconvb = rows_of(*tiles(flat(ffn_conv_b), 88))
    c_premix = rows_of(*tiles(g_pre_mix_2, 16))
    c_conv2 = rows_of(conv_w_2.rearrange("j (k p) -> (j k) p", p=P), 24)
    c_mu = rows_of(mu_rwkv_2[0:3072].rearrange("(k p) -> k p", p=P), 24)
    c_mug = rows_of(mu_rwkv_2[3264:3520].rearrange("(k p) -> k p", p=P), 2)
    c_w0 = rows_of(*tiles(w0_2, 8))
    c_a0 = rows_of(*tiles(a0_2, 8))
    c_kk = rows_of(*tiles(k_k_2, 8))
    c_ka = rows_of(*tiles(k_a_2, 8))
    c_rk = rows_of(*tiles(flat(r_k_2), 8))
    c_lnw = rows_of(*tiles(ln_x_w_2, 8))
    c_lnb = rows_of(*tiles(ln_x_b_2, 8))
    c_postmix = rows_of(*tiles(g_post_mix_2, 16))
    c_preffn = rows_of(*tiles(g_pre_ffn_2, 16))
    gconv = conv_ffn_2.rearrange("j (k p) -> j k p", p=P)
    c_gconv = [rows_of(gconv[j], 44) for j in range(3)]
    c_postffn = rows_of(*tiles(g_post_ffn_2, 16))
    c_mulow = rows_of(None, 2)
    NROWS = sum(r[1] for r in rows)
    NPACK = -(-NROWS // P)
    par = sb("par", [P, NPACK * P])
    assert c_mulow // P == (c_mulow + 1) // P

    def col(c):
        return par[:, c:c + 1]


    def shared(shapes, keep=None):
        own = ExitStack()
        got = {n: own.enter_context(nc.sbuf_tensor(n, [P, *s], d)) for n, s, d in shapes}
        if keep is None:
            own.close()
        else:
            keep.enter_context(own)
        return got

    M = {}
    for names in (
        [("packs", [NPACK, P], F32), ("x_rows", [2, D], F32), ("meta_rows", [D], F32)],
        [
            ("proj", [45, T1], F32),
            ("squares1", [8, T2], F32),
            ("head_sq", [4, T1], F32), ("head_r", [4, T1], F32),
            ("q_still", [2, T1], F32), ("v_still", [2, T1], F32),
            ("causal", [384], F32), ("scores", [2, 384], F32), ("probs_t", [2, 384], F32),
            ("v_rows", [2, 2 * P], F32), ("soft", [2, 8], F32),
        ],
        [
            ("proj_ssd", [45, T1], F32), ("upto", [P], F32), ("conv_out", [2, T1], F32),
            ("step", [7, T1], F32), ("step_rows", [5, 16], F32), ("minus_a", [1], F32),
            ("cb", [4, P], F32), ("b_rows", [2, P], F32), ("xdt", [2, 1024], F32),
            ("xdte", [1024], F32), ("state0", [2, 512], F32), ("diag", [2, 512], F32),
            ("seg", [2, 512], F32), ("gmat", [2, 512], F32), ("cte", [2, 512], F32),
            ("y_sq", [4, T1], F32), ("y_r", [2, T1], F32),
        ],
        [
            ("up", [8, T2], F32), ("conv", [8, T2], F32), ("ff", [4, T2], F32),
            ("mixed", [KD, T2], F32), ("squares2", [8, T2], F32),
            ("ff_hi", [4, T2], F32R), ("ff_lo", [4, T2], F32R), ("out_rows", [2, D], F32),
        ],
    ):
        M.update(shared(names))
    both = ExitStack()
    M.update(shared([
        ("z2", [24, RT], F32),
        ("rk_a", [RW, RT], F32),
        ("rk_b", [RW, RT], F32),
        ("bonus", [RW, RT], F32), ("low", [4, RT], F32), ("wc", [RW, 9], F32),
    ], both))
    M.update(shared([("squares3", [8, T2], F32)]))
    M.update(shared([
        ("t5", [RW, RT], F32), ("t6", [RW, RT], F32), ("t7", [RW, RT], F32),
        ("w_low", [2, 1024], F32), ("scan_keep", [RT], F32),
    ]))
    M.update(shared([
        ("fs", [2, 5, RB], F32),
        ("ldt", [4, RB], F32), ("lot", [4, RB], F32), ("rbt", [4, RB], F32),
        ("akt", [4, RB], F32), ("rkt", [4, RB], F32), ("ld", [4, RB], F32),
        ("p1", [4, RB], F32), ("l2", [4, RB], F32), ("l2t", [4, RB], F32),
        ("l4", [4, RB], F32), ("l4t", [4, RB], F32),
        ("rhs", [4, P], F32), ("y1", [4, P], F32), ("zz", [4, P], F32), ("uu", [2, 4, 64], F32),
        ("b_tok", [2 * P], F32), ("kv_tok", [2, 2 * P], F32), ("ru", [2, RB], F32),
        ("mt", [3, 2, P], F32), ("state", [2, P], F32),
        ("m_ldt", [RB], F32), ("m_lot", [RB], F32), ("m_r", [RB], F32), ("m_a", [RB], F32),
        ("m_ld", [RB], F32),
    ]))
    M.update(shared([("t8", [RW, RT], F32), ("g_up", [2, 1024], F32)]))
    M.update(shared([("bch", [3, 2, T2], F32), ("cv", [2, T2], F32), ("y_conv", [8, T2], F32)]))
    both.close()

    proj = M["proj"]
    psum = nc.alloc_psum_tensor("psum", [P, 8, 512], F32)
    l8, p2, p3, p4 = M["l2"], M["ld"], M["p1"], M["ldt"]

    def over(ap, axis, n):
        wide = ap.unsqueeze(axis)
        shape = list(wide.shape)
        shape[axis] = n
        return wide.to_broadcast(shape)

    def four(bank):
        return psum[0:RB, bank, 0:4 * RB].rearrange("p (h t) -> p h t", t=RB)

    def unit_rows(w):
        return w.rearrange("(j r p) n -> j p r n", r=RK, p=P)

    w_in1, w_out1, w_up1, w_dn1 = (unit_rows(w[0]) for w in (w_in, w_out, w_up, w_down))
    w_in2, w_out2, w_up2, w_dn2 = (unit_rows(w) for w in (w_in_2, w_out_2, w_gate_up_2, w_down_2))
    IN2_LOW, IN2_RKV, IN2_CONV = 2, 12, 12
    n_param_loads = []

    with nc.Block() as block:

        @block.sync
        def _(sp):
            def load(u, slot, src, wide=256):
                if not isinstance(u, int) or u >= NSLOT:
                    sp.wait_ge(S["lo_done"], u - NSLOT + 1)
                dst = raw[:, slot].rearrange("p (r n) -> p r n", r=RK)[:, :, 0:wide]
                sp.dma_start(dst, src).then_inc(landed[slot], 16)

            def load_group(u, w, c0, wide=256):
                for j in range(4):
                    load(u + j, j, w[j][:, :, bass.ds(c0, wide)], wide)

            sp.dma_start(M["x_rows"][:, 0], x[0, 0:P, :]).then_inc(S["x_landed"], 16)
            sp.dma_start(M["x_rows"][:, 1], x[0, P:2 * P, :]).then_inc(S["x_landed"], 16)
            sp.dma_start(M["meta_rows"][0:META], meta_tokens_2).then_inc(S["x_landed"], 16)
            sp.dma_start(head_par[0:8, 4:6], d_skip.rearrange("a (j b) -> (a j) b", b=2)) \
                .then_inc(S["d_landed"], 16)
            sp.wait_ge(S["packs_cleared"], 1)
            n = 0
            for ap, count, at in rows:
                if ap is None:
                    continue
                done = 0
                while done < count:
                    pack, row = divmod(at + done, P)
                    k = min(count - done, P - row)
                    sp.dma_start(M["packs"][row:row + k, pack], ap[done:done + k]) \
                        .then_inc(S["params_landed"], 16)
                    done += k
                    n += 1
            pack, row = divmod(c_mulow, P)
            sp.dma_start(M["packs"][row:row + 2, pack, 0:96],
                         mu_rwkv_2[3072:3264].rearrange("(a b) -> a b", a=2)) \
                .then_inc(S["params_landed"], 16)
            n_param_loads.append(n + 1)
            sp.dma_start(head_par[0:16, 0:1], dt_bias.rearrange("a h -> h a")) \
                .then_inc(S["heads_landed"], 16)
            sp.dma_start(head_par[0:16, 1:2], a_log.rearrange("a h -> h a")) \
                .then_inc(S["heads_landed"], 16)
            u = stream.unit0["in1"]
            load_group(u, w_in1, 0)
            with sp.Fori(1, G_IN1) as g:
                load_group(u + 4 * g, w_in1, 256 * g)
            load_group(u + 4 * G_IN1, w_in1, 256 * G_IN1, 16)
            u = stream.unit0["out1"]
            with sp.Fori(0, 8) as g:
                load_group(u + 4 * g, w_out1, 256 * g)

            def ffn_loads(name, w_up, w_dn):
                u = stream.unit0[name]

                def ups(u, i):
                    for j, c0 in enumerate((0, 256, DFF, DFF + 256)):
                        load_group(u + 4 * j, w_up, c0 + 512 * i)

                def downs(u, i):
                    for d in range(8):
                        load(u + d, d % 4, w_dn[bass.ds(i, 1)][0][:, :, 256 * d:256 * d + 256])

                ups(u, 0)
                with sp.Fori(1, FCH) as i:
                    ups(u + 24 * i - 8, i)
                    downs(u + 24 * i + 8, i - 1)
                downs(u + 24 * FCH - 8, FCH - 1)

            ffn_loads("ffn1", w_up1, w_dn1)
            u = stream.unit0["in2"]
            load_group(u, w_in2, 6144, 192)
            load_group(u + 4, w_in2, 6336)
            with sp.Fori(0, IN2_RKV) as g:
                load_group(u + 8 + 4 * g, w_in2, 3072 + 256 * g)
            u = u + 8 + 4 * IN2_RKV
            with sp.Fori(0, 4) as q:
                for j in range(3):
                    load_group(u + 12 * q + 4 * j, w_in2, 1024 * j + 256 * q)
            u = stream.unit0["out2"]
            with sp.Fori(0, 8) as g:
                load_group(u + 4 * g, w_out2, 256 * g)
            ffn_loads("ffn2", w_up2, w_dn2)
            for tt in range(2):
                sp.wait_ge(S["out_copied"], 4 * tt + 4)
                sp.dma_start(out[0, tt * P:tt * P + P, :], M["out_rows"][:, tt]) \
                    .then_inc(S["stored"], 16)
            sp.wait_ge(S["stored"], 32)

        @block.gpsimd
        def _(pool):
            def select(out, in_, pattern, op, fill, base, mult):
                pool.wait_ge(S["made"], made[0])
                pool.affine_select(out=out, in_=in_, pattern=pattern, compare_op=op, fill=fill,
                                   base=base, channel_multiplier=mult).then_inc(S["made"], 1)
                made[0] += 1

            made = [0]
            for t, v in ((ones, 1.0), (ident, 1.0), (halves, 1.0)):
                pool.memset(t[:], v).then_inc(S["made"], 1)
            made[0] += 3
            select(ident[:], ident[:], [[-1, P]], ALU.is_equal, 0.0, 0, 1)
            h3 = halves[:].rearrange("p (b c) -> p b c", b=2)
            select(h3, h3, [[-64, 2], [0, 64]], ALU.is_ge, 0.0, 0, 1)
            select(h3, h3, [[64, 2], [0, 64]], ALU.is_ge, 0.0, 63, -1)

            def sum_squares(name, sq, T):
                for j in range(1, 4):
                    pool.wait_ge(*norm_at(name, "sq", j + 1))
                    if j > 1:
                        pool.wait_ge(*norm_at(name, "add", j - 1))
                    pool.tensor_tensor(sq[:, 0:4, 0:T], sq[:, 0:4, 0:T], sq[:, 4:8, 0:T], ALU.add) \
                        .then_inc(S["norm_add"], 1)
                pool.wait_ge(*norm_at(name, "add", 3))
                pool.tensor_tensor(sq[:, 0:2, 0:T], sq[:, 0:2, 0:T], sq[:, 2:4, 0:T], ALU.add) \
                    .then_inc(S["norm_add"], 1)
                pool.wait_ge(*norm_at(name, "add", 4))
                pool.tensor_tensor(ss_part[:, 0:T], sq[:, 0, 0:T], sq[:, 1, 0:T], ALU.add) \
                    .then_inc(S["norm_add"], 1)

            sum_squares("n0", M["squares1"], T1)
            pool.memset(M["causal"][:], 0.0).then_inc(S["made"], 1)
            made[0] += 1
            select(M["causal"][:, 0:P], M["causal"][:, 0:P], [[-1, P]], ALU.is_ge, -BIG, 0, 1)
            select(M["causal"][:, P:384], M["causal"][:, P:384], [[-1, 256]], ALU.is_ge, -BIG, P, 1)
            pool.wait_ge(S["qk_done"], 4)
            with pool.Fori(0, 4) as i:
                for b in range(2):
                    pool.wait_ge(S["at_scored"], 2 * i + b + 1)
                    pool.wait_ge(S["at_v_turned"], 2 * i + b + 1)
                    pool.tensor_copy(M["q_still"][:, b], proj[:, bass.ds(2 * i + b, 1)][:, 0]) \
                        .then_inc(S["at_still"], 1)
                    pool.tensor_copy(M["v_still"][:, b], proj[:, bass.ds(2 * i + b + 16, 1)][:, 0]) \
                        .then_inc(S["at_still"], 1)
            pool.wait_ge(S["attention_over"], 1)
            pool.memset(M["upto"][:], 1.0).then_inc(S["made"], 1)
            made[0] += 1
            select(M["upto"][:], M["upto"][:], [[1, P]], ALU.is_ge, 0.0, 0, -1)
            sum_squares("n1", M["squares2"], T1)
            sum_squares("n2", M["squares3"], T2)
            pool.wait_ge(*norm_at("n2", "rstd", 1))
            sk = M["scan_keep"][:].rearrange("p (c t) -> p c t", t=RC)
            pool.memset(M["scan_keep"][:], 1.0).then_inc(S["made"], 1)
            made[0] += 1
            select(sk, sk, [[0, RT // RC], [1, RC]], ALU.is_gt, 0.0, 0, 0)
            pool.wait_ge(S["rpre_over"], 1)
            for n in ("m_ldt", "m_lot", "m_r", "m_a", "m_ld"):
                pool.memset(M[n][0:RB], 1.0).then_inc(S["made"], 1)
            made[0] += 5

            def same(name, w):
                m = M[name][0:RB].rearrange("p (b c) -> p b c", c=w)
                select(m, m, [[-w, RB // w], [0, w]], ALU.is_ge, 0.0, 0, 1)
                select(m, m, [[w, RB // w], [0, w]], ALU.is_ge, 0.0, w - 1, -1)

            def beyond(name, op, sign):
                m = M[name][0:RB]
                select(m, m, [[sign, RB]], op, 0.0, 0, -sign)

            same("m_ldt", 16)
            beyond("m_ldt", ALU.is_gt, 1)
            same("m_r", RC)
            beyond("m_r", ALU.is_ge, 1)
            same("m_a", RC)
            beyond("m_a", ALU.is_gt, 1)
            same("m_ld", 16)
            beyond("m_ld", ALU.is_gt, -1)
            pool.wait_ge(S["made"], made[0])
            pool.tensor_tensor(M["m_lot"][0:RB], M["m_a"][0:RB], M["m_ldt"][0:RB], ALU.subtract) \
                .then_inc(S["made"], 1)
            assert made[0] + 1 == MADE_RWKV
            with pool.Fori(0, 4) as q:
                with pool.Fori(0, 3) as tt:
                    pool.wait_ge(S["rw_end"], 3 * q + tt + 1)
                    for k, (src, t0) in enumerate((("rk_b", 0), ("z2", 8), ("z2", 16))):
                        pool.tensor_copy(
                            M["fs"][:, :, 2 + k],
                            M[src][:, bass.ds(2 * q + t0, 2), bass.ds(RB * tt, RB)],
                        ).then_inc(S["rw_still"], 1)
            sum_squares("n3", M["squares2"], T2)
            sum_squares("n4", M["squares2"], T2)
            sum_squares("n5", M["squares2"], T2)

        @block.scalar
        def _(act):
            def hi(u, slot):
                act.wait_ge(landed[slot], 16 * (u // 4 + 1) if isinstance(u, int)
                            else landed_at(u, slot))
                if not isinstance(u, int) or u >= NSLOT:
                    act.wait_ge(S["unit_used"], u - NSLOT + 1)
                act.activation(w_hi[:, slot], raw[:, slot], ACT.Copy).then_inc(S["hi_done"], 1)

            def wait_apart(sem, value):
                act.wait_ge(sem, value)
                act.wait_ge(S["par_placed"], 2)

            def landed_at(u, slot):
                return (u - slot) * 4 + 16

            def hi_group(u):
                for j in range(4):
                    hi(u + j, j)

            def squares(name, src, sq, tc, ready=None):
                T = tc.stop - tc.start
                for j in range(4):
                    if ready:
                        act.wait_ge(*ready(4 * j + 3))
                    if j >= 2:
                        act.wait_ge(*norm_at(name, "add", j - 1))
                    half = sq[:, 0:4, 0:T] if j == 0 else sq[:, 4:8, 0:T]
                    act.activation(half, src[:, 4 * j:4 * j + 4, tc], ACT.Square) \
                        .then_inc(S["norm_sq"], 1)

            def norm_in(name, c, sq, tc, ready=None):
                T = tc.stop - tc.start
                for j in range(4):
                    for k in range(4 * j, 4 * j + 4):
                        if ready:
                            act.wait_ge(*ready(k))
                        act.activation(act_hi[:, k, tc], resid[:, k, tc], ACT.Identity,
                                       scale=col(c + k)).then_inc(S["norm_hi"], 1)
                    if j >= 2:
                        act.wait_ge(*norm_at(name, "add", j - 1))
                    half = sq[:, 0:4, 0:T] if j == 0 else sq[:, 4:8, 0:T]
                    act.activation(half, resid[:, 4 * j:4 * j + 4, tc], ACT.Square) \
                        .then_inc(S["norm_sq"], 1)

            def rstd_root(name, T):
                act.wait_ge(*norm_at(name, "inv", 1))
                act.activation(rstd[:, 0:T], rstd[:, 0:T], ACT.Sqrt).then_inc(S["norm_rstd"], 1)

            TC1, TC2 = slice(T0, T2), slice(0, T2)

            hi_group(stream.unit0["in1"])
            act.wait_ge(S["x_placed"], 9)
            act.wait_ge(S["par_placed"], 2)
            norm_in("n0", c_norm1, M["squares1"], TC1)
            rstd_root("n0", T1)
            u = stream.unit0["in1"]
            with act.Fori(1, G_IN1) as g:
                hi_group(u + 4 * g)
            hi_group(u + 4 * G_IN1)
            hi_group(stream.unit0["out1"])
            act.wait_ge(S["evicted"], 16 // 2)
            for n in range(4):
                if n:
                    act.wait_ge(S["qk_ss"], n)
                act.activation(M["head_sq"][:], proj[:, 4 * n:4 * n + 4], ACT.Square) \
                    .then_inc(S["qk_sq"], 1)
                act.wait_ge(S["qk_inv"], n + 1)
                act.activation(M["head_r"][:], M["head_r"][:], ACT.Sqrt).then_inc(S["qk_rstd"], 1)
            scale = 128.0 ** -0.5
            act.sem_inc(S["at_pt"], 2)
            with act.Fori(0, 4) as i:
                for b in range(2):
                    act.wait_ge(S["at_v_turned"], 2 * i + b + 3)
                    act.wait_ge(S["at_out"], 2 * i + b + 1)
                    act.activation(M["v_rows"][:, b], psum[:, 6 + b, 0:256], ACT.Copy) \
                        .then_inc(S["at_v"], 1)
                for b in range(2):
                    act.wait_ge(S["at_shift"], 2 * i + b + 1)
                    for k, (lo, wide) in enumerate(((0, P), (P, 256))):
                        s = M["scores"][:, b, lo:lo + wide]
                        act.activation(s, s, ACT.Exp, bias=M["soft"][:, b, 2 + k:3 + k], scale=scale,
                                       accum_out=M["soft"][:, b, 4 + k:5 + k]) \
                            .then_inc(S["at_exp"], 1)
                for b in range(2):
                    act.wait_ge(S["at_p_turned"], 2 * i + b + 3)
                    act.wait_ge(S["at_out"], 2 * i + b + 1)
                    act.activation(M["probs_t"][:, b], psum[:, 6 + b, 0:384], ACT.Copy) \
                        .then_inc(S["at_pt"], 1)
            act.wait_ge(S["attention_over"], 1)
            for n in range(12):
                if n >= 2:
                    act.wait_ge(S["sc_silu"], n - 1)
                act.activation(M["conv_out"][:, n % 2], proj[:, 32 + n], ACT.Identity,
                               bias=col(c_sconvb + n), scale=col(c_sconv + 36 + n)) \
                    .then_inc(S["sc_first"], 1)
                if n:
                    act.wait_ge(S["sc_taps"], 3 * n)
                    act.activation(proj[:, 31 + n], M["conv_out"][:, (n - 1) % 2], ACT.Silu) \
                        .then_inc(S["sc_silu"], 1)
            act.wait_ge(S["sc_taps"], 36)
            act.activation(proj[:, 43], M["conv_out"][:, 1], ACT.Silu).then_inc(S["sc_silu"], 1)
            act.activation(proj[:, 24:32], proj[:, 24:32], ACT.Silu).then_inc(S["z_silu"], 1)
            step, srows = M["step"], M["step_rows"]
            act.wait_ge(S["dt_abs"], 2)
            act.activation(step[0:16, 2], step[0:16, 1], ACT.Exp, scale=-1.0) \
                .then_inc(S["dt_exp"], 1)
            act.wait_ge(S["heads_landed"], 32)
            act.activation(head_par[0:16, 2:3], head_par[0:16, 1:2], ACT.Exp) \
                .then_inc(S["dt_exp"], 1)
            act.wait_ge(S["dt_exp"], 1)
            act.activation(step[0:16, 2], step[0:16, 2], ACT.Ln, bias=1.0).then_inc(S["dt_ln"], 1)
            act.wait_ge(S["dt_cum"], 2)
            act.activation(step[0:16, 6, 0:P], step[0:16, 5, 0:P], ACT.Exp, scale=-1.0,
                           bias=step[0:16, 5, P - 1:P]).then_inc(S["dt_end"], 1)
            for n in range(8):
                if n % 2:
                    act.wait_ge(S["sg_row"], n + 1)
                    act.wait_ge(S["sg_seg"], 2 * n + 1)
                    if n > 2:
                        act.wait_ge(S["sg_cte"], (n - 1) // 2)
                    act.activation(M["cte"][:, 0], psum[:, 4 + n % 2], ACT.Exp) \
                        .then_inc(S["sg_e1"], 1)
                act.wait_ge(S["sg_seg"], 2 * n + 2)
                act.activation(M["seg"][:, n % 2], M["seg"][:, n % 2], ACT.Exp) \
                    .then_inc(S["sg_exp"], 1)
            for g in range(2):
                act.wait_ge(S["y_gated"], 2 * g + 2)
                if g:
                    act.wait_ge(S["yn_ss"], 1)
                act.activation(M["y_sq"][:], proj[:, 32 + 4 * g:36 + 4 * g], ACT.Square) \
                    .then_inc(S["yn_sq"], 1)
            for g in range(2):
                act.wait_ge(S["yn_inv"], g + 1)
                act.activation(M["y_r"][:, g], M["y_r"][:, g], ACT.Sqrt).then_inc(S["yn_rstd"], 1)
            act.activation(act_hi[:, 0:8, TC1], proj[:, 0:8], ACT.Copy).then_inc(S["mix_hi"], 1)
            act.wait_ge(S["yn_done"], 8)
            act.activation(act_hi[:, 8:16, TC1], proj[:, 32:40], ACT.Copy) \
                .then_inc(S["mix_hi"], 1)
            u = stream.unit0["out1"]
            with act.Fori(1, 8) as g:
                hi_group(u + 4 * g)
            hi_group(stream.unit0["ffn1"])

            def ffn(name, T, cc, cb, vals, u_next, g_down):
                u, g0, n0 = stream.unit0[name], stream.group0[name], chunks_before[name]
                nt = 8 if vals else 4
                K1 = len(cc) - 1

                def first_taps(i):
                    for t in range(nt):
                        c = (44 if t >= 4 else 0) + t % 4
                        how = dict(scale=par[:, bass.ds(4 * i + (c + cc[K1]), 1)])
                        if cb is not None:
                            how["bias"] = par[:, bass.ds(4 * i + (c + cb), 1)]
                        act.activation(M["conv"][:, t, 0:T], M["up"][:, t, 0:T], ACT.Identity,
                                       **how).then_inc(S["ff_first"], 1)

                def silu(i):
                    act.wait_ge(S["ff_taps"], 2 * nt * i + (16 * n0 + 8))
                    act.activation(M["conv"][:, 0:4, 0:T], M["conv"][:, 0:4, 0:T], ACT.Silu) \
                        .then_inc(S["ff_silu"], 1)

                def product_hi(i, u_down):
                    act.wait_ge(S["ff_ff"], i + (n0 + 1))
                    if u_down is not None:
                        act.wait_ge(S["unit_used"], u_down)
                    act.activation(M["ff_hi"][:, :, 0:T], M["ff"][:, :, 0:T], ACT.Copy) \
                        .then_inc(S["ff_ffhi"], 1)

                for j in range(1, 4):
                    hi_group(u + 4 * j)
                with act.Fori(1, FCH) as i:
                    v = u + 24 * i - 8
                    hi_group(v)
                    wait_apart(S["evicted"], 12 * i - 8 + g0)
                    first_taps(i - 1)
                    hi_group(v + 4)
                    silu(i - 1)
                    hi_group(v + 8)
                    product_hi(i - 1, v)
                    hi_group(v + 12)
                    hi_group(v + 16)
                    hi_group(v + 20)
                v = u + 24 * FCH - 8
                hi_group(v)
                act.wait_ge(S["evicted"], g0 + 12 * FCH - 8)
                first_taps(FCH - 1)
                silu(FCH - 1)
                product_hi(FCH - 1, v)
                hi_group(v + 4)
                if u_next is not None:
                    hi_group(u_next)

            g = stream.group0["out1"]
            act.wait_ge(S["unit_used"], stream.unit0["ffn1"])
            norm_in("n1", c_norm2, M["squares2"], TC1,
                    lambda k: (S["evicted"], stream.group0["out1"] + k // 2 + 1))
            rstd_root("n1", T1)
            ffn("ffn1", T1, c_fconv, c_fconvb, True, stream.unit0["in2"], None)
            norm_in("n2", c_premix, M["squares3"], TC2,
                    lambda k: (S["evicted"], stream.group0["in2"] - 8 + k // 2 + 1))
            rstd_root("n2", T2)
            act.dma_start(M["w_low"][0:96, 0], w_decay_up_2).then_inc(S["low_landed"], 16)
            act.dma_start(M["w_low"][0:96, 1], a_up_2).then_inc(S["low_landed"], 16)
            u = stream.unit0["in2"]
            hi_group(u + 4)
            with act.Fori(0, IN2_RKV) as g:
                hi_group(u + 8 + 4 * g)
            hi_group(u + 8 + 4 * IN2_RKV)
            low, t5, t6, t7 = M["low"], M["t5"], M["t6"], M["t7"]
            rk_a, rk_b = M["rk_a"], M["rk_b"]
            act.wait_ge(S["low_shifted"], 4)
            act.activation(low[0:96, 0], low[0:96, 0], ACT.Tanh).then_inc(S["low_act"], 1)
            act.activation(low[:, 2:4], low[:, 2:4], ACT.Sigmoid).then_inc(S["low_act"], 1)
            for n in range(16):
                j = n % 8
                act.wait_ge(S["low_up"], n + 1)
                dst = t5 if n < 8 else rk_b
                act.activation(dst[:, j, PAD:RT], psum[:, 4 + n % 4, 0:T2], ACT.Sigmoid,
                               bias=col((c_w0 if n < 8 else c_a0) + j)).then_inc(S["low_out"], 1)
            act.wait_ge(S["kk_scaled"], 8)
            act.activation(t7[:], rk_a[:], ACT.Square).then_inc(S["kk_sq"], 1)
            act.wait_ge(S["kk_inv"], 1)
            act.activation(t7[:], t7[:], ACT.Sqrt).then_inc(S["kk_root"], 1)
            act.wait_ge(S["decay_prev"], 1)
            act.activation(t5[:], t5[:], ACT.Exp).then_inc(S["decay_exp"], 1)
            act.wait_ge(S["a_made"], 1)
            act.activation(t5[:], t6[:], ACT.Exp, scale=-1.0).then_inc(S["decay_exp"], 1)
            act.wait_ge(S["bk_made"], 2)
            act.activation(t5[:], t6[:], ACT.Exp).then_inc(S["decay_exp"], 1)
            act.wait_ge(S["rpre_over"], 1)
            fs = M["fs"]
            with act.Fori(0, 4) as q:
                with act.Fori(0, 3) as tt:
                    it = 3 * q + tt
                    wait_apart(S["rw_end"], it + 1)
                    for k, (src, t0) in enumerate((("rk_a", 0), ("z2", 0))):
                        act.activation(
                            fs[:, :, k], M[src][:, bass.ds(2 * q + t0, 2), bass.ds(RB * tt, RB)],
                            ACT.Copy).then_inc(S["rw_still_act"], 1)
                    act.wait_ge(*rw_pe.at("tab", it))
                    act.activation(M["rhs"][0:RB, :, 0:64],
                                   psum[0:RB, 6, 0:256].rearrange("p (h k) -> p h k", k=64),
                                   ACT.Copy).then_inc(S["rw_scalar"], 1)
                    act.activation(M["b_tok"][0:RB], psum[0:RB, 6, 256:512], ACT.Copy) \
                        .then_inc(S["rw_scalar"], 1)
                    act.wait_ge(*rw_pe.at("tkv", it))
                    act.activation(M["kv_tok"][0:RB].rearrange("p a b -> p (a b)"),
                                   psum[0:RB, 7, 0:512], ACT.Copy).then_inc(S["rw_scalar"], 1)
                    act.wait_ge(*rw_pe.at("l2t", it))
                    act.activation(M["l2t"][0:RB], four(5), ACT.Copy).then_inc(S["rw_scalar"], 1)
                    act.wait_ge(*rw_pe.at("akv", it))
                    act.activation(M["rhs"][0:RB, :, 64:P],
                                   psum[0:RB, 6, 0:256].rearrange("p (h k) -> p h k", k=64),
                                   ACT.Copy).then_inc(S["rw_scalar"], 1)
                    act.wait_ge(*rw_pe.at("l4", it))
                    act.activation(M["l4"][0:RB], four(4), ACT.Copy).then_inc(S["rw_scalar"], 1)
                    act.wait_ge(*rw_pe.at("l8", it))
                    act.activation(l8[0:RB], four(4), ACT.Copy).then_inc(S["rw_scalar"], 1)
                    act.wait_ge(*rw_pe.at("y1", it))
                    act.activation(M["y1"][0:RB].rearrange("p h k -> p (h k)"),
                                   psum[0:RB, 4, 0:512], ACT.Copy).then_inc(S["rw_scalar"], 1)
            act.wait_ge(S["rw_end"], 13)
            act.dma_start(M["g_up"][:], g_up_2.rearrange("(a p) n -> p a n", p=P)) \
                .then_inc(S["gup_landed"], 16)
            t8 = M["t8"]
            act.wait_ge(S["gn_centred"], 8)
            act.activation(t8[:], rk_a[:], ACT.Square).then_inc(S["gn_sq"], 1)
            act.wait_ge(S["gn_inv"], 1)
            act.activation(t8[:], t8[:], ACT.Sqrt).then_inc(S["gn_root"], 1)
            u2 = u + 8 + 4 * IN2_RKV
            for j in (1, 2):
                hi_group(u2 + 4 * j)
            with act.Fori(1, 4) as q:
                for j in range(3):
                    hi_group(u2 + 12 * q + 4 * j)
            hi_group(stream.unit0["out2"])
            act.wait_ge(S["unit_used"], stream.unit0["out2"])
            act.wait_ge(S["gn_done"], 8)
            act.activation(act_hi[:, 8:16], rk_a[:, :, PAD:RT], ACT.Copy).then_inc(S["mix_hi"], 1)
            act.wait_ge(S["cv_done"], 5)
            act.activation(act_hi[:, 0:8], M["y_conv"][:], ACT.Copy).then_inc(S["mix_hi"], 1)
            u = stream.unit0["out2"]
            with act.Fori(1, 8) as g:
                hi_group(u + 4 * g)
            hi_group(stream.unit0["ffn2"])
            squares("n3", M["mixed"], M["squares2"], TC2,
                    lambda k: (S["evicted"], stream.group0["out2"] + k // 2 + 1))
            rstd_root("n3", T2)
            act.wait_ge(*norm_at("n3", "add", 5))
            norm_in("n4", c_preffn, M["squares2"], TC2, lambda k: (S["post"], k + 1))
            rstd_root("n4", T2)
            ffn("ffn2", T2, c_gconv, None, False, None, None)
            squares("n5", M["mixed"], M["squares2"], TC2,
                    lambda k: (S["evicted"], stream.groups - 8 + k // 2 + 1))
            rstd_root("n5", T2)

        @block.vector
        def _(dve):
            def lo(u, slot):
                dve.wait_ge(S["hi_done"], u + 1)
                dve.tensor_tensor(w_lo[:, slot], raw[:, slot], w_hi[:, slot].bitcast(F32),
                                  ALU.subtract).then_inc(S["lo_done"], 1)

            def lo_group(u):
                for j in range(4):
                    lo(u + j, j)

            def bank_pair(pair, T, rows_=P):
                return psum[0:rows_, 2 * pair:2 * pair + 2, 0:T]

            def leave(u_end, pair, dst, T, rows_=P, how="scaled", single=False):
                dve.wait_ge(S["unit_used"], u_end)
                src = bank_pair(pair, T, rows_)
                if single:
                    src = psum[0:rows_, 2 * pair, 0:T]
                if how == "scaled":
                    r = rstd[0:rows_, 0:T] if single else over(rstd[0:rows_, 0:T], 1, 2)
                    ins = dve.tensor_tensor(dst, src, r, ALU.mult)
                elif how == "added":
                    ins = dve.tensor_tensor(dst, src, dst, ALU.add)
                else:
                    ins = dve.tensor_copy(dst, src)
                ins.then_inc(S["evicted"], 1)

            def rstd_of(name, T, width, eps):
                dve.wait_ge(*norm_at(name, "ss", 1))
                dve.tensor_scalar(rstd[:, 0:T], psum[:, 7, 0:T], 1.0 / width, eps, ALU.mult,
                                  ALU.add).then_inc(S["norm_ms"], 1)
                dve.wait_ge(*norm_at(name, "ms", 1))
                dve.reciprocal(rstd[:, 0:T], rstd[:, 0:T]).then_inc(S["norm_inv"], 1)
                dve.wait_ge(*norm_at(name, "rstd", 1))

            def norm_lo(name, c, tc):
                for k in range(KD):
                    dve.wait_ge(*norm_at(name, "hi", k + 1))
                    dve.scalar_tensor_tensor(
                        out=act_lo[:, k, tc], in0=resid[:, k, tc], scalar=col(c + k),
                        in1=act_hi[:, k, tc].bitcast(F32), op0=ALU.mult, op1=ALU.subtract,
                    ).then_inc(S["norm_lo"], 1)

            links = [0]

            def link(ins):
                links[0] += 1
                ins.then_inc(S["dve_links"], 1)
                dve.wait_ge(S["dve_links"], links[0])

            TC1, TC2 = slice(T0, T2), slice(0, T2)

            dve.memset(M["packs"][:], 0.0).then_inc(S["packs_cleared"], 1)
            dve.wait_ge(S["packs_cleared"], 1)
            dve.wait_ge(S["d_landed"], 16)
            assert c_dskip == 0
            dve.tensor_copy(M["packs"][0:8, 0].rearrange("p (b e) -> p b e", b=2),
                            over(head_par[0:8, 4:6], 2, 64)).then_inc(S["d_placed"], 1)
            for n in range(8):
                tt, g = divmod(n, 4)
                dve.wait_ge(S["x_turned"], n + 1)
                dve.tensor_copy(resid[:, 4 * g:4 * g + 4, T0 + P * tt:T0 + P * tt + P],
                                psum[:, 4 + n % 4].rearrange("p (k t) -> p k t", t=P)) \
                    .then_inc(S["x_placed"], 1)
            dve.wait_ge(S["x_turned"], 9)
            dve.tensor_copy(resid[:, :, 0:T0],
                            psum[:, 4, 0:KD * T0].rearrange("p (k t) -> p k t", t=T0)) \
                .then_inc(S["x_placed"], 1)
            for n in range(2):
                w = min(512, NPACK * P - 512 * n)
                dve.wait_ge(S["par_turned"], n + 1)
                dve.tensor_copy(par[:, 512 * n:512 * n + w], psum[:, 5 + n, 0:w]) \
                    .then_inc(S["par_placed"], 1)
            lo_group(stream.unit0["in1"])
            dve.wait_ge(S["par_placed"], 2)
            norm_lo("n0", c_norm1, TC1)
            rstd_of("n0", T1, D, EPS)
            u, g0 = stream.unit0["in1"], stream.group0["in1"]
            lo_group(u + 4)
            leave(u + 4, 0, proj[:, 0:2], T1)
            lo_group(u + 8)
            leave(u + 8, 1, proj[:, 2:4], T1)
            lo_group(u + 12)
            leave(u + 12, 0, proj[:, 4:6], T1)
            with dve.Fori(2, G_IN1 // 2) as i:
                for b in range(2):
                    g = 2 * i + b
                    lo_group(u + 4 * g)
                    leave(u + 4 * g, (b + 1) % 2, proj[:, bass.ds(2 * g - 2, 2)], T1)
            lo_group(u + 4 * G_IN1)
            leave(u + 4 * G_IN1, (G_IN1 - 1) % 2, proj[:, 2 * G_IN1 - 2:2 * G_IN1], T1)
            lo_group(stream.unit0["out1"])
            leave(u + 4 * G_IN1 + 4, G_IN1 % 2, proj[0:16, 44], T1, 16, single=True)
            for n in range(4):
                pair = 4 + 2 * (n % 2)
                hr = M["head_r"]
                if n:
                    dve.wait_ge(S["qk_done"], n)
                dve.wait_ge(S["qk_ss"], n + 1)
                link(dve.tensor_scalar(
                    hr[:].rearrange("p (a b) t -> p a (b t)", a=2), psum[:, pair:pair + 2],
                    1.0 / 128, EPS, ALU.mult, ALU.add))
                dve.reciprocal(hr[:], hr[:]).then_inc(S["qk_inv"], 1)
                dve.wait_ge(S["qk_rstd"], n + 1)
                q4 = proj[:, 4 * n:4 * n + 4]
                dve.scalar_tensor_tensor(out=q4, in0=q4, scalar=col(c_qn if n < 2 else c_kn),
                                         in1=hr[:], op0=ALU.mult, op1=ALU.mult) \
                    .then_inc(S["qk_done"], 1)
            dve.wait_ge(S["made"], MADE_CAUSAL)
            dve.sem_inc(S["at_done"], 2)
            scale = 128.0 ** -0.5
            with dve.Fori(0, 4) as i:
                for b in range(2):
                    sc, sf = M["scores"][:, b], M["soft"][:, b]
                    dve.wait_ge(S["at_scored"], 2 * i + b + 3)
                    dve.wait_ge(S["at_p_turned"], 2 * i + b + 1)
                    dve.tensor_tensor(sc, psum[:, 4 + b, 0:384], M["causal"][:], ALU.add) \
                        .then_inc(S["at_masked"], 1)
                    dve.wait_ge(S["at_masked"], 2 * i + b + 1)
                    dve.tensor_reduce(sf[:, 0:1], sc[:, 0:P], AX_X, ALU.max) \
                        .then_inc(S["at_max"], 1)
                    dve.tensor_reduce(sf[:, 1:2], sc[:, P:384], AX_X, ALU.max) \
                        .then_inc(S["at_max"], 1)
                    dve.wait_ge(S["at_max"], 4 * i + 2 * b + 2)
                    dve.tensor_scalar(sf[:, 2:4], sf[:, 0:2], -scale, None, ALU.mult) \
                        .then_inc(S["at_shift"], 1)
                for b in range(2):
                    sc, sf = M["scores"][:, b], M["soft"][:, b]
                    dve.wait_ge(S["at_exp"], 4 * i + 2 * b + 2)
                    dve.reciprocal(sf[:, 6:8], sf[:, 4:6]).then_inc(S["at_sum"], 1)
                    dve.wait_ge(S["at_sum"], 2 * i + b + 1)
                    for k, (at, wide) in enumerate(((0, P), (P, 256))):
                        dve.tensor_scalar(sc[:, at:at + wide], sc[:, at:at + wide],
                                          sf[:, 6 + k:7 + k], None, ALU.mult) \
                            .then_inc(S["at_probs"], 1)
                for b in range(2):
                    dve.wait_ge(S["at_out"], 2 * i + b + 3)
                    dve.tensor_copy(proj[:, bass.ds(2 * i + b, 1)][:, 0], psum[:, 4 + b, 0:256]) \
                        .then_inc(S["at_done"], 1)
            dve.wait_ge(S["at_done"], 10)
            dve.sem_inc(S["attention_over"], 1)
            with dve.Fori(0, 6) as i:
                for b in range(2):
                    dve.wait_ge(S["sc_first"], 2 * i + b + 1)
                    for k in range(1, 4):
                        if k > 1:
                            dve.wait_ge(S["sc_taps"], 6 * i + 3 * b + k - 1)
                        cv = M["conv_out"][:, b, k:T1]
                        dve.scalar_tensor_tensor(
                            out=cv, in0=proj[:, bass.ds(2 * i + b + 32, 1)][:, 0, 0:T1 - k],
                            scalar=par[:, bass.ds(2 * i + b + (c_sconv + 12 * (3 - k)), 1)],
                            in1=cv, op0=ALU.mult, op1=ALU.add).then_inc(S["sc_taps"], 1)
            step, srows = M["step"], M["step_rows"]
            s_ = [step[0:16, k] for k in range(7)]
            dve.wait_ge(S["heads_landed"], 32)
            dve.tensor_scalar(s_[0], proj[0:16, 44], head_par[0:16, 0:1], None, ALU.add) \
                .then_inc(S["dt_abs"], 1)
            dve.wait_ge(S["dt_abs"], 1)
            dve.scalar_tensor_tensor(out=s_[1], in0=s_[0], scalar=-1.0, in1=s_[0], op0=ALU.mult,
                                     op1=ALU.max).then_inc(S["dt_abs"], 1)
            dve.wait_ge(S["dt_ln"], 1)
            link(dve.scalar_tensor_tensor(out=s_[3], in0=s_[0], scalar=0.0, in1=s_[2],
                                          op0=ALU.max, op1=ALU.add))
            dve.wait_ge(S["dt_exp"], 2)
            link(dve.tensor_scalar(s_[4], s_[3], head_par[0:16, 2:3], -1.0, ALU.mult, ALU.mult))
            for c in range(2):
                cs = slice(c * CH, c * CH + CH)
                dve.tensor_tensor_scan(s_[5][:, cs], ones[0:16, 0:CH], s_[4][:, cs], 0.0,
                                       ALU.mult, ALU.add).then_inc(S["dt_cum"], 1)
            dve.wait_ge(S["dt_end"], 1)
            dve.tensor_tensor(s_[6][:, 0:P], s_[6][:, 0:P], s_[3][:, 0:P], ALU.mult) \
                .then_inc(S["ssd_vector"], 1)
            dve.wait_ge(*ssd_pe.at("dt_turned"))
            dve.tensor_copy(srows[:], psum[:, 4, 0:80].rearrange("p (k h) -> p k h", h=16)) \
                .then_inc(S["ssd_vector"], 1)
            dve.wait_ge(*ssd_pe.at("cb_made"))
            dve.wait_ge(S["made"], MADE_UPTO)
            dve.tensor_tensor(M["cb"][:], psum[:, 5].rearrange("p (k l) -> p k l", l=P),
                              over(M["upto"][:], 1, 4), ALU.mult).then_inc(S["ssd_vector"], 1)
            dve.wait_ge(*ssd_pe.at("b_turned"))
            dve.tensor_copy(M["b_rows"][:], psum[:, 6, 0:256].rearrange("p (k l) -> p k l", l=P)) \
                .then_inc(S["ssd_vector"], 1)
            dve.wait_ge(*ssd_dve.at("dt_rows"))
            for n in range(4):
                c, half = divmod(n, 2)
                dve.wait_ge(S["xs_turned"], n + 1)
                bank = (7, 4, 5, 6)[n]
                xt = psum[:, bank].rearrange("p (h k) -> p h k", k=64)
                hs = slice(8 * half, 8 * half + 8)
                dst = M["xdt"][:, c, 512 * half:512 * half + 512]
                dve.tensor_tensor(dst.rearrange("p (h k) -> p h k", k=64), xt,
                                  over(srows[:, 2 + c, hs], 2, 64), ALU.mult) \
                    .then_inc(S["xdt_made"], 1)
                if c == 0:
                    dst = M["xdte"][:, 512 * half:512 * half + 512]
                    dve.tensor_tensor(dst.rearrange("p (h k) -> p h k", k=64), xt,
                                      over(srows[:, 4, hs], 2, 64), ALU.mult) \
                        .then_inc(S["xdt_made"], 1)
            for g in range(2):
                dve.wait_ge(S["st_made"], g + 1)
                dve.tensor_copy(M["state0"][:, g], psum[:, 7 - 3 * g]).then_inc(S["st_placed"], 1)

            def gate(hb):
                dve.wait_ge(S["sg_used"], 2 * hb + 2)
                if hb == 0:
                    dve.wait_ge(S["z_silu"], 1)
                for p in range(2):
                    j = 2 * hb + p
                    link(dve.scalar_tensor_tensor(
                        out=proj[:, 32 + j], in0=proj[:, 32 + j], scalar=col(c_dskip + j),
                        in1=psum[:, 6 + hb % 2, 256 * p:256 * p + 256], op0=ALU.mult, op1=ALU.add))
                dve.tensor_tensor(proj[:, 32 + 2 * hb:34 + 2 * hb], proj[:, 32 + 2 * hb:34 + 2 * hb],
                                  proj[:, 24 + 2 * hb:26 + 2 * hb], ALU.mult) \
                    .then_inc(S["y_gated"], 1)

            for n in range(8):
                hb, c = divmod(n, 2)
                h4 = slice(4 * hb, 4 * hb + 4)
                cs = slice(c * CH, c * CH + CH)
                if n >= 2:
                    dve.wait_ge(S["sg_row"], n - 1)
                dg = M["diag"][0:16, n % 2].rearrange("p (h l) -> p h l", l=CH)
                dve.tensor_tensor(dg, over(s_[5][:, cs], 1, 4), over(ident[0:16, h4], 2, CH),
                                  ALU.mult).then_inc(S["sg_diag"], 1)
                seg = M["seg"][:, n % 2]
                seg3 = seg.rearrange("p (h l) -> p h l", l=CH)
                dve.wait_ge(S["sg_row"], n + 1)
                dve.tensor_tensor(seg3, psum[:, 4 + n % 2].rearrange("p (h l) -> p h l", l=CH),
                                  over(srows[:, c, h4], 2, CH), ALU.subtract) \
                    .then_inc(S["sg_seg"], 1)
                dve.wait_ge(S["sg_seg"], 2 * n + 1)
                dve.tensor_scalar(seg, seg, 0.0, None, ALU.min).then_inc(S["sg_seg"], 1)
                if n >= 2:
                    dve.wait_ge(S["sg_used"], n - 1)
                if c:
                    dve.wait_ge(S["sg_e1"], (n + 1) // 2)
                    e3 = M["cte"][:, 0].rearrange("p (h l) -> p h l", l=CH)
                    c3 = M["cte"][:, 1].rearrange("p (h l) -> p h l", l=CH)
                    dve.tensor_tensor(c3, e3, over(proj[:, 42 + hb // 2, cs], 1, 4), ALU.mult) \
                        .then_inc(S["sg_cte"], 1)
                dve.wait_ge(S["sg_exp"], n + 1)
                dve.tensor_tensor(M["gmat"][:, n % 2].rearrange("p (h l) -> p h l", l=CH), seg3,
                                  over(M["cb"][:, 2 * (hb // 2) + c], 1, 4), ALU.mult) \
                    .then_inc(S["sg_g"], 1)
                if n in (3, 5, 7):
                    gate((n - 3) // 2)
            gate(3)
            for g in range(2):
                dve.wait_ge(S["yn_ss"], g + 1)
                link(dve.tensor_scalar(M["y_r"][:, g], psum[:, 4 + g, 0:T1], 1.0 / 512, EPS,
                                       ALU.mult, ALU.add))
                dve.reciprocal(M["y_r"][:, g], M["y_r"][:, g]).then_inc(S["yn_inv"], 1)
            for j in range(8):
                dve.wait_ge(S["yn_rstd"], j // 4 + 1)
                dve.scalar_tensor_tensor(out=proj[:, 32 + j], in0=proj[:, 32 + j],
                                         scalar=col(c_snorm + j), in1=M["y_r"][:, j // 4],
                                         op0=ALU.mult, op1=ALU.mult).then_inc(S["yn_done"], 1)
            dve.wait_ge(S["mix_hi"], 1)
            dve.tensor_tensor(act_lo[:, 0:8, TC1], proj[:, 0:8], act_hi[:, 0:8, TC1].bitcast(F32),
                              ALU.subtract).then_inc(S["mix_lo"], 1)
            dve.wait_ge(S["mix_hi"], 2)
            dve.tensor_tensor(act_lo[:, 8:16, TC1], proj[:, 32:40],
                              act_hi[:, 8:16, TC1].bitcast(F32), ALU.subtract) \
                .then_inc(S["mix_lo"], 1)
            u, g0 = stream.unit0["out1"], stream.group0["out1"]
            lo_group(u + 4)
            leave(u + 4, g0 % 2, resid[:, 0:2, TC1], T1, how="added")
            with dve.Fori(1, 4) as i:
                for b in range(2):
                    g = 2 * i + b
                    lo_group(u + 4 * g)
                    leave(u + 4 * g, (g0 + b + 1) % 2, resid[:, bass.ds(2 * g - 2, 2), TC1], T1,
                          how="added")
            lo_group(stream.unit0["ffn1"])
            leave(u + 32, (g0 + 7) % 2, resid[:, 14:16, TC1], T1, how="added")

            def ffn(name, T, tc, cc, vals, acc, u_next):
                u, g0, n0 = stream.unit0[name], stream.group0[name], chunks_before[name]
                pair0 = g0 % 2
                nt = 8 if vals else 4
                up, conv, ff = M["up"], M["conv"], M["ff"]

                def taps(i, t0):
                    for t in range(t0, t0 + 4):
                        dve.wait_ge(S["ff_first"], nt * i + (8 * n0 + t + 1))
                        c = (44 if t >= 4 else 0) + t % 4
                        for k in (1, 2):
                            if k == 2:
                                dve.wait_ge(S["ff_taps"], 2 * nt * i + (16 * n0 + 2 * t + 1))
                            cv = conv[:, t, k:T]
                            dve.scalar_tensor_tensor(
                                out=cv, in0=up[:, t, 0:T - k],
                                scalar=par[:, bass.ds(4 * i + (c + cc[2 - k]), 1)],
                                in1=cv, op0=ALU.mult, op1=ALU.add) \
                                .then_inc(S["ff_taps"], 1)

                def product(i):
                    dve.wait_ge(S["ff_silu"], i + (n0 + 1))
                    dve.wait_ge(S["ff_taps"], 2 * nt * i + (16 * n0 + 2 * nt))
                    v = conv[:, 4:8, 0:T] if vals else up[:, 4:8, 0:T]
                    dve.tensor_tensor(ff[:, :, 0:T], conv[:, 0:4, 0:T], v, ALU.mult) \
                        .then_inc(S["ff_ff"], 1)

                def product_lo(i):
                    dve.wait_ge(S["ff_ffhi"], i + (n0 + 1))
                    dve.tensor_tensor(M["ff_lo"][:, :, 0:T], ff[:, :, 0:T],
                                      M["ff_hi"][:, :, 0:T].bitcast(F32), ALU.subtract) \
                        .then_inc(S["ff_fflo"], 1)

                def leave_up(v, j):
                    leave(v + 4 * j + 4, (pair0 + j) % 2, up[:, 2 * j:2 * j + 2, 0:T], T)

                def leave_down(v, d):
                    leave(v + d + 1, (pair0 + d) % 2, acc[:, 2 * d:2 * d + 2, tc], T, how="added")

                for j in range(1, 4):
                    lo_group(u + 4 * j)
                    leave_up(u, j - 1)
                leave_up(u, 3)
                with dve.Fori(1, FCH) as i:
                    v = u + 24 * i - 8
                    lo_group(v)
                    taps(i - 1, 0)
                    lo_group(v + 4)
                    if vals:
                        taps(i - 1, 4)
                    leave_up(v, 0)
                    lo_group(v + 8)
                    product(i - 1)
                    leave_up(v, 1)
                    lo_group(v + 12)
                    product_lo(i - 1)
                    leave_up(v, 2)
                    w = v + 16
                    lo(w, 0)
                    lo(w + 1, 1)
                    leave_up(v, 3)
                    for d in range(8):
                        if d + 2 < 8:
                            lo(w + d + 2, (d + 2) % 4)
                        leave_down(w, d)
                v = u + 24 * FCH - 8
                taps(FCH - 1, 0)
                if vals:
                    taps(FCH - 1, 4)
                product(FCH - 1)
                lo_group(v)
                product_lo(FCH - 1)
                for d in range(8):
                    if d + 4 < 8:
                        lo(v + d + 4, d % 4)
                    leave_down(v, d)
                if u_next is not None:
                    lo_group(u_next)

            norm_lo("n1", c_norm2, TC1)
            rstd_of("n1", T1, D, EPS)
            ffn("ffn1", T1, TC1, c_fconv, True, resid, stream.unit0["in2"])
            norm_lo("n2", c_premix, TC2)
            rstd_of("n2", T2, D, EPS)
            u, g0 = stream.unit0["in2"], stream.group0["in2"]
            z2, low = M["z2"], M["low"]
            rk_a, rk_b, bonus = M["rk_a"], M["rk_b"], M["bonus"]
            t5, t6, t7 = M["t5"], M["t6"], M["t7"]
            link(dve.memset(z2[:, :, 0:PAD], 0.0))
            link(dve.memset(low[:, :, 0:PAD], 0.0))
            lo_group(u + 4)
            leave(u + 4, g0 % 2, low[0:96, 0:2, PAD:RT], T2, 96)
            lo_group(u + 8)
            leave(u + 8, (g0 + 1) % 2, low[:, 2:4, PAD:RT], T2)
            lo_group(u + 12)
            leave(u + 12, g0 % 2, z2[:, 0:2, PAD:RT], T2)
            lo_group(u + 16)
            leave(u + 16, (g0 + 1) % 2, z2[:, 2:4, PAD:RT], T2)
            lo_group(u + 20)
            leave(u + 20, g0 % 2, z2[:, 4:6, PAD:RT], T2)
            with dve.Fori(0, (IN2_RKV - 4) // 2) as i:
                for b in range(2):
                    n = 2 * i + (b + 3)
                    lo_group(u + 12 + 4 * n)
                    leave(u + 12 + 4 * n, (g0 + b + 1) % 2, z2[:, bass.ds(2 * n, 2), PAD:RT], T2)
            lo_group(u + 8 + 4 * IN2_RKV)
            leave(u + 8 + 4 * IN2_RKV, (g0 + 1) % 2, z2[:, 22:24, PAD:RT], T2)
            for t in (t5, rk_a, rk_b, bonus):
                link(dve.memset(t[:, :, 0:PAD], 0.0))

            def shift(t, n, cols_, low_before=None, rows_=P):
                cur, before = t[0:rows_, :, PAD:RT], t[0:rows_, :, PAD - 1:RT - 1]
                link(dve.tensor_tensor(t7[0:rows_, 0:n, 0:T2], before, cur, ALU.subtract))
                for j in range(n):
                    ins = dve.scalar_tensor_tensor(
                        out=t[0:rows_, j, PAD:RT], in0=t7[0:rows_, j, 0:T2],
                        scalar=par[0:rows_, cols_ + j:cols_ + j + 1], in1=t[0:rows_, j, PAD:RT],
                        op0=ALU.mult, op1=ALU.add)
                    if low_before is None:
                        link(ins)
                    else:
                        ins.then_inc(S["low_shifted"], 1)
                        dve.wait_ge(S["low_shifted"], low_before + j + 1)

            shift(low[:, 0:2], 2, c_mulow, 0, 96)
            shift(low[:, 2:4], 2, c_mug, 2)
            shift(z2[:, 8:16], 8, c_mu + 8)
            shift(z2[:, 0:8], 8, c_mu)
            shift(z2[:, 16:24], 8, c_mu + 16)
            for j in range(8):
                dve.tensor_scalar(rk_a[:, j], z2[:, 8 + j], col(c_kk + j), None, ALU.mult) \
                    .then_inc(S["kk_scaled"], 1)
            dve.wait_ge(S["low_out"], 8)
            link(dve.tensor_scalar(t5[:, :, PAD:RT], t5[:, :, PAD:RT], -DECAY, None, ALU.mult))
            dve.wait_ge(S["made"], MADE_SCAN)
            for j in range(8):
                link(dve.tensor_tensor_scan(t6[:, j], M["scan_keep"][:], t5[:, j], 0.0,
                                            ALU.mult, ALU.add))
            for j in range(8):
                dve.wait_ge(S["kk_ss"], j + 1)
                ins = dve.tensor_scalar(t7[:, j], psum[:, 4 + j % 4, 0:RT], 1e-24, None, ALU.max)
                ins.then_inc(S["kk_max"], 1)
            dve.wait_ge(S["kk_max"], 8)
            dve.reciprocal(t7[:], t7[:]).then_inc(S["kk_inv"], 1)
            dve.wait_ge(S["kk_root"], 1)
            link(dve.tensor_tensor(rk_a[:], rk_a[:], t7[:], ALU.mult))
            dve.wait_ge(S["low_out"], 16)
            for j in range(8):
                link(dve.tensor_scalar(t7[:, j], rk_b[:, j], -1.0, col(c_ka + j), ALU.add,
                                       ALU.mult))
            kz = z2[:, 8:16].rearrange("p a b -> p (a b)")
            f7 = t7[:].rearrange("p a b -> p (a b)")
            link(dve.scalar_tensor_tensor(out=kz, in0=f7, scalar=1.0, in1=kz, op0=ALU.add,
                                          op1=ALU.mult))
            link(dve.tensor_tensor(t7[:], z2[:, 0:8], z2[:, 8:16], ALU.mult))
            for j in range(8):
                dve.tensor_scalar(t7[:, j], t7[:, j], col(c_rk + j), None, ALU.mult) \
                    .then_inc(S["bo_scaled"], 1)
            link(dve.tensor_tensor(rk_b[:], rk_b[:], rk_a[:], ALU.mult))
            for j in range(8):
                dve.wait_ge(S["bo_sum"], j + 1)
                dve.tensor_tensor(bonus[:, j, PAD:RT], psum[:, 4 + j % 4, 0:T2],
                                  z2[:, 16 + j, PAD:RT], ALU.mult).then_inc(S["bo_made"], 1)
            dve.tensor_tensor(t5[:], t6[:], t5[:], ALU.subtract).then_inc(S["decay_prev"], 1)
            fa, f5 = (t[:].rearrange("p a b -> p (a b)") for t in (rk_a, t5))
            dve.wait_ge(S["decay_exp"], 1)
            dve.scalar_tensor_tensor(out=fa, in0=fa, scalar=-1.0, in1=f5, op0=ALU.mult,
                                     op1=ALU.mult).then_inc(S["a_made"], 1)
            dve.wait_ge(S["decay_exp"], 2)
            dve.tensor_tensor(rk_b[:], rk_b[:], t5[:], ALU.mult).then_inc(S["bk_made"], 1)
            dve.tensor_tensor(z2[:, 8:16], z2[:, 8:16], t5[:], ALU.mult) \
                .then_inc(S["bk_made"], 1)
            dve.wait_ge(S["decay_exp"], 3)
            link(dve.tensor_copy(M["wc"][:], t5[:].rearrange("p a (c t) -> p a c t", t=RC)
                                 [:, :, :, RC - 1]))
            dve.tensor_tensor(z2[:, 0:8], z2[:, 0:8], t5[:], ALU.mult) \
                .then_inc(S["rpre_over"], 1)
            fs, mt, st, ru = M["fs"], M["mt"], M["state"], M["ru"]
            dve.wait_ge(S["rpre_over"], 1)
            link(dve.memset(mt[:], 0.0))
            dve.wait_ge(S["made"], MADE_RWKV)

            def heads4(name):
                return M[name][0:RB].rearrange("s (p e) t -> s e p t", e=2)

            def mask4(name):
                m = M[name][0:RB]
                return over(over(m, 1, 2), 1, 2)

            def one_mask(name):
                return over(M[name][0:RB], 1, 2)

            def masked(dst, banks, at, wide, mask):
                src = psum[0:RB, banks:banks + 2, 0:2 * wide] \
                    .rearrange("s e (p w) -> s e p w", p=2)[:, :, :, at:at + RB]
                dve.tensor_tensor(heads4(dst), src, mask4(mask), ALU.mult) \
                    .then_inc(S["rw_vector"], 1)

            dve.sem_inc(S["rw_end"], 1)
            with dve.Fori(0, 4) as q:
                dve.wait_ge(S["rw_end"], 3 * q + 1)
                dve.memset(st[:], 0.0).then_inc(S["rw_s"], 1)
                with dve.Fori(0, 3) as tt:
                    it = 3 * q + tt
                    dve.wait_ge(*rw_pe.at("lt", it))
                    masked("ldt", 4, 0, 192, "m_ldt")
                    masked("lot", 4, 0, 192, "m_lot")
                    masked("rbt", 4, RB, 192, "m_r")
                    dve.wait_ge(*rw_pe.at("ak", it))
                    masked("akt", 6, 0, 192, "m_a")
                    masked("rkt", 6, RB, 192, "m_r")
                    dve.wait_ge(*rw_dve.at("ldt", it))
                    dve.tensor_tensor(M["p1"][0:RB], M["ldt"][0:RB], over(ident[0:RB, 0:RB], 1, 4),
                                      ALU.add).then_inc(S["rw_vector"], 1)
                    dve.wait_ge(*rw_pe.at("l", it))
                    masked("ld", 4, 0, RB, "m_ld")
                    dve.wait_ge(*rw_pe.at("l2", it))
                    dve.tensor_copy(M["l2"][0:RB], four(4)).then_inc(S["rw_vector"], 1)
                    dve.wait_ge(*rw_pe.at("l4t", it))
                    dve.tensor_copy(M["l4t"][0:RB], four(5)).then_inc(S["rw_vector"], 1)
                    dve.wait_ge(*rw_pe.at("p2m", it))
                    dve.tensor_tensor(p2[0:RB], four(7), M["p1"][0:RB], ALU.add) \
                        .then_inc(S["rw_vector"], 1)
                    dve.wait_ge(*rw_pe.at("p3m", it))
                    dve.wait_ge(*rw_dve.at("p2", it))
                    dve.tensor_tensor(p3[0:RB], four(6), p2[0:RB], ALU.add) \
                        .then_inc(S["rw_vector"], 1)
                    dve.wait_ge(*rw_pe.at("p4m", it))
                    dve.wait_ge(*rw_dve.at("p3", it))
                    dve.tensor_tensor(p4[0:RB], four(7), p3[0:RB], ALU.add) \
                        .then_inc(S["rw_vector"], 1)
                    dve.wait_ge(*rw_pe.at("zm", it))
                    dve.tensor_copy(M["zz"][0:RB].rearrange("p h k -> p (h k)"),
                                    psum[0:RB, 5, 0:512]).then_inc(S["rw_vector"], 1)
                    dve.wait_ge(*rw_pe.at("xm", it))
                    dve.tensor_tensor(M["uu"][0:RB].rearrange("p a h k -> p h a k"),
                                      psum[0:RB, 6, 0:512].rearrange("p (h a k) -> p h a k", h=4,
                                                                     a=2),
                                      M["y1"][0:RB].rearrange("p h (a k) -> p h a k", a=2),
                                      ALU.add) \
                        .then_inc(S["rw_vector"], 1)
                    dve.wait_ge(*rw_pe.at("rum", it))
                    dve.tensor_tensor(ru[:], psum[:, 7, 0:192].rearrange("p (a t) -> p a t", a=2),
                                      fs[:, :, 1], ALU.add).then_inc(S["rw_vector"], 1)
                    dve.wait_ge(*rw_pe.at("mtm", it))
                    for e in range(2):
                        h = slice(64 * e, 64 * e + 64)
                        src = psum[h, 4:7, 0:256].rearrange("p c (a k) -> p c a k", a=2)[:, :, :, h]
                        dve.tensor_tensor(mt[h, :, :, h], src,
                                          over(over(ident[h, h], 1, 2), 1, 3), ALU.add) \
                            .then_inc(S["rw_vector"], 1)
                    for c in range(3):
                        dve.wait_ge(*rw_pe.at(f"step{c}", it))
                        for e in range(2):
                            h = slice(64 * e, 64 * e + 64)
                            src = psum[h, 4 + c, 0:256].rearrange("p (a k) -> p a k", a=2)[:, :, h]
                            w = M["wc"][h, bass.ds(2 * q, 2), bass.ds(3 * tt + c, 1)]
                            dve.tensor_tensor(st[h, :, h], src, w.to_broadcast([64, 2, 64]),
                                              ALU.mult).then_inc(S["rw_s"], 1)
                    dve.tensor_copy(rk_a[:, bass.ds(2 * q, 2), bass.ds(RB * tt, RB)],
                                    psum[:, 7, 256:448].rearrange("p (a t) -> p a t", a=2)) \
                        .then_inc(S["rw_end"], 1)
            t8 = M["t8"]
            dve.wait_ge(S["rw_end"], 13)
            for j in range(8):
                dve.wait_ge(S["gn_mean"], j + 1)
                ya = rk_a[:, j, PAD:RT]
                dve.scalar_tensor_tensor(out=ya, in0=psum[:, 4 + j % 4, 0:T2], scalar=-1.0 / 64,
                                         in1=ya, op0=ALU.mult, op1=ALU.add) \
                    .then_inc(S["gn_centred"], 1)
            for j in range(8):
                dve.wait_ge(S["gn_ss"], j + 1)
                dve.tensor_scalar(t8[:, j], psum[:, 4 + j % 4, 0:RT], 1.0 / 64, GN_EPS, ALU.mult,
                                  ALU.add).then_inc(S["gn_used"], 1)
            dve.wait_ge(S["gn_used"], 8)
            dve.reciprocal(t8[:], t8[:]).then_inc(S["gn_inv"], 1)
            dve.wait_ge(S["gn_root"], 1)
            link(dve.tensor_tensor(rk_a[:], rk_a[:], t8[:], ALU.mult))
            for j in range(8):
                link(dve.tensor_scalar(rk_a[:, j], rk_a[:, j], col(c_lnw + j), col(c_lnb + j),
                                       ALU.mult, ALU.add))
            link(dve.tensor_tensor(rk_a[:], rk_a[:], bonus[:], ALU.add))
            for j in range(8):
                dve.wait_ge(S["gate_made"], j + 1)
                dve.tensor_tensor(rk_a[:, j, PAD:RT], rk_a[:, j, PAD:RT],
                                  psum[:, 4 + j % 4, 0:T2], ALU.mult).then_inc(S["gn_done"], 1)
            dve.wait_ge(S["gn_done"], 8)

            bch, cv, yc = M["bch"], M["cv"], M["y_conv"]
            u2 = u + 8 + 4 * IN2_RKV

            def conv_tail(q, n):
                dve.wait_ge(S["evicted"], n)
                dve.tensor_tensor(bch[:, 1], bch[:, 1], bch[:, 2], ALU.mult) \
                    .then_inc(S["cv_step"], 1)
                dve.wait_ge(S["cv_step"], 7 * q + 1)
                for p in range(2):
                    def c(k):
                        return par[:, bass.ds(2 * q + (p + c_conv2 + 8 * k), 1)]
                    dve.tensor_scalar(cv[:, p], bch[:, 1, p], c(2), None, ALU.mult) \
                        .then_inc(S["cv_step"], 1)
                    for k in (1, 2):
                        dve.wait_ge(S["cv_step"], 7 * q + 1 + 3 * p + k)
                        dve.scalar_tensor_tensor(out=cv[:, p, k:T2], in0=bch[:, 1, p, 0:T2 - k],
                                                 scalar=c(2 - k), in1=cv[:, p, k:T2],
                                                 op0=ALU.mult, op1=ALU.add) \
                            .then_inc(S["cv_step"], 1)
                dve.wait_ge(S["cv_step"], 7 * q + 7)
                dve.tensor_tensor(yc[:, bass.ds(2 * q, 2)], cv[:], bch[:, 0], ALU.mult) \
                    .then_inc(S["cv_done"], 1)

            gc = g0 + 2 + IN2_RKV
            dve.sem_inc(S["cv_done"], 1)
            with dve.Fori(0, 2) as i:
                for b in range(2):
                    q = 2 * i + b
                    dve.wait_ge(S["cv_done"], q + 1)
                    for m in range(3):
                        v = u2 + 24 * i + 12 * b + 4 * m + 4
                        lo_group(v)
                        leave(v, (gc + 3 * b + m) % 2, bch[:, m], T2)
                    conv_tail(q, 3 * q + (gc + 3))
            dve.wait_ge(S["mix_hi"], 3)
            dve.tensor_tensor(act_lo[:, 8:16], rk_a[:, :, PAD:RT], act_hi[:, 8:16].bitcast(F32),
                              ALU.subtract).then_inc(S["mix_lo"], 1)
            dve.wait_ge(S["mix_hi"], 4)
            dve.tensor_tensor(act_lo[:, 0:8], yc[:], act_hi[:, 0:8].bitcast(F32),
                              ALU.subtract).then_inc(S["mix_lo"], 1)
            mixed = M["mixed"]
            u, g0 = stream.unit0["out2"], stream.group0["out2"]
            lo_group(u + 4)
            leave(u + 4, g0 % 2, mixed[:, 0:2], T2, how="copied")
            with dve.Fori(1, 4) as i:
                for b in range(2):
                    g = 2 * i + b
                    lo_group(u + 4 * g)
                    leave(u + 4 * g, (g0 + b + 1) % 2, mixed[:, bass.ds(2 * g - 2, 2)], T2,
                          how="copied")
            lo_group(stream.unit0["ffn2"])
            leave(u + 32, (g0 + 7) % 2, mixed[:, 14:16], T2, how="copied")

            def post(before, c):
                for k in range(KD):
                    dve.scalar_tensor_tensor(out=mixed[:, k], in0=mixed[:, k], scalar=col(c + k),
                                             in1=rstd[:], op0=ALU.mult, op1=ALU.mult) \
                        .then_inc(S["post_scaled"], 1)
                    dve.wait_ge(S["post_scaled"], before + k + 1)
                    dve.tensor_tensor(resid[:, k], resid[:, k], mixed[:, k], ALU.add) \
                        .then_inc(S["post"], 1)

            rstd_of("n3", T2, D, EPS)
            dve.wait_ge(S["evicted"], stream.group0["ffn2"])
            post(0, c_postmix)
            norm_lo("n4", c_preffn, TC2)
            rstd_of("n4", T2, D, EPS)
            link(dve.memset(mixed[:], 0.0))
            ffn("ffn2", T2, TC2, c_gconv, False, mixed, None)
            rstd_of("n5", T2, D, EPS)
            dve.wait_ge(S["evicted"], stream.groups)
            post(KD, c_postffn)
            for n in range(8):
                tt, g = divmod(n, 4)
                dve.wait_ge(S["out_turned"], n + 1)
                dve.tensor_copy(M["out_rows"][:, tt, 512 * g:512 * g + 512], psum[:, 4 + n % 4]) \
                    .then_inc(S["out_copied"], 1)

        @block.tensor
        def _(pe):
            def unit(u, slot, pair, hi_, lo_, k0, T, first, last, m=P, ncol=2, shift=P):
                pe.wait_ge(S["lo_done"], u + 1)
                for r in range(RK):
                    for c in range(ncol):
                        out_ = psum[0:m, 2 * pair + c, 0:T]
                        at = 256 * r + shift * c
                        wh, wl = w_hi[:, slot, at:at + m], w_lo[:, slot, at:at + m]
                        xh, xl = hi_[:, k0 + r], lo_[:, k0 + r]
                        pe.matmul(out_, wh, xh, start=first and r == 0, stop=False)
                        pe.matmul(out_, wh, xl, start=False, stop=False)
                        mm = pe.matmul(out_, wl, xh, start=False, stop=last and r == RK - 1)
                mm.then_inc(S["unit_used"], 1)

            def bank_free(g):
                if not isinstance(g, int) or g >= 2:
                    pe.wait_ge(S["evicted"], g - 1)

            def group(u, g, pair, tc, T, ready=None, **how):
                bank_free(g)
                for j in range(4):
                    if ready:
                        pe.wait_ge(*ready(j))
                    unit(u + j, j, pair, act_hi[:, :, tc], act_lo[:, :, tc], 4 * j, T,
                         j == 0, j == 3, **how)

            def sum_over(name, T):
                pe.wait_ge(*norm_at(name, "add", 5))
                pe.matmul(psum[:, 7, 0:T], ones[:], ss_part[:, 0:T], start=True, stop=True) \
                    .then_inc(S["norm_ss"], 1)

            TC1, TC2 = slice(T0, T2), slice(0, T2)

            pe.wait_ge(S["made"], MADE_CONSTS)
            pe.wait_ge(S["x_landed"], 48)
            for n in range(8):
                tt, g = divmod(n, 4)
                if n >= 4:
                    pe.wait_ge(S["x_placed"], n - 3)
                for k in range(4):
                    c = P * (4 * g + k)
                    mm = pe.transpose(psum[:, 4 + n % 4, P * k:P * k + P],
                                      M["x_rows"][:, tt, c:c + P], ident[:])
                mm.then_inc(S["x_turned"], 1)
            pe.wait_ge(S["x_placed"], 5)
            for k in range(KD):
                mm = pe.transpose(psum[:, 4, T0 * k:T0 * k + T0],
                                  M["meta_rows"][0:T0, P * k:P * k + P], ident[0:T0, 0:T0])
            mm.then_inc(S["x_turned"], 1)
            pe.wait_ge(S["x_placed"], 7)
            pe.wait_ge(S["params_landed"], 16 * n_param_loads[0])
            pe.wait_ge(S["d_placed"], 1)
            for n in range(NPACK):
                mm = pe.transpose(psum[:, 5 + n // 4, P * (n % 4):P * (n % 4) + P],
                                  M["packs"][:, n], ident[:])
                if n == 3 or n == NPACK - 1:
                    mm.then_inc(S["par_turned"], 1)
            u = stream.unit0["in1"]
            group(u, 0, 0, TC1, T1, lambda j: norm_at("n0", "lo", 4 * j + 4))
            pe.wait_ge(S["par_placed"], 2)
            sum_over("n0", T1)
            group(u + 4, 1, 1, TC1, T1)
            with pe.Fori(1, G_IN1 // 2) as i:
                for b in range(2):
                    group(u + 8 * i + 4 * b, 2 * i + b, b, TC1, T1)
            group(u + 4 * G_IN1, G_IN1, G_IN1 % 2, TC1, T1, ncol=1)
            pe.sem_inc(S["at_scored"], 2)
            pe.sem_inc(S["at_v_turned"], 2)
            pe.sem_inc(S["at_p_turned"], 2)
            pe.sem_inc(S["at_out"], 2)
            for n in range(4):
                pe.wait_ge(S["qk_sq"], n + 1)
                if n >= 2:
                    pe.wait_ge(S["qk_inv"], n - 1)
                for k in range(2):
                    mm = pe.matmul(psum[:, 4 + 2 * (n % 2) + k], ones[:],
                                   M["head_sq"][:, 2 * k:2 * k + 2].rearrange("p a t -> p (a t)"),
                                   start=True, stop=True)
                mm.then_inc(S["qk_ss"], 1)
            pe.wait_ge(S["qk_done"], 4)
            with pe.Fori(0, 4) as i:
                for b in range(2):
                    h = 2 * i + b
                    qs, vs = M["q_still"][:, b], M["v_still"][:, b]
                    pe.wait_ge(S["at_still"], 2 * h + 2)
                    pe.wait_ge(S["at_done"], h + 1)
                    kt = proj[:, bass.ds(h + 8, 1)][:, 0]
                    pe.matmul(psum[:, 4 + b, 0:P], qs[:, 0:P], kt[:, 0:P], start=True, stop=True)
                    pe.matmul(psum[:, 4 + b, P:384], qs[:, P:256], kt, start=True, stop=True) \
                        .then_inc(S["at_scored"], 1)
                    pe.wait_ge(S["at_pt"], h + 1)
                    pe.transpose(psum[:, 6 + b, 0:P], vs[:, 0:P], ident[:])
                    pe.transpose(psum[:, 6 + b, P:256], vs[:, P:256], ident[:]) \
                        .then_inc(S["at_v_turned"], 1)
                for b in range(2):
                    h = 2 * i + b
                    pe.wait_ge(S["at_probs"], 2 * h + 2)
                    pe.wait_ge(S["at_v"], h + 1)
                    for k in range(3):
                        mm = pe.transpose(psum[:, 6 + b, P * k:P * k + P],
                                          M["scores"][:, b, P * k:P * k + P], ident[:])
                    mm.then_inc(S["at_p_turned"], 1)
                for b in range(2):
                    h = 2 * i + b
                    pe.wait_ge(S["at_pt"], h + 3)
                    vr, pt = M["v_rows"][:, b], M["probs_t"][:, b]
                    pe.matmul(psum[:, 4 + b, 0:P], vr[:, 0:P], pt[:, 0:P], start=True, stop=True)
                    pe.matmul(psum[:, 4 + b, P:256], vr[:, 0:P], pt[:, P:256],
                              start=True, stop=False)
                    pe.matmul(psum[:, 4 + b, P:256], vr[:, P:256], pt[:, 256:384],
                              start=False, stop=True) \
                        .then_inc(S["at_out"], 1)
            step = M["step"]
            pe.wait_ge(S["attention_over"], 1)
            pe.wait_ge(S["dt_cum"], 2)
            pe.wait_ge(*ssd_dve.at("dt_w"))
            for k, (row, at) in enumerate(((5, 0), (5, P), (3, 0), (3, P), (6, 0))):
                mm = pe.transpose(psum[:, 4, 16 * k:16 * k + 16], step[0:16, row, at:at + P],
                                  ident[0:16, 0:16])
            mm.then_inc(S["ssd_tensor"], 1)
            pe.wait_ge(S["sc_silu"], 12)
            for g in range(2):
                for c in range(2):
                    cs = slice(c * CH, c * CH + CH)
                    mm = pe.matmul(psum[:, 5, P * (2 * g + c):P * (2 * g + c) + P],
                                   proj[:, 40 + g, cs], proj[:, 42 + g, cs], start=True, stop=True)
            mm.then_inc(S["ssd_tensor"], 1)
            for g in range(2):
                mm = pe.transpose(psum[:, 6, P * g:P * g + P], proj[:, 40 + g, 0:P], ident[:])
            mm.then_inc(S["ssd_tensor"], 1)
            for n in range(4):
                c, half = divmod(n, 2)
                bank = (7, 4, 5, 6)[n]
                if n:
                    pe.wait_ge(*ssd_dve.at(("dt_rows", "cb_masked", "b_placed")[n - 1]))
                for k in range(4):
                    mm = pe.transpose(psum[:, bank, P * k:P * k + P],
                                      proj[:, 32 + 4 * half + k, c * CH:c * CH + CH], ident[:])
                mm.then_inc(S["xs_turned"], 1)
            pe.wait_ge(*ssd_dve.at("b_placed"))
            pe.wait_ge(S["xdt_made"], 6)
            for g in range(2):
                pe.matmul(psum[:, 7 - 3 * g], M["b_rows"][:, g], M["xdte"][:, 512 * g:512 * g + 512],
                          start=True, stop=True).then_inc(S["st_made"], 1)
            pe.wait_ge(S["st_placed"], 2)

            def rows_out(n):
                pe.wait_ge(S["sg_diag"], n + 1)
                if n >= 2:
                    pe.wait_ge(S["sg_seg"], 2 * n - 2)
                    if n % 2:
                        pe.wait_ge(S["sg_e1"], (n - 1) // 2)
                pe.matmul(psum[:, 4 + n % 2], ones[0:16, :], M["diag"][0:16, n % 2],
                          start=True, stop=True).then_inc(S["sg_row"], 1)

            rows_out(0)
            for n in range(8):
                hb, c = divmod(n, 2)
                if n < 7:
                    rows_out(n + 1)
                pe.wait_ge(S["sg_g"], n + 1)
                if c:
                    pe.wait_ge(S["sg_cte"], hb + 1)
                elif hb >= 2:
                    pe.wait_ge(S["y_gated"], hb - 1)
                for k in range(4):
                    h = 4 * hb + k
                    e, p = h % 2, (h // 2) % 2
                    at = 256 * p + CH * c
                    out_ = psum[64 * e:64 * e + 64, 6 + hb % 2, at:at + CH]
                    mm = pe.matmul(out_, M["xdt"][:, c, 64 * h:64 * h + 64],
                                   M["gmat"][:, n % 2, CH * k:CH * k + CH], start=True, stop=not c)
                    if c:
                        mm = pe.matmul(out_, M["state0"][:, h // 8, 64 * (h % 8):64 * (h % 8) + 64],
                                       M["cte"][:, 1, CH * k:CH * k + CH], start=False, stop=True)
                mm.then_inc(S["sg_used"], 1)
            for g in range(2):
                pe.wait_ge(S["yn_sq"], g + 1)
                for k in range(4):
                    mm = pe.matmul(psum[:, 4 + g, 0:T1], ones[:], M["y_sq"][:, k],
                                   start=(k == 0), stop=(k == 3))
                mm.then_inc(S["yn_ss"], 1)
            u, g0 = stream.unit0["out1"], stream.group0["out1"]
            pe.wait_ge(S["mix_lo"], 2)
            with pe.Fori(0, 4) as i:
                for b in range(2):
                    group(u + 8 * i + 4 * b, g0 + 2 * i + b, (g0 + b) % 2, TC1, T1)

            def ffn(name, norm, T, tc):
                u, g0, n0 = stream.unit0[name], stream.group0[name], chunks_before[name]
                pair0 = g0 % 2

                def ups(v, g):
                    for j in range(4):
                        group(v + 4 * j, g + j, (pair0 + j) % 2, tc, T)

                def downs(v, g, i):
                    pe.wait_ge(S["ff_fflo"], i + (n0 + 1))
                    for d in range(8):
                        bank_free(g + d)
                        unit(v + d, d % 4, (pair0 + d) % 2, M["ff_hi"][:, :, 0:T],
                             M["ff_lo"][:, :, 0:T], 0, T, True, True)

                group(u, g0, pair0, tc, T, lambda j: norm_at(norm, "lo", 4 * j + 4))
                sum_over(norm, T)
                for j in range(1, 4):
                    group(u + 4 * j, g0 + j, (pair0 + j) % 2, tc, T)
                with pe.Fori(1, FCH) as i:
                    ups(u + 24 * i - 8, 12 * i - 8 + g0)
                    downs(u + 24 * i + 8, 12 * i - 4 + g0, i - 1)
                downs(u + 24 * FCH - 8, g0 + 12 * FCH - 8, FCH - 1)

            ffn("ffn1", "n1", T1, TC1)
            u, g0 = stream.unit0["in2"], stream.group0["in2"]
            group(u, g0, g0 % 2, TC2, T2, lambda j: norm_at("n2", "lo", 4 * j + 4), m=96, shift=96)
            sum_over("n2", T2)
            group(u + 4, g0 + 1, (g0 + 1) % 2, TC2, T2)
            with pe.Fori(0, IN2_RKV // 2) as i:
                for b in range(2):
                    group(u + 8 + 8 * i + 4 * b, g0 + 2 + 2 * i + b, (g0 + b) % 2, TC2, T2)
            low, t7, rk_a = M["low"], M["t7"], M["rk_a"]
            pe.wait_ge(S["low_landed"], 32)
            pe.wait_ge(S["low_act"], 1)
            for n in range(16):
                if n >= 4:
                    pe.wait_ge(S["low_out"], n - 3)
                j = n % 8
                pe.matmul(psum[:, 4 + n % 4, 0:T2], M["w_low"][0:96, n // 8, P * j:P * j + P],
                          low[0:96, n // 8, PAD:RT], start=True, stop=True) \
                    .then_inc(S["low_up"], 1)
            pe.wait_ge(S["kk_sq"], 1)
            for j in range(8):
                if j == 0:
                    pe.wait_ge(S["low_out"], 16)
                if j >= 4:
                    pe.wait_ge(S["kk_max"], j - 3)
                pe.matmul(psum[:, 4 + j % 4, 0:RT], halves[:], t7[:, j], start=True, stop=True) \
                    .then_inc(S["kk_ss"], 1)
            for j in range(8):
                pe.wait_ge(S["bo_scaled"], j + 1)
                if j >= 4:
                    pe.wait_ge(S["bo_made"], j - 3)
                pe.matmul(psum[:, 4 + j % 4, 0:T2], halves[:], t7[:, j, PAD:RT], start=True,
                          stop=True).then_inc(S["bo_sum"], 1)
            fs, uu, mt, st = M["fs"], M["uu"], M["mt"], M["state"]
            b_tok, kv, ru = M["b_tok"], M["kv_tok"], M["ru"]
            halfp = [slice(64 * e, 64 * e + 64) for e in range(2)]

            def each_head(lhs, rhs_, bank, wide=RB):
                for h in range(4):
                    mm = pe.matmul(psum[0:RB, bank, wide * h:wide * h + wide], lhs[0:RB, h],
                                   rhs_(h), start=True, stop=True)
                mm.then_inc(S["rw_tensor"], 1)

            pe.wait_ge(S["bo_made"], 8)
            with pe.Fori(0, 4) as q:
                with pe.Fori(0, 3) as tt:
                    it = 3 * q + tt
                    n = it + 1
                    pe.wait_ge(S["rw_still"], 3 * it + 3)
                    pe.wait_ge(S["rw_still_act"], 2 * it + 2)
                    for k, bank in ((2, 4), (3, 6)):
                        for p in range(2):
                            for e in range(2):
                                mm = pe.matmul(psum[0:RB, bank + e, 192 * p:192 * p + 192],
                                               fs[halfp[e], p, k], fs[halfp[e], p, 0:2],
                                               start=True, stop=True)
                        mm.then_inc(S["rw_tensor"], 1)
                    pe.wait_ge(*rw_dve.at("rbt", it))
                    for p in range(2):
                        for e in range(2):
                            mm = pe.matmul(psum[0:RB, 4 + e, RB * p:RB * p + RB],
                                           fs[halfp[e], p, 0], fs[halfp[e], p, 2],
                                           start=True, stop=True)
                    mm.then_inc(S["rw_tensor"], 1)
                    pe.wait_ge(*rw_dve.at("rkt", it))
                    for ks, bank in (((0, 2), 6), ((3, 4), 7)):
                        for a, k in enumerate(ks):
                            for p in range(2):
                                at = P * (2 * a + p)
                                mm = pe.transpose(psum[0:RB, bank, at:at + P], fs[:, p, k],
                                                  ident[:])
                        mm.then_inc(S["rw_tensor"], 1)
                    pe.wait_ge(*rw_dve.at("ld", it))
                    each_head(M["ldt"], lambda h: M["ld"][0:RB, h], 4)
                    each_head(M["ld"], lambda h: M["ldt"][0:RB, h], 5)
                    pe.wait_ge(*rw_act.at("b_tok", it))
                    pe.wait_ge(*rw_act.at("kv", it))
                    each_head(M["akt"], lambda h: kv[0:RB, 1, 64 * h:64 * h + 64], 6, 64)
                    pe.wait_ge(*rw_dve.at("l2_out", it))
                    pe.wait_ge(*rw_act.at("l2t_out", it))
                    pe.wait_ge(*rw_dve.at("p1", it))
                    each_head(M["l2t"], lambda h: M["l2"][0:RB, h], 4)
                    each_head(M["l2"], lambda h: M["l2t"][0:RB, h], 5)
                    each_head(M["l2"], lambda h: M["p1"][0:RB, h], 7)
                    pe.wait_ge(*rw_act.at("l4_out", it))
                    pe.wait_ge(*rw_dve.at("l4t_out", it))
                    each_head(M["l4t"], lambda h: M["l4"][0:RB, h], 4)
                    pe.wait_ge(*rw_dve.at("p2", it))
                    pe.wait_ge(*rw_act.at("rhs_v", it))
                    each_head(M["l4"], lambda h: p2[0:RB, h], 6)
                    pe.wait_ge(*rw_act.at("l8_out", it))
                    pe.wait_ge(*rw_dve.at("p3", it))
                    each_head(l8, lambda h: p3[0:RB, h], 7)
                    pe.wait_ge(*rw_dve.at("p4", it))
                    each_head(p4, lambda h: M["rhs"][0:RB, h], 4, P)
                    pe.wait_ge(*rw_act.at("y1_out", it))
                    each_head(M["lot"], lambda h: M["y1"][0:RB, h], 5, P)
                    pe.wait_ge(*rw_dve.at("z", it))
                    each_head(p4, lambda h: M["zz"][0:RB, h], 6, P)
                    pe.wait_ge(*rw_dve.at("u", it))
                    for p in range(2):
                        for e in range(2):
                            h = 2 * p + e
                            mm = pe.matmul(psum[halfp[e], 7, RB * p:RB * p + RB],
                                           uu[0:RB, 0, h], M["rbt"][0:RB, h],
                                           start=(p == 0), stop=True, skip_group_check=True)
                    mm.then_inc(S["rw_tensor"], 1)
                    for c in range(3):
                        rows32 = slice(RC * c, RC * c + RC)
                        for p in range(2):
                            mm = pe.matmul(psum[:, 4 + c, P * p:P * p + P],
                                           uu[rows32, 0, 2 * p:2 * p + 2].rearrange("p h k -> p (h k)"),
                                           b_tok[rows32, P * p:P * p + P],
                                           start=True, stop=True)
                    mm.then_inc(S["rw_tensor"], 1)
                    pe.wait_ge(*rw_dve.at("ru", it))
                    for p in range(2):
                        for e in range(2):
                            h = 2 * p + e
                            o = psum[halfp[e], 7, 256 + RB * p:256 + RB * p + RB]
                            pe.matmul(o, uu[0:RB, 1, h], M["rbt"][0:RB, h], start=(p == 0),
                                      stop=False, skip_group_check=True)
                            pe.matmul(o, kv[0:RB, 1, 64 * h:64 * h + 64], M["rkt"][0:RB, h],
                                      start=False, stop=False, skip_group_check=True)
                    pe.wait_ge(*rw_dve.at("mt1", it))
                    for c in range(3):
                        rows32 = slice(RC * c, RC * c + RC)
                        for p in range(2):
                            o = psum[:, 4 + c, P * p:P * p + P]
                            pe.matmul(o, b_tok[rows32, P * p:P * p + P],
                                      uu[rows32, 1, 2 * p:2 * p + 2], start=(p == 0),
                                      stop=False, skip_group_check=True)
                            pe.matmul(o, kv[rows32, 0, P * p:P * p + P],
                                      kv[rows32, 1, P * p:P * p + P], start=False, stop=False,
                                      skip_group_check=True)
                        pe.wait_ge(S["rw_s"], 19 * q + 1 + 6 * tt + 2 * c)
                        for p in range(2):
                            at = 256 + RB * p + RC * c
                            pe.matmul(psum[:, 7, at:at + RC], st[:, p],
                                      ru[:, p, RC * c:RC * c + RC], start=False, stop=True,
                                      skip_group_check=True)
                        for p in range(2):
                            mm = pe.matmul(psum[:, 4 + c, P * p:P * p + P], mt[:, c, p], st[:, p],
                                           start=False, stop=True, skip_group_check=True)
                        mm.then_inc(S["rw_tensor"], 1)
            t8 = M["t8"]
            pe.wait_ge(S["rw_end"], 13)
            for j in range(8):
                if j >= 4:
                    pe.wait_ge(S["gn_centred"], j - 3)
                pe.matmul(psum[:, 4 + j % 4, 0:T2], halves[:], rk_a[:, j, PAD:RT], start=True,
                          stop=True).then_inc(S["gn_mean"], 1)
            pe.wait_ge(S["gn_sq"], 1)
            for j in range(8):
                if j >= 4:
                    pe.wait_ge(S["gn_used"], j - 3)
                pe.matmul(psum[:, 4 + j % 4, 0:RT], halves[:], t8[:, j], start=True, stop=True) \
                    .then_inc(S["gn_ss"], 1)
            pe.wait_ge(S["gup_landed"], 16)
            pe.wait_ge(S["gn_inv"], 1)
            for j in range(8):
                if j >= 4:
                    pe.wait_ge(S["gn_done"], j - 3)
                for k in range(2):
                    mm = pe.matmul(psum[:, 4 + j % 4, 0:T2], M["g_up"][:, k, P * j:P * j + P],
                                   low[:, 2 + k, PAD:RT], start=(k == 0), stop=(k == 1))
                mm.then_inc(S["gate_made"], 1)
            u2, gc = u + 8 + 4 * IN2_RKV, g0 + 2 + IN2_RKV
            with pe.Fori(0, 2) as i:
                for m in range(6):
                    group(u2 + 24 * i + 4 * m, gc + 6 * i + m, (gc + m) % 2, TC2, T2)
            u, g0 = stream.unit0["out2"], stream.group0["out2"]
            pe.wait_ge(S["mix_lo"], 4)
            with pe.Fori(0, 4) as i:
                for b in range(2):
                    group(u + 8 * i + 4 * b, g0 + 2 * i + b, (g0 + b) % 2, TC2, T2)
            sum_over("n3", T2)
            ffn("ffn2", "n4", T2, TC2)
            sum_over("n5", T2)
            for n in range(8):
                tt, g = divmod(n, 4)
                if n == 3:
                    pe.wait_ge(*norm_at("n5", "ms", 1))
                if n >= 4:
                    pe.wait_ge(S["out_copied"], n - 3)
                pe.wait_ge(S["post"], KD + 4 * g + 4)
                for k in range(4):
                    mm = pe.transpose(psum[:, 4 + n % 4, P * k:P * k + P],
                                      resid[:, 4 * g + k, T0 + P * tt:T0 + P * tt + P], ident[:])
                mm.then_inc(S["out_turned"], 1)


_INS = [
    "x", "norm1_w", "w_in", "q_norm_w", "k_norm_w", "ssm_conv_w", "ssm_conv_b", "dt_bias", "a_log",
    "d_skip", "ssm_norm_w", "w_out", "norm2_w", "w_up", "ffn_conv_w", "ffn_conv_b", "w_down",
    "meta_tokens_2", "g_pre_mix_2", "w_in_2", "conv_w_2", "mu_rwkv_2", "w_decay_up_2", "w0_2",
    "a_up_2", "a0_2", "g_up_2", "k_k_2", "k_a_2", "r_k_2", "ln_x_w_2", "ln_x_b_2", "w_out_2",
    "g_post_mix_2", "g_pre_ffn_2", "w_gate_up_2", "conv_ffn_2", "w_down_2", "g_post_ffn_2",
]


def kernel(**inputs):
    import numpy as np
    from concourse import bacc
    from concourse.bass_utils import run_bass_kernel_spmd

    nc = bacc.Bacc("TRN2", target_bir_lowering=False, num_devices=1)
    arrays, args = {}, []
    for name in _INS:
        a = np.ascontiguousarray(inputs[name])
        arrays[f"in_{name}"] = a
        args.append(nc.dram_tensor(f"in_{name}", a.shape, mybir.dt.from_np(a.dtype),
                                   kind="ExternalInput").ap())
    x = arrays["in_x"]
    out = nc.dram_tensor("out_x", x.shape, mybir.dt.from_np(x.dtype), kind="ExternalOutput").ap()
    two_blocks(nc, *args, out)
    got = run_bass_kernel_spmd(nc, [arrays], core_ids=[0])
    return got.results[0]["out_x"]
```

```python
import math
from contextlib import ExitStack

import concourse.bass as bass
from concourse import mybir

ALU = mybir.AluOpType
ACT = mybir.ActivationFunctionType
F32 = mybir.dt.float32
F32R = mybir.dt.float32r
AX_X = mybir.AxisListType.X

P = 128
BIG = 1.0e30


class Semaphores:

    def __init__(self, nc):
        self.nc, self.made = nc, {}

    def __getitem__(self, name):
        if name not in self.made:
            self.made[name] = self.nc.alloc_semaphore(name)
        return self.made[name]


class Tally:

    def __init__(self, sem, names, start=0):
        self.sem, self.names, self.start = sem, names.split(), start

    def at(self, name, again=0):
        return self.sem, again * len(self.names) + (self.start + self.names.index(name) + 1)


class Stream:

    def __init__(self):
        self.units = self.groups = 0
        self.unit0, self.group0 = {}, {}

    def phase(self, name, groups, units):
        self.unit0[name], self.group0[name] = self.units, self.groups
        self.units += units
        self.groups += groups


def two_blocks(
    nc, x, norm1_w, w_in, q_norm_w, k_norm_w, ssm_conv_w, ssm_conv_b, dt_bias, a_log, d_skip,
    ssm_norm_w, w_out, norm2_w, w_up, ffn_conv_w, ffn_conv_b, w_down, meta_tokens_2,
    g_pre_mix_2, w_in_2, conv_w_2, mu_rwkv_2, w_decay_up_2, w0_2, a_up_2, a0_2, g_up_2, k_k_2,
    k_a_2, r_k_2, ln_x_w_2, ln_x_b_2, w_out_2, g_post_mix_2, g_pre_ffn_2, w_gate_up_2,
    conv_ffn_2, w_down_2, g_post_ffn_2, out,
):
    _, SEQ, D = x.shape
    META = meta_tokens_2.shape[0]
    T1, T2 = SEQ, SEQ + META
    T0 = META
    LEAD = 2
    T3 = SEQ + LEAD
    TC1, TC2, TC3 = slice(T0, T2), slice(0, T2), slice(T0 - LEAD, T2)
    KD = D // P
    AH = 8
    SH = dt_bias.shape[1]
    SG, SN, SPD = 2, 128, 64
    CH = 128
    DFF = w_down.shape[1]
    FCH = DFF // 512
    assert D == 2048 and SEQ == 256 and META == 16 and DFF == FCH * 512
    RK = 4
    NSLOT = 4
    RT = 288
    PAD = RT - T2
    RB = 96
    RC = 32
    RW = 8

    EPS = 1e-6
    GN_EPS = 64e-5
    DECAY = math.exp(-0.5)

    stream = Stream()
    G_IN1 = 22
    stream.phase("in1", G_IN1 + 1, 4 * (G_IN1 + 1))
    stream.phase("out1", 16, 32)
    stream.phase("ffn1", 4 * FCH + 8 * FCH, 24 * FCH)
    stream.phase("in2", 26, 104)
    stream.phase("out2", 16, 32)
    stream.phase("ffn2", 4 * FCH + 8 * FCH, 24 * FCH)

    chunks_before = {"ffn1": 0, "ffn2": FCH}

    S = Semaphores(nc)
    landed = [S[f"raw_landed_{j}"] for j in range(NSLOT)]

    rw_pe = Tally(S["rw_tensor"], "lt ak l tab tkv l2 l2t akv l4 l4t p2m l8 p3m p4m y1 zm xm rum "
                                  "mtm step0 step1 step2")
    rw_dve = Tally(S["rw_vector"], "ldt lot rbt akt rkt p1 ld l2_out l4t_out p2 p3 p4 z u ru mt0 "
                                   "mt1", start=3)
    rw_act = Tally(S["rw_scalar"], "rhs_a b_tok kv l2t_out rhs_v l4_out l8_out y1_out")
    ssd_pe = Tally(S["ssd_tensor"], "dt_turned cb_made b_turned")
    ssd_dve = Tally(S["ssd_vector"], "dt_w dt_rows cb_masked b_placed")
    MADE_CONSTS = 6
    MADE_CAUSAL = MADE_CONSTS + 3
    MADE_UPTO = MADE_CAUSAL + 2
    MADE_SCAN = MADE_UPTO + 2
    MADE_RWKV = MADE_SCAN + 5 + 2 + 2 + 2 + 2 + 4 + 1
    NORM_SIGNALS = dict(sq=4, add=5, ss=1, ms=1, inv=1, rstd=1, hi=16, lo=16)
    HI_NORMS = ("n0", "n1", "n2", "n4")

    def norm_at(name, what, n):
        before = HI_NORMS.index(name) if what in ("hi", "lo") else int(name[1])
        return S["norm_" + what], NORM_SIGNALS[what] * before + n

    def sb(name, shape, dtype=F32):
        return nc.alloc_sbuf_tensor(name, shape, dtype)

    raw = sb("raw", [P, NSLOT, RK * 256])
    w_hi = sb("w_hi", [P, NSLOT, RK * 256], F32R)
    w_lo = sb("w_lo", [P, NSLOT, RK * 256], F32R)
    resid = sb("resid", [P, KD, T2])
    act_hi = sb("act_hi", [P, KD, T2], F32R)
    act_lo = sb("act_lo", [P, KD, T2], F32R)
    ident = sb("ident", [P, P])
    ones = sb("ones", [P, P])
    halves = sb("halves", [P, P])
    rstd = sb("rstd", [P, T2])
    ss_part = sb("ss_part", [P, T2])
    head_par = sb("head_par", [P, 6])

    rows = []

    def rows_of(ap, n):
        at = sum(r[1] for r in rows)
        rows.append((ap, n, at))
        return at

    def flat(ap):
        return ap.rearrange("a d -> (a d)")

    def tiles(ap1, n):
        return ap1.rearrange("(k p) -> k p", p=P), n

    c_dskip = rows_of(None, 8)
    c_norm1 = rows_of(*tiles(flat(norm1_w), 16))
    c_qn = rows_of(q_norm_w, 1)
    c_kn = rows_of(k_norm_w, 1)
    c_sconv = rows_of(ssm_conv_w.rearrange("a j (k p) -> (a j k) p", p=P), 48)
    c_sconvb = rows_of(*tiles(flat(ssm_conv_b), 12))
    c_snorm = rows_of(*tiles(flat(ssm_norm_w), 8))
    c_norm2 = rows_of(*tiles(flat(norm2_w), 16))
    fconv = ffn_conv_w.rearrange("a j (k p) -> (a j) k p", p=P)
    c_fconv = [rows_of(fconv[j], 88) for j in range(3)]
    c_fconvb = rows_of(*tiles(flat(ffn_conv_b), 88))
    c_premix = rows_of(*tiles(g_pre_mix_2, 16))
    c_conv2 = rows_of(conv_w_2.rearrange("j (k p) -> (j k) p", p=P), 24)
    c_mu = rows_of(mu_rwkv_2[0:3072].rearrange("(k p) -> k p", p=P), 24)
    c_mug = rows_of(mu_rwkv_2[3264:3520].rearrange("(k p) -> k p", p=P), 2)
    c_w0 = rows_of(*tiles(w0_2, 8))
    c_a0 = rows_of(*tiles(a0_2, 8))
    c_kk = rows_of(*tiles(k_k_2, 8))
    c_ka = rows_of(*tiles(k_a_2, 8))
    c_rk = rows_of(*tiles(flat(r_k_2), 8))
    c_lnw = rows_of(*tiles(ln_x_w_2, 8))
    c_lnb = rows_of(*tiles(ln_x_b_2, 8))
    c_postmix = rows_of(*tiles(g_post_mix_2, 16))
    c_preffn = rows_of(*tiles(g_pre_ffn_2, 16))
    gconv = conv_ffn_2.rearrange("j (k p) -> j k p", p=P)
    c_gconv = [rows_of(gconv[j], 44) for j in range(3)]
    c_postffn = rows_of(*tiles(g_post_ffn_2, 16))
    c_mulow = rows_of(None, 2)
    NROWS = sum(r[1] for r in rows)
    NPACK = -(-NROWS // P)
    par = sb("par", [P, NPACK * P])
    assert c_mulow // P == (c_mulow + 1) // P

    def col(c):
        return par[:, c:c + 1]


    def shared(shapes, keep=None):
        own = ExitStack()
        got = {n: own.enter_context(nc.sbuf_tensor(n, [P, *s], d)) for n, s, d in shapes}
        if keep is None:
            own.close()
        else:
            keep.enter_context(own)
        return got

    M = {}
    for names in (
        [("packs", [NPACK, P], F32), ("x_rows", [2, D], F32), ("meta_rows", [D], F32)],
        [
            ("proj", [45, T1], F32),
            ("squares1", [8, T2], F32),
            ("head_sq", [4, T1], F32), ("head_r", [4, T1], F32),
            ("q_still", [2, T1], F32), ("v_still", [2, T1], F32),
            ("causal", [384], F32), ("scores", [2, 384], F32), ("probs_t", [2, 384], F32),
            ("v_rows", [2, 2 * P], F32), ("soft", [2, 8], F32),
        ],
        [
            ("proj_ssd", [45, T1], F32), ("upto", [P], F32), ("conv_out", [2, T1], F32),
            ("step", [7, T1], F32), ("step_rows", [5, 16], F32), ("minus_a", [1], F32),
            ("cb", [4, P], F32), ("b_rows", [2, P], F32), ("xdt", [2, 1024], F32),
            ("xdte", [1024], F32), ("state0", [2, 512], F32), ("diag", [2, 512], F32),
            ("seg", [2, 512], F32), ("gmat", [2, 512], F32), ("cte", [2, 512], F32),
            ("y_sq", [4, T1], F32), ("y_r", [2, T1], F32),
        ],
        [
            ("up", [8, T3], F32), ("conv", [8, T1], F32), ("ff", [4, T1], F32),
            ("squares2", [8, T2], F32),
            ("ff_hi", [4, T1], F32R), ("ff_lo", [4, T1], F32R),
            ("last_hi", [4, T1], F32R), ("last_lo", [4, T1], F32R), ("out_rows", [2, D], F32),
        ],
    ):
        M.update(shared(names))
    both = ExitStack()
    M.update(shared([
        ("z2", [24, RT], F32),
        ("rk_a", [RW, RT], F32),
        ("rk_b", [RW, RT], F32),
        ("bonus", [RW, RT], F32), ("low", [4, RT], F32), ("wc", [RW, 9], F32),
    ], both))
    M.update(shared([("squares3", [8, T2], F32)]))
    M.update(shared([
        ("t5", [RW, RT], F32), ("t6", [RW, RT], F32), ("t7", [RW, RT], F32),
        ("w_low", [2, 1024], F32), ("scan_keep", [RT], F32),
    ]))
    M.update(shared([
        ("fs", [2, 5, RB], F32),
        ("ldt", [4, RB], F32), ("lot", [4, RB], F32), ("rbt", [4, RB], F32),
        ("akt", [4, RB], F32), ("rkt", [4, RB], F32), ("ld", [4, RB], F32),
        ("p1", [4, RB], F32), ("l2", [4, RB], F32), ("l2t", [4, RB], F32),
        ("rhs", [4, P], F32), ("y1", [4, P], F32), ("uu", [2, 4, 64], F32),
        ("b_tok", [2 * P], F32), ("kv_tok", [2, 2 * P], F32), ("ru", [2, RB], F32),
        ("mt", [3, 2, P], F32), ("state", [2, P], F32),
        ("m_ldt", [RB], F32), ("m_lot", [RB], F32), ("m_r", [RB], F32), ("m_a", [RB], F32),
        ("m_ld", [RB], F32),
        ("gate_b", [2, T2], F32), ("gate_c", [2, T2], F32),
    ]))
    M.update(shared([("t8", [RW, RT], F32), ("g_up", [2, 1024], F32), ("mixed", [KD, T2], F32)]))
    both.close()

    proj = M["proj"]
    psum = nc.alloc_psum_tensor("psum", [P, 8, 512], F32)
    l8, p2, p3, p4 = M["l2"], M["ld"], M["p1"], M["ldt"]
    l4, l4t, zz = M["akt"], M["l2t"], M["rhs"]
    y_conv = M["z2"][:, 0:8, PAD:RT]

    def over(ap, axis, n):
        wide = ap.unsqueeze(axis)
        shape = list(wide.shape)
        shape[axis] = n
        return wide.to_broadcast(shape)

    def four(bank):
        return psum[0:RB, bank, 0:4 * RB].rearrange("p (h t) -> p h t", t=RB)

    def unit_rows(w):
        return w.rearrange("(j r p) n -> j p r n", r=RK, p=P)

    w_in1, w_out1, w_up1, w_dn1 = (unit_rows(w[0]) for w in (w_in, w_out, w_up, w_down))
    w_in2, w_out2, w_up2, w_dn2 = (unit_rows(w) for w in (w_in_2, w_out_2, w_gate_up_2, w_down_2))
    IN2_LOW, IN2_RKV, IN2_CONV = 2, 12, 12
    n_param_loads = []

    with nc.Block() as block:

        @block.sync
        def _(sp):
            def load(u, slot, src, wide=256):
                if not isinstance(u, int) or u >= NSLOT:
                    sp.wait_ge(S["lo_done"], u - NSLOT + 1)
                dst = raw[:, slot].rearrange("p (r n) -> p r n", r=RK)[:, :, 0:wide]
                sp.dma_start(dst, src).then_inc(landed[slot], 16)

            def load_group(u, w, c0, wide=256):
                for j in range(4):
                    load(u + j, j, w[j][:, :, bass.ds(c0, wide)], wide)

            def half_loads(u, w):
                for half in range(2):
                    with sp.Fori(0, 4) as i:
                        for b in range(2):
                            for j in range(2):
                                load(u + 16 * half + 4 * i + 2 * b + j, 2 * b + j,
                                     w[2 * half + j][:, :, bass.ds(512 * i + 256 * b, 256)])

            sp.dma_start(M["x_rows"][:, 0], x[0, 0:P, :]).then_inc(S["x_landed"], 16)
            sp.dma_start(M["x_rows"][:, 1], x[0, P:2 * P, :]).then_inc(S["x_landed"], 16)
            sp.dma_start(M["meta_rows"][0:META], meta_tokens_2).then_inc(S["x_landed"], 16)
            sp.dma_start(head_par[0:8, 4:6], d_skip.rearrange("a (j b) -> (a j) b", b=2)) \
                .then_inc(S["d_landed"], 16)
            sp.wait_ge(S["packs_cleared"], 1)
            n = 0
            for ap, count, at in rows:
                if ap is None:
                    continue
                done = 0
                while done < count:
                    pack, row = divmod(at + done, P)
                    k = min(count - done, P - row)
                    sp.dma_start(M["packs"][row:row + k, pack], ap[done:done + k]) \
                        .then_inc(S["params_landed"], 16)
                    done += k
                    n += 1
            pack, row = divmod(c_mulow, P)
            sp.dma_start(M["packs"][row:row + 2, pack, 0:96],
                         mu_rwkv_2[3072:3264].rearrange("(a b) -> a b", a=2)) \
                .then_inc(S["params_landed"], 16)
            n_param_loads.append(n + 1)
            sp.dma_start(head_par[0:16, 0:1], dt_bias.rearrange("a h -> h a")) \
                .then_inc(S["heads_landed"], 16)
            sp.dma_start(head_par[0:16, 1:2], a_log.rearrange("a h -> h a")) \
                .then_inc(S["heads_landed"], 16)
            u = stream.unit0["in1"]
            load_group(u, w_in1, 0)
            with sp.Fori(1, G_IN1) as g:
                load_group(u + 4 * g, w_in1, 256 * g)
            load_group(u + 4 * G_IN1, w_in1, 256 * G_IN1, 16)
            half_loads(stream.unit0["out1"], w_out1)

            def ffn_loads(name, w_up, w_dn):
                u = stream.unit0[name]

                def ups(u, i):
                    for j, c0 in enumerate((0, 256, DFF, DFF + 256)):
                        load_group(u + 4 * j, w_up, c0 + 512 * i)

                def downs(u, i):
                    for d in range(8):
                        load(u + d, d % 4, w_dn[bass.ds(i, 1)][0][:, :, 256 * d:256 * d + 256])

                ups(u, 0)
                with sp.Fori(1, FCH) as i:
                    ups(u + 24 * i - 8, i)
                    downs(u + 24 * i + 8, i - 1)
                downs(u + 24 * FCH - 8, FCH - 1)

            ffn_loads("ffn1", w_up1, w_dn1)
            u = stream.unit0["in2"]
            load_group(u, w_in2, 6144, 192)
            load_group(u + 4, w_in2, 6336)
            with sp.Fori(0, IN2_RKV) as g:
                load_group(u + 8 + 4 * g, w_in2, 3072 + 256 * g)
            u = u + 8 + 4 * IN2_RKV
            with sp.Fori(0, 4) as q:
                for j in range(3):
                    load_group(u + 12 * q + 4 * j, w_in2, 1024 * j + 256 * q)
            half_loads(stream.unit0["out2"], w_out2)
            ffn_loads("ffn2", w_up2, w_dn2)
            for tt in range(2):
                sp.wait_ge(S["out_copied"], 4 * tt + 4)
                sp.dma_start(out[0, tt * P:tt * P + P, :], M["out_rows"][:, tt]) \
                    .then_inc(S["stored"], 16)
            sp.wait_ge(S["stored"], 32)

        @block.gpsimd
        def _(pool):
            def select(out, in_, pattern, op, fill, base, mult):
                pool.wait_ge(S["made"], made[0])
                pool.affine_select(out=out, in_=in_, pattern=pattern, compare_op=op, fill=fill,
                                   base=base, channel_multiplier=mult).then_inc(S["made"], 1)
                made[0] += 1

            made = [0]
            for t, v in ((ones, 1.0), (ident, 1.0), (halves, 1.0)):
                pool.memset(t[:], v).then_inc(S["made"], 1)
            made[0] += 3
            select(ident[:], ident[:], [[-1, P]], ALU.is_equal, 0.0, 0, 1)
            h3 = halves[:].rearrange("p (b c) -> p b c", b=2)
            select(h3, h3, [[-64, 2], [0, 64]], ALU.is_ge, 0.0, 0, 1)
            select(h3, h3, [[64, 2], [0, 64]], ALU.is_ge, 0.0, 63, -1)

            def sum_squares(name, sq, T):
                for j in range(1, 4):
                    pool.wait_ge(*norm_at(name, "sq", j + 1))
                    if j > 1:
                        pool.wait_ge(*norm_at(name, "add", j - 1))
                    pool.tensor_tensor(sq[:, 0:4, 0:T], sq[:, 0:4, 0:T], sq[:, 4:8, 0:T], ALU.add) \
                        .then_inc(S["norm_add"], 1)
                pool.wait_ge(*norm_at(name, "add", 3))
                pool.tensor_tensor(sq[:, 0:2, 0:T], sq[:, 0:2, 0:T], sq[:, 2:4, 0:T], ALU.add) \
                    .then_inc(S["norm_add"], 1)
                pool.wait_ge(*norm_at(name, "add", 4))
                pool.tensor_tensor(ss_part[:, 0:T], sq[:, 0, 0:T], sq[:, 1, 0:T], ALU.add) \
                    .then_inc(S["norm_add"], 1)

            sum_squares("n0", M["squares1"], T1)
            pool.memset(M["causal"][:], 0.0).then_inc(S["made"], 1)
            made[0] += 1
            select(M["causal"][:, 0:P], M["causal"][:, 0:P], [[-1, P]], ALU.is_ge, -BIG, 0, 1)
            select(M["causal"][:, P:384], M["causal"][:, P:384], [[-1, 256]], ALU.is_ge, -BIG, P, 1)
            pool.wait_ge(S["qk_done"], 4)
            with pool.Fori(0, 4) as i:
                for b in range(2):
                    pool.wait_ge(S["at_scored"], 2 * i + b + 1)
                    pool.wait_ge(S["at_v_turned"], 2 * i + b + 1)
                    pool.tensor_copy(M["q_still"][:, b], proj[:, bass.ds(2 * i + b, 1)][:, 0]) \
                        .then_inc(S["at_still"], 1)
                    pool.tensor_copy(M["v_still"][:, b], proj[:, bass.ds(2 * i + b + 16, 1)][:, 0]) \
                        .then_inc(S["at_still"], 1)
            pool.wait_ge(S["attention_over"], 1)
            pool.memset(M["upto"][:], 1.0).then_inc(S["made"], 1)
            made[0] += 1
            select(M["upto"][:], M["upto"][:], [[1, P]], ALU.is_ge, 0.0, 0, -1)
            sum_squares("n1", M["squares2"], T1)
            sum_squares("n2", M["squares3"], T2)
            pool.wait_ge(*norm_at("n2", "rstd", 1))
            sk = M["scan_keep"][:].rearrange("p (c t) -> p c t", t=RC)
            pool.memset(M["scan_keep"][:], 1.0).then_inc(S["made"], 1)
            made[0] += 1
            select(sk, sk, [[0, RT // RC], [1, RC]], ALU.is_gt, 0.0, 0, 0)
            pool.wait_ge(S["rpre_over"], 1)
            for n in ("m_ldt", "m_lot", "m_r", "m_a", "m_ld"):
                pool.memset(M[n][0:RB], 1.0).then_inc(S["made"], 1)
            made[0] += 5

            def same(name, w):
                m = M[name][0:RB].rearrange("p (b c) -> p b c", c=w)
                select(m, m, [[-w, RB // w], [0, w]], ALU.is_ge, 0.0, 0, 1)
                select(m, m, [[w, RB // w], [0, w]], ALU.is_ge, 0.0, w - 1, -1)

            def beyond(name, op, sign):
                m = M[name][0:RB]
                select(m, m, [[sign, RB]], op, 0.0, 0, -sign)

            same("m_ldt", 16)
            beyond("m_ldt", ALU.is_gt, 1)
            same("m_r", RC)
            beyond("m_r", ALU.is_ge, 1)
            same("m_a", RC)
            beyond("m_a", ALU.is_gt, 1)
            same("m_ld", 16)
            beyond("m_ld", ALU.is_gt, -1)
            pool.wait_ge(S["made"], made[0])
            pool.tensor_tensor(M["m_lot"][0:RB], M["m_a"][0:RB], M["m_ldt"][0:RB], ALU.subtract) \
                .then_inc(S["made"], 1)
            assert made[0] + 1 == MADE_RWKV
            with pool.Fori(0, 4) as q:
                with pool.Fori(0, 3) as tt:
                    pool.wait_ge(*rw_dve.at("ru", 3 * q + tt - 1))
                    for k, (src, t0) in enumerate((("rk_b", 0), ("z2", 8), ("z2", 16))):
                        pool.tensor_copy(
                            M["fs"][:, :, 2 + k],
                            M[src][:, bass.ds(2 * q + t0, 2), bass.ds(RB * tt, RB)],
                        ).then_inc(S["rw_still"], 1)
            sum_squares("n3", M["squares2"], T3)
            sum_squares("n4", M["squares2"], T3)
            sum_squares("n5", M["squares2"], T1)

        @block.scalar
        def _(act):
            def hi(u, slot):
                act.wait_ge(landed[slot], 16 * (u // 4 + 1) if isinstance(u, int)
                            else landed_at(u, slot))
                if not isinstance(u, int) or u >= NSLOT:
                    act.wait_ge(S["unit_used"], u - NSLOT + 1)
                act.activation(w_hi[:, slot], raw[:, slot], ACT.Copy).then_inc(S["hi_done"], 1)

            def wait_apart(sem, value):
                act.wait_ge(sem, value)
                act.wait_ge(S["par_placed"], 2)

            def landed_at(u, slot):
                return (u - slot) * 4 + 16

            def hi_group(u):
                for j in range(4):
                    hi(u + j, j)

            def square(name, src, sq, j, tc):
                if j >= 2:
                    act.wait_ge(*norm_at(name, "add", j - 1))
                half = sq[:, 0:4] if j == 0 else sq[:, 4:8]
                act.activation(half[:, :, 0:tc.stop - tc.start], src[:, 4 * j:4 * j + 4, tc],
                               ACT.Square).then_inc(S["norm_sq"], 1)

            def norm_tiles(name, c, sq, d, tc):
                for k in (2 * d, 2 * d + 1):
                    act.activation(act_hi[:, k, tc], resid[:, k, tc], ACT.Identity,
                                   scale=col(c + k)).then_inc(S["norm_hi"], 1)
                if d % 2:
                    square(name, resid, sq, d // 2, tc)

            def rstd_root(name, T):
                act.wait_ge(*norm_at(name, "inv", 1))
                act.activation(rstd[:, 0:T], rstd[:, 0:T], ACT.Sqrt).then_inc(S["norm_rstd"], 1)

            hi_group(stream.unit0["in1"])
            act.wait_ge(S["x_placed"], 9)
            act.wait_ge(S["par_placed"], 2)
            for d in range(8):
                norm_tiles("n0", c_norm1, M["squares1"], d, TC1)
            rstd_root("n0", T1)
            u = stream.unit0["in1"]
            with act.Fori(1, G_IN1) as g:
                hi_group(u + 4 * g)
            hi_group(u + 4 * G_IN1)
            hi_group(stream.unit0["out1"])
            act.wait_ge(S["evicted"], 16 // 2)
            for n in range(4):
                if n:
                    act.wait_ge(S["qk_ss"], n)
                act.activation(M["head_sq"][:], proj[:, 4 * n:4 * n + 4], ACT.Square) \
                    .then_inc(S["qk_sq"], 1)
                act.wait_ge(S["qk_inv"], n + 1)
                act.activation(M["head_r"][:], M["head_r"][:], ACT.Sqrt).then_inc(S["qk_rstd"], 1)
            scale = 128.0 ** -0.5
            act.sem_inc(S["at_pt"], 2)
            with act.Fori(0, 4) as i:
                for b in range(2):
                    act.wait_ge(S["at_v_turned"], 2 * i + b + 3)
                    act.wait_ge(S["at_out"], 2 * i + b + 1)
                    act.activation(M["v_rows"][:, b], psum[:, 6 + b, 0:256], ACT.Copy) \
                        .then_inc(S["at_v"], 1)
                for b in range(2):
                    act.wait_ge(S["at_shift"], 2 * i + b + 1)
                    for k, (lo, wide) in enumerate(((0, P), (P, 256))):
                        s = M["scores"][:, b, lo:lo + wide]
                        act.activation(s, s, ACT.Exp, bias=M["soft"][:, b, 2 + k:3 + k], scale=scale,
                                       accum_out=M["soft"][:, b, 4 + k:5 + k]) \
                            .then_inc(S["at_exp"], 1)
                for b in range(2):
                    act.wait_ge(S["at_p_turned"], 2 * i + b + 3)
                    act.wait_ge(S["at_out"], 2 * i + b + 1)
                    act.activation(M["probs_t"][:, b], psum[:, 6 + b, 0:384], ACT.Copy) \
                        .then_inc(S["at_pt"], 1)
            act.wait_ge(S["attention_over"], 1)
            for n in range(12):
                if n >= 2:
                    act.wait_ge(S["sc_silu"], n - 1)
                act.activation(M["conv_out"][:, n % 2], proj[:, 32 + n], ACT.Identity,
                               bias=col(c_sconvb + n), scale=col(c_sconv + 36 + n)) \
                    .then_inc(S["sc_first"], 1)
                if n:
                    act.wait_ge(S["sc_taps"], 3 * n)
                    act.activation(proj[:, 31 + n], M["conv_out"][:, (n - 1) % 2], ACT.Silu) \
                        .then_inc(S["sc_silu"], 1)
            act.wait_ge(S["sc_taps"], 36)
            act.activation(proj[:, 43], M["conv_out"][:, 1], ACT.Silu).then_inc(S["sc_silu"], 1)
            act.activation(proj[:, 24:32], proj[:, 24:32], ACT.Silu).then_inc(S["z_silu"], 1)
            step, srows = M["step"], M["step_rows"]
            act.wait_ge(S["dt_abs"], 2)
            act.activation(step[0:16, 2], step[0:16, 1], ACT.Exp, scale=-1.0) \
                .then_inc(S["dt_exp"], 1)
            act.wait_ge(S["heads_landed"], 32)
            act.activation(head_par[0:16, 2:3], head_par[0:16, 1:2], ACT.Exp) \
                .then_inc(S["dt_exp"], 1)
            act.wait_ge(S["dt_exp"], 1)
            act.activation(step[0:16, 2], step[0:16, 2], ACT.Ln, bias=1.0).then_inc(S["dt_ln"], 1)
            act.wait_ge(S["dt_cum"], 2)
            act.activation(step[0:16, 6, 0:P], step[0:16, 5, 0:P], ACT.Exp, scale=-1.0,
                           bias=step[0:16, 5, P - 1:P]).then_inc(S["dt_end"], 1)
            for n in range(8):
                if n % 2:
                    act.wait_ge(S["sg_row"], n + 1)
                    act.wait_ge(S["sg_seg"], 2 * n + 1)
                    if n > 2:
                        act.wait_ge(S["sg_cte"], (n - 1) // 2)
                    act.activation(M["cte"][:, 0], psum[:, 4 + n % 2], ACT.Exp) \
                        .then_inc(S["sg_e1"], 1)
                act.wait_ge(S["sg_seg"], 2 * n + 2)
                act.activation(M["seg"][:, n % 2], M["seg"][:, n % 2], ACT.Exp) \
                    .then_inc(S["sg_exp"], 1)
            for g in range(2):
                act.wait_ge(S["y_gated"], 2 * g + 2)
                if g:
                    act.wait_ge(S["yn_ss"], 1)
                act.activation(M["y_sq"][:], proj[:, 32 + 4 * g:36 + 4 * g], ACT.Square) \
                    .then_inc(S["yn_sq"], 1)
            for g in range(2):
                act.wait_ge(S["yn_inv"], g + 1)
                act.activation(M["y_r"][:, g], M["y_r"][:, g], ACT.Sqrt).then_inc(S["yn_rstd"], 1)
            act.activation(act_hi[:, 0:8, TC1], proj[:, 0:8], ACT.Copy).then_inc(S["mix_hi"], 1)
            act.wait_ge(S["yn_done"], 8)
            act.activation(act_hi[:, 8:16, TC1], proj[:, 32:40], ACT.Copy) \
                .then_inc(S["mix_hi"], 1)
            u, g0 = stream.unit0["out1"], stream.group0["out1"]
            with act.Fori(1, 5) as g:
                hi_group(u + 4 * g)
            for d in range(8):
                for k in range(2):
                    hi(u + 20 + 2 * d + k, (2 * d + k) % 4)
                if d < 4:
                    act.wait_ge(S["evicted"], g0 + 9 + d)
                    norm_tiles("n1", c_norm2, M["squares2"], d, TC1)
            act.wait_ge(S["unit_used"], u + 32)
            for d in range(4, 8):
                act.wait_ge(S["evicted"], g0 + 9 + d)
                norm_tiles("n1", c_norm2, M["squares2"], d, TC1)

            def ffn(name, lead, cc, cb, vals, last_step):
                u, g0, n0 = stream.unit0[name], stream.group0[name], chunks_before[name]
                nt = 8 if vals else 4
                K1 = len(cc) - 1

                def first_taps(i):
                    for t in range(nt):
                        c = (44 if t >= 4 else 0) + t % 4
                        how = dict(scale=par[:, bass.ds(4 * i + (c + cc[K1]), 1)])
                        if cb is not None:
                            how["bias"] = par[:, bass.ds(4 * i + (c + cb), 1)]
                        act.activation(M["conv"][:, t], M["up"][:, t, lead:lead + T1],
                                       ACT.Identity, **how).then_inc(S["ff_first"], 1)

                def silu(i):
                    act.wait_ge(S["ff_taps"], 2 * nt * i + (16 * n0 + 8))
                    act.activation(M["conv"][:, 0:4], M["conv"][:, 0:4], ACT.Silu) \
                        .then_inc(S["ff_silu"], 1)

                def product_hi(i, u_down, dst):
                    act.wait_ge(S["ff_ff"], i + (n0 + 1))
                    if u_down is not None:
                        act.wait_ge(S["unit_used"], u_down)
                    act.activation(dst[:], M["ff"][:], ACT.Copy).then_inc(S["ff_ffhi"], 1)

                def while_up(i, v):
                    hi_group(v)
                    wait_apart(S["evicted"], 12 * i - 8 + g0)
                    first_taps(i - 1)
                    hi_group(v + 4)
                    silu(i - 1)
                    hi_group(v + 8)
                    product_hi(i - 1, v, M["ff_hi"])
                    hi_group(v + 12)

                for j in range(1, 4):
                    hi_group(u + 4 * j)
                with act.Fori(1, FCH - 1) as i:
                    v = u + 24 * i - 8
                    while_up(i, v)
                    hi_group(v + 16)
                    hi_group(v + 20)
                i = FCH - 1
                w = u + 24 * i + 8
                while_up(i, w - 16)
                hi_group(w)
                act.wait_ge(S["evicted"], 12 * i - 4 + g0)
                first_taps(i)
                hi(w + 4, 0)
                hi(w + 5, 1)
                silu(i)
                for k in range(2, 5):
                    hi(w + 4 + k, k % 4)
                product_hi(i, None, M["last_hi"])
                for k in range(5, 8):
                    hi(w + 4 + k, k % 4)
                for d in range(8):
                    if d < 4 or w + 12 + d < stream.units:
                        hi(w + 12 + d, d % 4)
                    act.wait_ge(S["evicted"], g0 + 12 * FCH - 7 + d)
                    last_step(d)

            rstd_root("n1", T1)
            ffn("ffn1", 0, c_fconv, c_fconvb, True,
                lambda d: norm_tiles("n2", c_premix, M["squares3"], d, TC2))
            rstd_root("n2", T2)
            act.dma_start(M["w_low"][0:96, 0], w_decay_up_2).then_inc(S["low_landed"], 16)
            act.dma_start(M["w_low"][0:96, 1], a_up_2).then_inc(S["low_landed"], 16)
            u = stream.unit0["in2"]
            hi_group(u + 4)
            with act.Fori(0, IN2_RKV) as g:
                hi_group(u + 8 + 4 * g)
            hi_group(u + 8 + 4 * IN2_RKV)
            low, t5, t6, t7 = M["low"], M["t5"], M["t6"], M["t7"]
            rk_a, rk_b = M["rk_a"], M["rk_b"]
            act.wait_ge(S["low_shifted"], 4)
            act.activation(low[0:96, 0], low[0:96, 0], ACT.Tanh).then_inc(S["low_act"], 1)
            act.activation(low[:, 2:4], low[:, 2:4], ACT.Sigmoid).then_inc(S["low_act"], 1)
            for n in range(16):
                j = n % 8
                act.wait_ge(S["low_up"], n + 1)
                dst = t5 if n < 8 else rk_b
                act.activation(dst[:, j, PAD:RT], psum[:, 4 + n % 4, 0:T2], ACT.Sigmoid,
                               bias=col((c_w0 if n < 8 else c_a0) + j)).then_inc(S["low_out"], 1)
            act.wait_ge(S["kk_scaled"], 8)
            act.activation(t7[:], rk_a[:], ACT.Square).then_inc(S["kk_sq"], 1)
            act.wait_ge(S["kk_inv"], 1)
            act.activation(t7[:], t7[:], ACT.Sqrt).then_inc(S["kk_root"], 1)
            act.wait_ge(S["decay_prev"], 1)
            act.activation(t5[:], t5[:], ACT.Exp).then_inc(S["decay_exp"], 1)
            act.wait_ge(S["a_made"], 1)
            act.activation(t5[:], t6[:], ACT.Exp, scale=-1.0).then_inc(S["decay_exp"], 1)
            act.wait_ge(S["bk_made"], 2)
            act.activation(t5[:], t6[:], ACT.Exp).then_inc(S["decay_exp"], 1)
            act.wait_ge(S["rpre_over"], 1)
            fs = M["fs"]
            uc = u + 8 + 4 * IN2_RKV
            with act.Fori(0, 4) as q:
                with act.Fori(0, 3) as tt:
                    it = 3 * q + tt
                    wait_apart(*rw_dve.at("ru", it - 1))
                    for k, (src, t0) in enumerate((("rk_a", 0), ("z2", 0))):
                        act.activation(
                            fs[:, :, k], M[src][:, bass.ds(2 * q + t0, 2), bass.ds(RB * tt, RB)],
                            ACT.Copy).then_inc(S["rw_still_act"], 1)
                    act.wait_ge(*rw_pe.at("tab", it))
                    act.activation(M["rhs"][0:RB, :, 0:64],
                                   psum[0:RB, 6, 0:256].rearrange("p (h k) -> p h k", k=64),
                                   ACT.Copy).then_inc(S["rw_scalar"], 1)
                    act.activation(M["b_tok"][0:RB], psum[0:RB, 6, 256:512], ACT.Copy) \
                        .then_inc(S["rw_scalar"], 1)
                    act.wait_ge(*rw_pe.at("tkv", it))
                    act.activation(M["kv_tok"][0:RB].rearrange("p a b -> p (a b)"),
                                   psum[0:RB, 7, 0:512], ACT.Copy).then_inc(S["rw_scalar"], 1)
                    act.wait_ge(*rw_pe.at("l2t", it))
                    act.activation(M["l2t"][0:RB], four(5), ACT.Copy).then_inc(S["rw_scalar"], 1)
                    v = uc + 4 + 12 * q + 4 * tt
                    hi(v, 0)
                    act.wait_ge(*rw_pe.at("akv", it))
                    act.activation(M["rhs"][0:RB, :, 64:P],
                                   psum[0:RB, 6, 0:256].rearrange("p (h k) -> p h k", k=64),
                                   ACT.Copy).then_inc(S["rw_scalar"], 1)
                    act.wait_ge(*rw_pe.at("l4", it))
                    act.activation(l4[0:RB], four(4), ACT.Copy).then_inc(S["rw_scalar"], 1)
                    act.wait_ge(*rw_pe.at("l8", it))
                    act.activation(l8[0:RB], four(4), ACT.Copy).then_inc(S["rw_scalar"], 1)
                    hi(v + 1, 1)
                    act.wait_ge(*rw_pe.at("y1", it))
                    act.activation(M["y1"][0:RB].rearrange("p h k -> p (h k)"),
                                   psum[0:RB, 4, 0:512], ACT.Copy).then_inc(S["rw_scalar"], 1)
                    hi(v + 2, 2)
                    hi(v + 3, 3)
            act.wait_ge(S["rw_end"], 13)
            act.dma_start(M["g_up"][:], g_up_2.rearrange("(a p) n -> p a n", p=P)) \
                .then_inc(S["gup_landed"], 16)
            uo = stream.unit0["out2"]
            act.wait_ge(S["cv_done"], 5)
            act.wait_ge(S["unit_used"], uo)
            act.activation(act_hi[:, 0:8], y_conv, ACT.Copy).then_inc(S["mix_hi"], 1)
            t8 = M["t8"]
            hi_group(uo + 4)
            act.wait_ge(S["gn_centred"], 8)
            act.activation(t8[:], rk_a[:], ACT.Square).then_inc(S["gn_sq"], 1)
            hi(uo + 8, 0)
            hi(uo + 9, 1)
            act.wait_ge(S["gn_inv"], 1)
            act.activation(t8[:], t8[:], ACT.Sqrt).then_inc(S["gn_root"], 1)
            hi(uo + 10, 2)
            hi(uo + 11, 3)
            hi_group(uo + 12)
            act.wait_ge(S["gn_done"], 8)
            act.activation(act_hi[:, 8:16], rk_a[:, :, PAD:RT], ACT.Copy).then_inc(S["mix_hi"], 1)
            go = stream.group0["out2"]
            hi_group(uo + 16)
            for d in range(8):
                for k in range(2):
                    hi(uo + 20 + 2 * d + k, (2 * d + k) % 4)
                if d % 2:
                    act.wait_ge(S["evicted"], go + 9 + d)
                    square("n3", M["mixed"], M["squares2"], d // 2, TC3)
            rstd_root("n3", T3)
            act.wait_ge(*norm_at("n3", "add", 5))
            for d in range(8):
                act.wait_ge(S["post"], 2 * d + 2)
                norm_tiles("n4", c_preffn, M["squares2"], d, TC3)
            rstd_root("n4", T3)

            def last_squares(d):
                if d % 2:
                    square("n5", M["mixed"], M["squares2"], d // 2, TC1)

            ffn("ffn2", LEAD, c_gconv, None, False, last_squares)
            rstd_root("n5", T1)

        @block.vector
        def _(dve):
            def lo(u, slot):
                dve.wait_ge(S["hi_done"], u + 1)
                dve.tensor_tensor(w_lo[:, slot], raw[:, slot], w_hi[:, slot].bitcast(F32),
                                  ALU.subtract).then_inc(S["lo_done"], 1)

            def lo_group(u):
                for j in range(4):
                    lo(u + j, j)

            def bank_pair(pair, T, rows_=P):
                return psum[0:rows_, 2 * pair:2 * pair + 2, 0:T]

            def leave(u_end, pair, dst, T, rows_=P, how="scaled", single=False):
                dve.wait_ge(S["unit_used"], u_end)
                src = bank_pair(pair, T, rows_)
                if single:
                    src = psum[0:rows_, 2 * pair, 0:T]
                if how == "scaled":
                    r = rstd[0:rows_, 0:T] if single else over(rstd[0:rows_, 0:T], 1, 2)
                    ins = dve.tensor_tensor(dst, src, r, ALU.mult)
                elif how == "added":
                    ins = dve.tensor_tensor(dst, src, dst, ALU.add)
                else:
                    ins = dve.tensor_copy(dst, src)
                ins.then_inc(S["evicted"], 1)

            def rstd_of(name, T, width, eps):
                dve.wait_ge(*norm_at(name, "ss", 1))
                dve.tensor_scalar(rstd[:, 0:T], psum[:, 7, 0:T], 1.0 / width, eps, ALU.mult,
                                  ALU.add).then_inc(S["norm_ms"], 1)
                dve.wait_ge(*norm_at(name, "ms", 1))
                dve.reciprocal(rstd[:, 0:T], rstd[:, 0:T]).then_inc(S["norm_inv"], 1)
                dve.wait_ge(*norm_at(name, "rstd", 1))

            def norm_lo(name, c, tc, tiles=range(KD)):
                for k in tiles:
                    dve.wait_ge(*norm_at(name, "hi", k + 1))
                    dve.scalar_tensor_tensor(
                        out=act_lo[:, k, tc], in0=resid[:, k, tc], scalar=col(c + k),
                        in1=act_hi[:, k, tc].bitcast(F32), op0=ALU.mult, op1=ALU.subtract,
                    ).then_inc(S["norm_lo"], 1)

            def norm_pair(name, c, tc, d):
                if d >= 0:
                    norm_lo(name, c, tc, (2 * d, 2 * d + 1))

            links = [0]

            def link(ins):
                links[0] += 1
                ins.then_inc(S["dve_links"], 1)
                dve.wait_ge(S["dve_links"], links[0])

            dve.memset(M["packs"][:], 0.0).then_inc(S["packs_cleared"], 1)
            dve.wait_ge(S["packs_cleared"], 1)
            dve.wait_ge(S["d_landed"], 16)
            assert c_dskip == 0
            dve.tensor_copy(M["packs"][0:8, 0].rearrange("p (b e) -> p b e", b=2),
                            over(head_par[0:8, 4:6], 2, 64)).then_inc(S["d_placed"], 1)
            for n in range(8):
                tt, g = divmod(n, 4)
                dve.wait_ge(S["x_turned"], n + 1)
                dve.tensor_copy(resid[:, 4 * g:4 * g + 4, T0 + P * tt:T0 + P * tt + P],
                                psum[:, 4 + n % 4].rearrange("p (k t) -> p k t", t=P)) \
                    .then_inc(S["x_placed"], 1)
            dve.wait_ge(S["x_turned"], 9)
            dve.tensor_copy(resid[:, :, 0:T0],
                            psum[:, 4, 0:KD * T0].rearrange("p (k t) -> p k t", t=T0)) \
                .then_inc(S["x_placed"], 1)
            for n in range(2):
                w = min(512, NPACK * P - 512 * n)
                dve.wait_ge(S["par_turned"], n + 1)
                dve.tensor_copy(par[:, 512 * n:512 * n + w], psum[:, 5 + n, 0:w]) \
                    .then_inc(S["par_placed"], 1)
            lo_group(stream.unit0["in1"])
            dve.wait_ge(S["par_placed"], 2)
            norm_lo("n0", c_norm1, TC1)
            rstd_of("n0", T1, D, EPS)
            u, g0 = stream.unit0["in1"], stream.group0["in1"]
            lo_group(u + 4)
            leave(u + 4, 0, proj[:, 0:2], T1)
            lo_group(u + 8)
            leave(u + 8, 1, proj[:, 2:4], T1)
            lo_group(u + 12)
            leave(u + 12, 0, proj[:, 4:6], T1)
            with dve.Fori(2, G_IN1 // 2) as i:
                for b in range(2):
                    g = 2 * i + b
                    lo_group(u + 4 * g)
                    leave(u + 4 * g, (b + 1) % 2, proj[:, bass.ds(2 * g - 2, 2)], T1)
            lo_group(u + 4 * G_IN1)
            leave(u + 4 * G_IN1, (G_IN1 - 1) % 2, proj[:, 2 * G_IN1 - 2:2 * G_IN1], T1)
            lo_group(stream.unit0["out1"])
            leave(u + 4 * G_IN1 + 4, G_IN1 % 2, proj[0:16, 44], T1, 16, single=True)
            for n in range(4):
                pair = 4 + 2 * (n % 2)
                hr = M["head_r"]
                if n:
                    dve.wait_ge(S["qk_done"], n)
                dve.wait_ge(S["qk_ss"], n + 1)
                link(dve.tensor_scalar(
                    hr[:].rearrange("p (a b) t -> p a (b t)", a=2), psum[:, pair:pair + 2],
                    1.0 / 128, EPS, ALU.mult, ALU.add))
                dve.reciprocal(hr[:], hr[:]).then_inc(S["qk_inv"], 1)
                dve.wait_ge(S["qk_rstd"], n + 1)
                q4 = proj[:, 4 * n:4 * n + 4]
                dve.scalar_tensor_tensor(out=q4, in0=q4, scalar=col(c_qn if n < 2 else c_kn),
                                         in1=hr[:], op0=ALU.mult, op1=ALU.mult) \
                    .then_inc(S["qk_done"], 1)
            dve.wait_ge(S["made"], MADE_CAUSAL)
            dve.sem_inc(S["at_done"], 2)
            scale = 128.0 ** -0.5
            with dve.Fori(0, 4) as i:
                for b in range(2):
                    sc, sf = M["scores"][:, b], M["soft"][:, b]
                    dve.wait_ge(S["at_scored"], 2 * i + b + 3)
                    dve.wait_ge(S["at_p_turned"], 2 * i + b + 1)
                    dve.tensor_tensor(sc, psum[:, 4 + b, 0:384], M["causal"][:], ALU.add) \
                        .then_inc(S["at_masked"], 1)
                    dve.wait_ge(S["at_masked"], 2 * i + b + 1)
                    dve.tensor_reduce(sf[:, 0:1], sc[:, 0:P], AX_X, ALU.max) \
                        .then_inc(S["at_max"], 1)
                    dve.tensor_reduce(sf[:, 1:2], sc[:, P:384], AX_X, ALU.max) \
                        .then_inc(S["at_max"], 1)
                    dve.wait_ge(S["at_max"], 4 * i + 2 * b + 2)
                    dve.tensor_scalar(sf[:, 2:4], sf[:, 0:2], -scale, None, ALU.mult) \
                        .then_inc(S["at_shift"], 1)
                for b in range(2):
                    sc, sf = M["scores"][:, b], M["soft"][:, b]
                    dve.wait_ge(S["at_exp"], 4 * i + 2 * b + 2)
                    dve.reciprocal(sf[:, 6:8], sf[:, 4:6]).then_inc(S["at_sum"], 1)
                    dve.wait_ge(S["at_sum"], 2 * i + b + 1)
                    for k, (at, wide) in enumerate(((0, P), (P, 256))):
                        dve.tensor_scalar(sc[:, at:at + wide], sc[:, at:at + wide],
                                          sf[:, 6 + k:7 + k], None, ALU.mult) \
                            .then_inc(S["at_probs"], 1)
                for b in range(2):
                    dve.wait_ge(S["at_out"], 2 * i + b + 3)
                    dve.tensor_copy(proj[:, bass.ds(2 * i + b, 1)][:, 0], psum[:, 4 + b, 0:256]) \
                        .then_inc(S["at_done"], 1)
            dve.wait_ge(S["at_done"], 10)
            dve.sem_inc(S["attention_over"], 1)
            with dve.Fori(0, 6) as i:
                for b in range(2):
                    dve.wait_ge(S["sc_first"], 2 * i + b + 1)
                    for k in range(1, 4):
                        if k > 1:
                            dve.wait_ge(S["sc_taps"], 6 * i + 3 * b + k - 1)
                        cv = M["conv_out"][:, b, k:T1]
                        dve.scalar_tensor_tensor(
                            out=cv, in0=proj[:, bass.ds(2 * i + b + 32, 1)][:, 0, 0:T1 - k],
                            scalar=par[:, bass.ds(2 * i + b + (c_sconv + 12 * (3 - k)), 1)],
                            in1=cv, op0=ALU.mult, op1=ALU.add).then_inc(S["sc_taps"], 1)
            step, srows = M["step"], M["step_rows"]
            s_ = [step[0:16, k] for k in range(7)]
            dve.wait_ge(S["heads_landed"], 32)
            dve.tensor_scalar(s_[0], proj[0:16, 44], head_par[0:16, 0:1], None, ALU.add) \
                .then_inc(S["dt_abs"], 1)
            dve.wait_ge(S["dt_abs"], 1)
            dve.scalar_tensor_tensor(out=s_[1], in0=s_[0], scalar=-1.0, in1=s_[0], op0=ALU.mult,
                                     op1=ALU.max).then_inc(S["dt_abs"], 1)
            dve.wait_ge(S["dt_ln"], 1)
            link(dve.scalar_tensor_tensor(out=s_[3], in0=s_[0], scalar=0.0, in1=s_[2],
                                          op0=ALU.max, op1=ALU.add))
            dve.wait_ge(S["dt_exp"], 2)
            link(dve.tensor_scalar(s_[4], s_[3], head_par[0:16, 2:3], -1.0, ALU.mult, ALU.mult))
            for c in range(2):
                cs = slice(c * CH, c * CH + CH)
                dve.tensor_tensor_scan(s_[5][:, cs], ones[0:16, 0:CH], s_[4][:, cs], 0.0,
                                       ALU.mult, ALU.add).then_inc(S["dt_cum"], 1)
            dve.wait_ge(S["dt_end"], 1)
            dve.tensor_tensor(s_[6][:, 0:P], s_[6][:, 0:P], s_[3][:, 0:P], ALU.mult) \
                .then_inc(S["ssd_vector"], 1)
            dve.wait_ge(*ssd_pe.at("dt_turned"))
            dve.tensor_copy(srows[:], psum[:, 4, 0:80].rearrange("p (k h) -> p k h", h=16)) \
                .then_inc(S["ssd_vector"], 1)
            dve.wait_ge(*ssd_pe.at("cb_made"))
            dve.wait_ge(S["made"], MADE_UPTO)
            dve.tensor_tensor(M["cb"][:], psum[:, 5].rearrange("p (k l) -> p k l", l=P),
                              over(M["upto"][:], 1, 4), ALU.mult).then_inc(S["ssd_vector"], 1)
            dve.wait_ge(*ssd_pe.at("b_turned"))
            dve.tensor_copy(M["b_rows"][:], psum[:, 6, 0:256].rearrange("p (k l) -> p k l", l=P)) \
                .then_inc(S["ssd_vector"], 1)
            dve.wait_ge(*ssd_dve.at("dt_rows"))
            for n in range(4):
                c, half = divmod(n, 2)
                dve.wait_ge(S["xs_turned"], n + 1)
                bank = (7, 4, 5, 6)[n]
                xt = psum[:, bank].rearrange("p (h k) -> p h k", k=64)
                hs = slice(8 * half, 8 * half + 8)
                dst = M["xdt"][:, c, 512 * half:512 * half + 512]
                dve.tensor_tensor(dst.rearrange("p (h k) -> p h k", k=64), xt,
                                  over(srows[:, 2 + c, hs], 2, 64), ALU.mult) \
                    .then_inc(S["xdt_made"], 1)
                if c == 0:
                    dst = M["xdte"][:, 512 * half:512 * half + 512]
                    dve.tensor_tensor(dst.rearrange("p (h k) -> p h k", k=64), xt,
                                      over(srows[:, 4, hs], 2, 64), ALU.mult) \
                        .then_inc(S["xdt_made"], 1)
            for g in range(2):
                dve.wait_ge(S["st_made"], g + 1)
                dve.tensor_copy(M["state0"][:, g], psum[:, 7 - 3 * g]).then_inc(S["st_placed"], 1)

            def gate(hb):
                dve.wait_ge(S["sg_used"], 2 * hb + 2)
                if hb == 0:
                    dve.wait_ge(S["z_silu"], 1)
                for p in range(2):
                    j = 2 * hb + p
                    link(dve.scalar_tensor_tensor(
                        out=proj[:, 32 + j], in0=proj[:, 32 + j], scalar=col(c_dskip + j),
                        in1=psum[:, 6 + hb % 2, 256 * p:256 * p + 256], op0=ALU.mult, op1=ALU.add))
                dve.tensor_tensor(proj[:, 32 + 2 * hb:34 + 2 * hb], proj[:, 32 + 2 * hb:34 + 2 * hb],
                                  proj[:, 24 + 2 * hb:26 + 2 * hb], ALU.mult) \
                    .then_inc(S["y_gated"], 1)

            for n in range(8):
                hb, c = divmod(n, 2)
                h4 = slice(4 * hb, 4 * hb + 4)
                cs = slice(c * CH, c * CH + CH)
                if n >= 2:
                    dve.wait_ge(S["sg_row"], n - 1)
                dg = M["diag"][0:16, n % 2].rearrange("p (h l) -> p h l", l=CH)
                dve.tensor_tensor(dg, over(s_[5][:, cs], 1, 4), over(ident[0:16, h4], 2, CH),
                                  ALU.mult).then_inc(S["sg_diag"], 1)
                seg = M["seg"][:, n % 2]
                seg3 = seg.rearrange("p (h l) -> p h l", l=CH)
                dve.wait_ge(S["sg_row"], n + 1)
                dve.tensor_tensor(seg3, psum[:, 4 + n % 2].rearrange("p (h l) -> p h l", l=CH),
                                  over(srows[:, c, h4], 2, CH), ALU.subtract) \
                    .then_inc(S["sg_seg"], 1)
                dve.wait_ge(S["sg_seg"], 2 * n + 1)
                dve.tensor_scalar(seg, seg, 0.0, None, ALU.min).then_inc(S["sg_seg"], 1)
                if n >= 2:
                    dve.wait_ge(S["sg_used"], n - 1)
                if c:
                    dve.wait_ge(S["sg_e1"], (n + 1) // 2)
                    e3 = M["cte"][:, 0].rearrange("p (h l) -> p h l", l=CH)
                    c3 = M["cte"][:, 1].rearrange("p (h l) -> p h l", l=CH)
                    dve.tensor_tensor(c3, e3, over(proj[:, 42 + hb // 2, cs], 1, 4), ALU.mult) \
                        .then_inc(S["sg_cte"], 1)
                dve.wait_ge(S["sg_exp"], n + 1)
                dve.tensor_tensor(M["gmat"][:, n % 2].rearrange("p (h l) -> p h l", l=CH), seg3,
                                  over(M["cb"][:, 2 * (hb // 2) + c], 1, 4), ALU.mult) \
                    .then_inc(S["sg_g"], 1)
                if n in (3, 5, 7):
                    gate((n - 3) // 2)
            gate(3)
            for g in range(2):
                dve.wait_ge(S["yn_ss"], g + 1)
                link(dve.tensor_scalar(M["y_r"][:, g], psum[:, 4 + g, 0:T1], 1.0 / 512, EPS,
                                       ALU.mult, ALU.add))
                dve.reciprocal(M["y_r"][:, g], M["y_r"][:, g]).then_inc(S["yn_inv"], 1)
            for j in range(8):
                dve.wait_ge(S["yn_rstd"], j // 4 + 1)
                dve.scalar_tensor_tensor(out=proj[:, 32 + j], in0=proj[:, 32 + j],
                                         scalar=col(c_snorm + j), in1=M["y_r"][:, j // 4],
                                         op0=ALU.mult, op1=ALU.mult).then_inc(S["yn_done"], 1)
            dve.wait_ge(S["mix_hi"], 1)
            dve.tensor_tensor(act_lo[:, 0:8, TC1], proj[:, 0:8], act_hi[:, 0:8, TC1].bitcast(F32),
                              ALU.subtract).then_inc(S["mix_lo"], 1)
            dve.wait_ge(S["mix_hi"], 2)
            dve.tensor_tensor(act_lo[:, 8:16, TC1], proj[:, 32:40],
                              act_hi[:, 8:16, TC1].bitcast(F32), ALU.subtract) \
                .then_inc(S["mix_lo"], 1)
            u, g0 = stream.unit0["out1"], stream.group0["out1"]

            def out1_half(u, b, tiles, next_units):
                leave(u, (g0 + b) % 2, resid[:, tiles, TC1], T1, how="added")
                for k in range(2):
                    lo(next_units + k, 2 * b + k)

            with dve.Fori(0, 4) as i:
                for b in range(2):
                    out1_half(u + 4 * i + 2 * b + 2, b, bass.ds(4 * i + 2 * b, 2),
                              u + 4 * i + 2 * b + 4)
            for d in range(8):
                out1_half(u + 18 + 2 * d, d % 2, slice(2 * d, 2 * d + 2), u + 20 + 2 * d)
                if 1 <= d <= 4:
                    norm_pair("n1", c_norm2, TC1, d - 1)
            for d in range(4, 8):
                norm_pair("n1", c_norm2, TC1, d)

            def ffn(name, lead, cc, vals, acc, last_step):
                u, g0, n0 = stream.unit0[name], stream.group0[name], chunks_before[name]
                pair0 = g0 % 2
                nt = 8 if vals else 4
                T = T1 + lead
                up, conv, ff = M["up"], M["conv"], M["ff"]

                def taps(i, t0):
                    for t in range(t0, t0 + 4):
                        dve.wait_ge(S["ff_first"], nt * i + (8 * n0 + t + 1))
                        c = (44 if t >= 4 else 0) + t % 4
                        for k in (1, 2):
                            if k == 2:
                                dve.wait_ge(S["ff_taps"], 2 * nt * i + (16 * n0 + 2 * t + 1))
                            n = max(k - lead, 0)
                            cv = conv[:, t, n:T1]
                            dve.scalar_tensor_tensor(
                                out=cv, in0=up[:, t, lead - k + n:lead - k + T1],
                                scalar=par[:, bass.ds(4 * i + (c + cc[2 - k]), 1)],
                                in1=cv, op0=ALU.mult, op1=ALU.add) \
                                .then_inc(S["ff_taps"], 1)

                def product(i):
                    dve.wait_ge(S["ff_silu"], i + (n0 + 1))
                    dve.wait_ge(S["ff_taps"], 2 * nt * i + (16 * n0 + 2 * nt))
                    v = conv[:, 4:8] if vals else up[:, 4:8, lead:T]
                    dve.tensor_tensor(ff[:], conv[:, 0:4], v, ALU.mult) \
                        .then_inc(S["ff_ff"], 1)

                def product_lo(i, hi_, lo_):
                    dve.wait_ge(S["ff_ffhi"], i + (n0 + 1))
                    dve.tensor_tensor(lo_[:], ff[:], hi_[:].bitcast(F32), ALU.subtract) \
                        .then_inc(S["ff_fflo"], 1)

                def leave_up(v, j):
                    leave(v + 4 * j + 4, (pair0 + j) % 2, up[:, 2 * j:2 * j + 2, 0:T], T)

                def leave_down(v, d):
                    leave(v + d + 1, (pair0 + d) % 2, acc[:, 2 * d:2 * d + 2, TC1], T1,
                          how="added")

                def while_up(i, v):
                    taps(i - 1, 0)
                    lo_group(v + 4)
                    if vals:
                        taps(i - 1, 4)
                    leave_up(v, 0)
                    lo_group(v + 8)
                    product(i - 1)
                    leave_up(v, 1)
                    lo_group(v + 12)
                    product_lo(i - 1, M["ff_hi"], M["ff_lo"])
                    leave_up(v, 2)
                    lo_group(v + 16)
                    leave_up(v, 3)

                for j in range(1, 4):
                    lo_group(u + 4 * j)
                    leave_up(u, j - 1)
                lo_group(u + 16)
                leave_up(u, 3)
                with dve.Fori(1, FCH - 1) as i:
                    v = u + 24 * i - 8
                    while_up(i, v)
                    for d in range(8):
                        leave_down(v + 16, d)
                        lo(v + 20 + d, d % 4)
                i = FCH - 1
                w = u + 24 * i + 8
                while_up(i, w - 16)
                for d in range(8):
                    leave_down(w, d)
                    lo(w + 4 + d, d % 4)
                    if d == 0:
                        taps(i, 0)
                    elif d == 1 and vals:
                        taps(i, 4)
                    elif d == 3:
                        product(i)
                    elif d == 4:
                        product_lo(i, M["last_hi"], M["last_lo"])
                for d in range(8):
                    leave_down(w + 8, d)
                    if d < 4 or w + 12 + d < stream.units:
                        lo(w + 12 + d, d % 4)
                    last_step(d)

            rstd_of("n1", T1, D, EPS)
            ffn("ffn1", 0, c_fconv, True, resid,
                lambda d: norm_pair("n2", c_premix, TC2, d - 1))
            norm_pair("n2", c_premix, TC2, 7)
            rstd_of("n2", T2, D, EPS)
            u, g0 = stream.unit0["in2"], stream.group0["in2"]
            z2, low = M["z2"], M["low"]
            rk_a, rk_b, bonus = M["rk_a"], M["rk_b"], M["bonus"]
            t5, t6, t7 = M["t5"], M["t6"], M["t7"]
            link(dve.memset(z2[:, :, 0:PAD], 0.0))
            link(dve.memset(low[:, :, 0:PAD], 0.0))
            lo_group(u + 4)
            leave(u + 4, g0 % 2, low[0:96, 0:2, PAD:RT], T2, 96)
            lo_group(u + 8)
            leave(u + 8, (g0 + 1) % 2, low[:, 2:4, PAD:RT], T2)
            lo_group(u + 12)
            leave(u + 12, g0 % 2, z2[:, 0:2, PAD:RT], T2)
            lo_group(u + 16)
            leave(u + 16, (g0 + 1) % 2, z2[:, 2:4, PAD:RT], T2)
            lo_group(u + 20)
            leave(u + 20, g0 % 2, z2[:, 4:6, PAD:RT], T2)
            with dve.Fori(0, (IN2_RKV - 4) // 2) as i:
                for b in range(2):
                    n = 2 * i + (b + 3)
                    lo_group(u + 12 + 4 * n)
                    leave(u + 12 + 4 * n, (g0 + b + 1) % 2, z2[:, bass.ds(2 * n, 2), PAD:RT], T2)
            lo_group(u + 8 + 4 * IN2_RKV)
            leave(u + 8 + 4 * IN2_RKV, (g0 + 1) % 2, z2[:, 22:24, PAD:RT], T2)
            for t in (t5, rk_a, rk_b, bonus):
                link(dve.memset(t[:, :, 0:PAD], 0.0))

            def shift(t, n, cols_, low_before=None, rows_=P):
                cur, before = t[0:rows_, :, PAD:RT], t[0:rows_, :, PAD - 1:RT - 1]
                link(dve.tensor_tensor(t7[0:rows_, 0:n, 0:T2], before, cur, ALU.subtract))
                for j in range(n):
                    ins = dve.scalar_tensor_tensor(
                        out=t[0:rows_, j, PAD:RT], in0=t7[0:rows_, j, 0:T2],
                        scalar=par[0:rows_, cols_ + j:cols_ + j + 1], in1=t[0:rows_, j, PAD:RT],
                        op0=ALU.mult, op1=ALU.add)
                    if low_before is None:
                        link(ins)
                    else:
                        ins.then_inc(S["low_shifted"], 1)
                        dve.wait_ge(S["low_shifted"], low_before + j + 1)

            shift(low[:, 0:2], 2, c_mulow, 0, 96)
            shift(low[:, 2:4], 2, c_mug, 2)
            shift(z2[:, 8:16], 8, c_mu + 8)
            shift(z2[:, 0:8], 8, c_mu)
            shift(z2[:, 16:24], 8, c_mu + 16)
            for j in range(8):
                dve.tensor_scalar(rk_a[:, j], z2[:, 8 + j], col(c_kk + j), None, ALU.mult) \
                    .then_inc(S["kk_scaled"], 1)
            dve.wait_ge(S["low_out"], 8)
            link(dve.tensor_scalar(t5[:, :, PAD:RT], t5[:, :, PAD:RT], -DECAY, None, ALU.mult))
            dve.wait_ge(S["made"], MADE_SCAN)
            for j in range(8):
                link(dve.tensor_tensor_scan(t6[:, j], M["scan_keep"][:], t5[:, j], 0.0,
                                            ALU.mult, ALU.add))
            for j in range(8):
                dve.wait_ge(S["kk_ss"], j + 1)
                ins = dve.tensor_scalar(t7[:, j], psum[:, 4 + j % 4, 0:RT], 1e-24, None, ALU.max)
                ins.then_inc(S["kk_max"], 1)
            dve.wait_ge(S["kk_max"], 8)
            dve.reciprocal(t7[:], t7[:]).then_inc(S["kk_inv"], 1)
            dve.wait_ge(S["kk_root"], 1)
            link(dve.tensor_tensor(rk_a[:], rk_a[:], t7[:], ALU.mult))
            dve.wait_ge(S["low_out"], 16)
            for j in range(8):
                link(dve.tensor_scalar(t7[:, j], rk_b[:, j], -1.0, col(c_ka + j), ALU.add,
                                       ALU.mult))
            kz = z2[:, 8:16].rearrange("p a b -> p (a b)")
            f7 = t7[:].rearrange("p a b -> p (a b)")
            link(dve.scalar_tensor_tensor(out=kz, in0=f7, scalar=1.0, in1=kz, op0=ALU.add,
                                          op1=ALU.mult))
            link(dve.tensor_tensor(t7[:], z2[:, 0:8], z2[:, 8:16], ALU.mult))
            for j in range(8):
                dve.tensor_scalar(t7[:, j], t7[:, j], col(c_rk + j), None, ALU.mult) \
                    .then_inc(S["bo_scaled"], 1)
            link(dve.tensor_tensor(rk_b[:], rk_b[:], rk_a[:], ALU.mult))
            for j in range(8):
                dve.wait_ge(S["bo_sum"], j + 1)
                dve.tensor_tensor(bonus[:, j, PAD:RT], psum[:, 4 + j % 4, 0:T2],
                                  z2[:, 16 + j, PAD:RT], ALU.mult).then_inc(S["bo_made"], 1)
            dve.tensor_tensor(t5[:], t6[:], t5[:], ALU.subtract).then_inc(S["decay_prev"], 1)
            fa, f5 = (t[:].rearrange("p a b -> p (a b)") for t in (rk_a, t5))
            dve.wait_ge(S["decay_exp"], 1)
            dve.scalar_tensor_tensor(out=fa, in0=fa, scalar=-1.0, in1=f5, op0=ALU.mult,
                                     op1=ALU.mult).then_inc(S["a_made"], 1)
            dve.wait_ge(S["decay_exp"], 2)
            dve.tensor_tensor(rk_b[:], rk_b[:], t5[:], ALU.mult).then_inc(S["bk_made"], 1)
            dve.tensor_tensor(z2[:, 8:16], z2[:, 8:16], t5[:], ALU.mult) \
                .then_inc(S["bk_made"], 1)
            dve.wait_ge(S["decay_exp"], 3)
            link(dve.tensor_copy(M["wc"][:], t5[:].rearrange("p a (c t) -> p a c t", t=RC)
                                 [:, :, :, RC - 1]))
            dve.tensor_tensor(z2[:, 0:8], z2[:, 0:8], t5[:], ALU.mult) \
                .then_inc(S["rpre_over"], 1)
            fs, mt, st, ru = M["fs"], M["mt"], M["state"], M["ru"]
            dve.wait_ge(S["rpre_over"], 1)
            link(dve.memset(mt[:], 0.0))
            dve.wait_ge(S["made"], MADE_RWKV)

            def heads4(name):
                return M[name][0:RB].rearrange("s (p e) t -> s e p t", e=2)

            def mask4(name):
                m = M[name][0:RB]
                return over(over(m, 1, 2), 1, 2)

            def one_mask(name):
                return over(M[name][0:RB], 1, 2)

            def masked(dst, banks, at, wide, mask):
                src = psum[0:RB, banks:banks + 2, 0:2 * wide] \
                    .rearrange("s e (p w) -> s e p w", p=2)[:, :, :, at:at + RB]
                dve.tensor_tensor(heads4(dst), src, mask4(mask), ALU.mult) \
                    .then_inc(S["rw_vector"], 1)

            dve.sem_inc(S["rw_end"], 1)
            dve.sem_inc(S["rw_vector"], rw_dve.start)
            uc = u + 8 + 4 * IN2_RKV
            gate_b, gate_c = M["gate_b"], M["gate_c"]
            gc = g0 + 2 + IN2_RKV

            def conv_tail(v, q):
                dve.wait_ge(S["unit_used"], v)
                dve.wait_ge(S["cv_step"], 7 * q + 1)
                dve.tensor_tensor(gate_c[:], bank_pair(0, T2), gate_c[:], ALU.mult) \
                    .then_inc(S["evicted"], 1)
                dve.wait_ge(S["evicted"], 3 * q + (gc + 3))
                y = y_conv[:, bass.ds(2 * q, 2)]
                for k in range(3):
                    for p in range(2):
                        c = par[:, bass.ds(2 * q + (p + c_conv2 + 8 * (2 - k)), 1)]
                        yp = y_conv[:, bass.ds(2 * q + p, 1)][:, 0]
                        if k == 0:
                            dve.tensor_scalar(yp, gate_c[:, p], c, None, ALU.mult) \
                                .then_inc(S["cv_step"], 1)
                            continue
                        dve.wait_ge(S["cv_step"], 7 * q + 2 * k + p)
                        dve.scalar_tensor_tensor(out=yp[:, k:T2], in0=gate_c[:, p, 0:T2 - k],
                                                 scalar=c, in1=yp[:, k:T2], op0=ALU.mult,
                                                 op1=ALU.add).then_inc(S["cv_step"], 1)
                dve.wait_ge(S["cv_step"], 7 * q + 7)
                dve.tensor_tensor(y, y, gate_b[:], ALU.mult).then_inc(S["cv_done"], 1)

            dve.sem_inc(S["cv_done"], 1)
            with dve.Fori(0, 4) as q:
                dve.wait_ge(S["rw_end"], 3 * q + 1)
                dve.memset(st[:], 0.0).then_inc(S["rw_s"], 1)
                for tt in range(3):
                    it = 3 * q + tt
                    dve.wait_ge(*rw_pe.at("lt", it))
                    masked("ldt", 4, 0, 192, "m_ldt")
                    masked("lot", 4, 0, 192, "m_lot")
                    masked("rbt", 4, RB, 192, "m_r")
                    dve.wait_ge(*rw_pe.at("ak", it))
                    masked("akt", 6, 0, 192, "m_a")
                    masked("rkt", 6, RB, 192, "m_r")
                    dve.wait_ge(*rw_dve.at("ldt", it))
                    dve.tensor_tensor(M["p1"][0:RB], M["ldt"][0:RB], over(ident[0:RB, 0:RB], 1, 4),
                                      ALU.add).then_inc(S["rw_vector"], 1)
                    dve.wait_ge(*rw_pe.at("l", it))
                    masked("ld", 4, 0, RB, "m_ld")
                    dve.wait_ge(*rw_pe.at("l2", it))
                    dve.tensor_copy(M["l2"][0:RB], four(4)).then_inc(S["rw_vector"], 1)
                    dve.wait_ge(*rw_pe.at("l4t", it))
                    dve.tensor_copy(l4t[0:RB], four(5)).then_inc(S["rw_vector"], 1)
                    v = uc + 4 + 12 * q + 4 * tt
                    lo(v, 0)
                    dve.wait_ge(*rw_pe.at("p2m", it))
                    dve.tensor_tensor(p2[0:RB], four(7), M["p1"][0:RB], ALU.add) \
                        .then_inc(S["rw_vector"], 1)
                    dve.wait_ge(*rw_pe.at("p3m", it))
                    dve.wait_ge(*rw_dve.at("p2", it))
                    dve.tensor_tensor(p3[0:RB], four(6), p2[0:RB], ALU.add) \
                        .then_inc(S["rw_vector"], 1)
                    dve.wait_ge(*rw_pe.at("p4m", it))
                    dve.wait_ge(*rw_dve.at("p3", it))
                    dve.tensor_tensor(p4[0:RB], four(7), p3[0:RB], ALU.add) \
                        .then_inc(S["rw_vector"], 1)
                    lo(v + 1, 1)
                    dve.wait_ge(*rw_pe.at("zm", it))
                    dve.tensor_copy(zz[0:RB].rearrange("p h k -> p (h k)"),
                                    psum[0:RB, 5, 0:512]).then_inc(S["rw_vector"], 1)
                    dve.wait_ge(*rw_pe.at("xm", it))
                    dve.tensor_tensor(M["uu"][0:RB].rearrange("p a h k -> p h a k"),
                                      psum[0:RB, 6, 0:512].rearrange("p (h a k) -> p h a k", h=4,
                                                                     a=2),
                                      M["y1"][0:RB].rearrange("p h (a k) -> p h a k", a=2),
                                      ALU.add) \
                        .then_inc(S["rw_vector"], 1)
                    dve.wait_ge(*rw_pe.at("rum", it))
                    dve.tensor_tensor(ru[:], psum[:, 7, 0:192].rearrange("p (a t) -> p a t", a=2),
                                      fs[:, :, 1], ALU.add).then_inc(S["rw_vector"], 1)
                    dve.wait_ge(*rw_pe.at("mtm", it))
                    for e in range(2):
                        h = slice(64 * e, 64 * e + 64)
                        src = psum[h, 4:7, 0:256].rearrange("p c (a k) -> p c a k", a=2)[:, :, :, h]
                        dve.tensor_tensor(mt[h, :, :, h], src,
                                          over(over(ident[h, h], 1, 2), 1, 3), ALU.add) \
                            .then_inc(S["rw_vector"], 1)
                    for c in range(3):
                        dve.wait_ge(*rw_pe.at(f"step{c}", it))
                        for e in range(2):
                            h = slice(64 * e, 64 * e + 64)
                            src = psum[h, 4 + c, 0:256].rearrange("p (a k) -> p a k", a=2)[:, :, h]
                            w = M["wc"][h, bass.ds(2 * q, 2), 3 * tt + c:3 * tt + c + 1]
                            dve.tensor_tensor(st[h, :, h], src, w.to_broadcast([64, 2, 64]),
                                              ALU.mult).then_inc(S["rw_s"], 1)
                    dve.tensor_copy(rk_a[:, bass.ds(2 * q, 2), RB * tt:RB * tt + RB],
                                    psum[:, 7, 256:448].rearrange("p (a t) -> p a t", a=2)) \
                        .then_inc(S["rw_end"], 1)
                    lo(v + 2, 2)
                    lo(v + 3, 3)
                    if tt == 0:
                        dve.wait_ge(S["cv_done"], q + 1)
                        leave(v, 0, gate_b[:], T2)
                    elif tt == 1:
                        leave(v, 0, gate_c[:], T2)
                        dve.wait_ge(S["evicted"], gc + 3 * q + 2)
                        dve.tensor_tensor(gate_c[:], gate_c[:], over(rstd[:], 1, 2), ALU.mult) \
                            .then_inc(S["cv_step"], 1)
                    else:
                        conv_tail(v, q)
            t8, mixed = M["t8"], M["mixed"]
            u, g0 = stream.unit0["out2"], stream.group0["out2"]
            dve.wait_ge(S["mix_hi"], 3)
            dve.tensor_tensor(act_lo[:, 0:8], y_conv, act_hi[:, 0:8].bitcast(F32),
                              ALU.subtract).then_inc(S["mix_lo"], 1)
            dve.wait_ge(S["rw_end"], 13)
            for j in range(8):
                dve.wait_ge(S["gn_mean"], j + 1)
                ya = rk_a[:, j, PAD:RT]
                dve.scalar_tensor_tensor(out=ya, in0=psum[:, 4 + j % 4, 0:T2], scalar=-1.0 / 64,
                                         in1=ya, op0=ALU.mult, op1=ALU.add) \
                    .then_inc(S["gn_centred"], 1)

            def out_half(n, next_units, how):
                leave(u + 2 * n + 2, (g0 + n) % 2, mixed[:, 2 * (n % 8):2 * (n % 8) + 2, TC3],
                      T3, how=how)
                for k in range(2):
                    lo(next_units + k, 2 * (n % 2) + k)

            out_half(0, u + 4, "copied")
            out_half(1, u + 6, "copied")
            for j in range(8):
                dve.wait_ge(S["gn_ss"], j + 1)
                dve.tensor_scalar(t8[:, j], psum[:, 4 + j % 4, 0:RT], 1.0 / 64, GN_EPS, ALU.mult,
                                  ALU.add).then_inc(S["gn_used"], 1)
            dve.wait_ge(S["gn_used"], 8)
            out_half(2, u + 8, "copied")
            dve.reciprocal(t8[:], t8[:]).then_inc(S["gn_inv"], 1)
            out_half(3, u + 10, "copied")
            dve.wait_ge(S["gn_root"], 1)
            link(dve.tensor_tensor(rk_a[:], rk_a[:], t8[:], ALU.mult))
            out_half(4, u + 12, "copied")
            for j in range(8):
                link(dve.tensor_scalar(rk_a[:, j], rk_a[:, j], col(c_lnw + j), col(c_lnb + j),
                                       ALU.mult, ALU.add))
            out_half(5, u + 14, "copied")
            link(dve.tensor_tensor(rk_a[:], rk_a[:], bonus[:], ALU.add))
            for j in range(8):
                dve.wait_ge(S["gate_made"], j + 1)
                dve.tensor_tensor(rk_a[:, j, PAD:RT], rk_a[:, j, PAD:RT],
                                  psum[:, 4 + j % 4, 0:T2], ALU.mult).then_inc(S["gn_done"], 1)
            dve.wait_ge(S["gn_done"], 8)
            dve.wait_ge(S["mix_hi"], 4)
            dve.tensor_tensor(act_lo[:, 8:16], rk_a[:, :, PAD:RT], act_hi[:, 8:16].bitcast(F32),
                              ALU.subtract).then_inc(S["mix_lo"], 1)
            out_half(6, u + 16, "copied")
            out_half(7, u + 18, "copied")
            with dve.Fori(0, 3) as i:
                for b in range(2):
                    leave(u + 4 * i + (18 + 2 * b), (g0 + b) % 2,
                          mixed[:, bass.ds(4 * i + 2 * b, 2), TC3], T3, how="added")
                    for k in range(2):
                        lo(u + 4 * i + (20 + 2 * b + k), 2 * b + k)
            for b in range(2):
                leave(u + 30 + 2 * b, (g0 + b) % 2, mixed[:, 12 + 2 * b:14 + 2 * b, TC3], T3,
                      how="added")
                for k in range(2):
                    lo(stream.unit0["ffn2"] + 2 * b + k, 2 * b + k)

            def post(before, c, tc):
                for k in range(KD):
                    m = mixed[:, k, tc]
                    dve.scalar_tensor_tensor(out=m, in0=m, scalar=col(c + k),
                                             in1=rstd[:, 0:tc.stop - tc.start], op0=ALU.mult,
                                             op1=ALU.mult) \
                        .then_inc(S["post_scaled"], 1)
                    dve.wait_ge(S["post_scaled"], before + k + 1)
                    dve.tensor_tensor(resid[:, k, tc], resid[:, k, tc], m, ALU.add) \
                        .then_inc(S["post"], 1)

            rstd_of("n3", T3, D, EPS)
            dve.wait_ge(S["evicted"], stream.group0["ffn2"])
            post(0, c_postmix, TC3)
            norm_lo("n4", c_preffn, TC3)
            rstd_of("n4", T3, D, EPS)
            link(dve.memset(mixed[:], 0.0))
            ffn("ffn2", LEAD, c_gconv, False, mixed, lambda d: None)
            rstd_of("n5", T1, D, EPS)
            dve.wait_ge(S["evicted"], stream.groups)
            post(KD, c_postffn, TC1)
            for n in range(8):
                tt, g = divmod(n, 4)
                dve.wait_ge(S["out_turned"], n + 1)
                dve.tensor_copy(M["out_rows"][:, tt, 512 * g:512 * g + 512], psum[:, 4 + n % 4]) \
                    .then_inc(S["out_copied"], 1)

        @block.tensor
        def _(pe):
            def unit(u, slot, pair, hi_, lo_, k0, T, first, last, m=P, ncol=2, shift=P):
                pe.wait_ge(S["lo_done"], u + 1)
                for r in range(RK):
                    mm = unit_row(slot, pair, hi_, lo_, k0, T, first, last, r, m, ncol, shift)
                mm.then_inc(S["unit_used"], 1)

            def unit_row(slot, pair, hi_, lo_, k0, T, first, last, r, m=P, ncol=2, shift=P):
                for c in range(ncol):
                    out_ = psum[0:m, 2 * pair + c, 0:T]
                    at = 256 * r + shift * c
                    wh, wl = w_hi[:, slot, at:at + m], w_lo[:, slot, at:at + m]
                    xh, xl = hi_[:, k0 + r], lo_[:, k0 + r]
                    pe.matmul(out_, wh, xh, start=first and r == 0, stop=False)
                    pe.matmul(out_, wh, xl, start=False, stop=False)
                    mm = pe.matmul(out_, wl, xh, start=False, stop=last and r == RK - 1)
                return mm

            def bank_free(g):
                if not isinstance(g, int) or g >= 2:
                    pe.wait_ge(S["evicted"], g - 1)

            def out_units(u, g, tc, T, half, out_pair0):
                for b in range(2):
                    bank_free(g + b)
                    for j in range(2):
                        unit(u + 2 * b + j, 2 * b + j, (out_pair0 + b) % 2, act_hi[:, :, tc],
                             act_lo[:, :, tc], 8 * half + 4 * j, T, j == 0, j == 1)

            def group(u, g, pair, tc, T, ready=None, **how):
                bank_free(g)
                for j in range(4):
                    if ready:
                        pe.wait_ge(*ready(j))
                    unit(u + j, j, pair, act_hi[:, :, tc], act_lo[:, :, tc], 4 * j, T,
                         j == 0, j == 3, **how)

            def sum_over(name, T):
                pe.wait_ge(*norm_at(name, "add", 5))
                pe.matmul(psum[:, 7, 0:T], ones[:], ss_part[:, 0:T], start=True, stop=True) \
                    .then_inc(S["norm_ss"], 1)

            pe.wait_ge(S["made"], MADE_CONSTS)
            pe.wait_ge(S["x_landed"], 48)
            for n in range(8):
                tt, g = divmod(n, 4)
                if n >= 4:
                    pe.wait_ge(S["x_placed"], n - 3)
                for k in range(4):
                    c = P * (4 * g + k)
                    mm = pe.transpose(psum[:, 4 + n % 4, P * k:P * k + P],
                                      M["x_rows"][:, tt, c:c + P], ident[:])
                mm.then_inc(S["x_turned"], 1)
            pe.wait_ge(S["x_placed"], 5)
            for k in range(KD):
                mm = pe.transpose(psum[:, 4, T0 * k:T0 * k + T0],
                                  M["meta_rows"][0:T0, P * k:P * k + P], ident[0:T0, 0:T0])
            mm.then_inc(S["x_turned"], 1)
            pe.wait_ge(S["x_placed"], 7)
            pe.wait_ge(S["params_landed"], 16 * n_param_loads[0])
            pe.wait_ge(S["d_placed"], 1)
            for n in range(NPACK):
                mm = pe.transpose(psum[:, 5 + n // 4, P * (n % 4):P * (n % 4) + P],
                                  M["packs"][:, n], ident[:])
                if n == 3 or n == NPACK - 1:
                    mm.then_inc(S["par_turned"], 1)
            u = stream.unit0["in1"]
            group(u, 0, 0, TC1, T1, lambda j: norm_at("n0", "lo", 4 * j + 4))
            pe.wait_ge(S["par_placed"], 2)
            sum_over("n0", T1)
            group(u + 4, 1, 1, TC1, T1)
            with pe.Fori(1, G_IN1 // 2) as i:
                for b in range(2):
                    group(u + 8 * i + 4 * b, 2 * i + b, b, TC1, T1)
            group(u + 4 * G_IN1, G_IN1, G_IN1 % 2, TC1, T1, ncol=1)
            pe.sem_inc(S["at_scored"], 2)
            pe.sem_inc(S["at_v_turned"], 2)
            pe.sem_inc(S["at_p_turned"], 2)
            pe.sem_inc(S["at_out"], 2)
            for n in range(4):
                pe.wait_ge(S["qk_sq"], n + 1)
                if n >= 2:
                    pe.wait_ge(S["qk_inv"], n - 1)
                for k in range(2):
                    mm = pe.matmul(psum[:, 4 + 2 * (n % 2) + k], ones[:],
                                   M["head_sq"][:, 2 * k:2 * k + 2].rearrange("p a t -> p (a t)"),
                                   start=True, stop=True)
                mm.then_inc(S["qk_ss"], 1)
            pe.wait_ge(S["qk_done"], 4)
            with pe.Fori(0, 4) as i:
                for b in range(2):
                    h = 2 * i + b
                    qs, vs = M["q_still"][:, b], M["v_still"][:, b]
                    pe.wait_ge(S["at_still"], 2 * h + 2)
                    pe.wait_ge(S["at_done"], h + 1)
                    kt = proj[:, bass.ds(h + 8, 1)][:, 0]
                    pe.matmul(psum[:, 4 + b, 0:P], qs[:, 0:P], kt[:, 0:P], start=True, stop=True)
                    pe.matmul(psum[:, 4 + b, P:384], qs[:, P:256], kt, start=True, stop=True) \
                        .then_inc(S["at_scored"], 1)
                    pe.wait_ge(S["at_pt"], h + 1)
                    pe.transpose(psum[:, 6 + b, 0:P], vs[:, 0:P], ident[:])
                    pe.transpose(psum[:, 6 + b, P:256], vs[:, P:256], ident[:]) \
                        .then_inc(S["at_v_turned"], 1)
                for b in range(2):
                    h = 2 * i + b
                    pe.wait_ge(S["at_probs"], 2 * h + 2)
                    pe.wait_ge(S["at_v"], h + 1)
                    for k in range(3):
                        mm = pe.transpose(psum[:, 6 + b, P * k:P * k + P],
                                          M["scores"][:, b, P * k:P * k + P], ident[:])
                    mm.then_inc(S["at_p_turned"], 1)
                for b in range(2):
                    h = 2 * i + b
                    pe.wait_ge(S["at_pt"], h + 3)
                    vr, pt = M["v_rows"][:, b], M["probs_t"][:, b]
                    pe.matmul(psum[:, 4 + b, 0:P], vr[:, 0:P], pt[:, 0:P], start=True, stop=True)
                    pe.matmul(psum[:, 4 + b, P:256], vr[:, 0:P], pt[:, P:256],
                              start=True, stop=False)
                    pe.matmul(psum[:, 4 + b, P:256], vr[:, P:256], pt[:, 256:384],
                              start=False, stop=True) \
                        .then_inc(S["at_out"], 1)
            step = M["step"]
            pe.wait_ge(S["attention_over"], 1)
            pe.wait_ge(S["dt_cum"], 2)
            pe.wait_ge(*ssd_dve.at("dt_w"))
            for k, (row, at) in enumerate(((5, 0), (5, P), (3, 0), (3, P), (6, 0))):
                mm = pe.transpose(psum[:, 4, 16 * k:16 * k + 16], step[0:16, row, at:at + P],
                                  ident[0:16, 0:16])
            mm.then_inc(S["ssd_tensor"], 1)
            pe.wait_ge(S["sc_silu"], 12)
            for g in range(2):
                for c in range(2):
                    cs = slice(c * CH, c * CH + CH)
                    mm = pe.matmul(psum[:, 5, P * (2 * g + c):P * (2 * g + c) + P],
                                   proj[:, 40 + g, cs], proj[:, 42 + g, cs], start=True, stop=True)
            mm.then_inc(S["ssd_tensor"], 1)
            for g in range(2):
                mm = pe.transpose(psum[:, 6, P * g:P * g + P], proj[:, 40 + g, 0:P], ident[:])
            mm.then_inc(S["ssd_tensor"], 1)
            for n in range(4):
                c, half = divmod(n, 2)
                bank = (7, 4, 5, 6)[n]
                if n:
                    pe.wait_ge(*ssd_dve.at(("dt_rows", "cb_masked", "b_placed")[n - 1]))
                for k in range(4):
                    mm = pe.transpose(psum[:, bank, P * k:P * k + P],
                                      proj[:, 32 + 4 * half + k, c * CH:c * CH + CH], ident[:])
                mm.then_inc(S["xs_turned"], 1)
            pe.wait_ge(*ssd_dve.at("b_placed"))
            pe.wait_ge(S["xdt_made"], 6)
            for g in range(2):
                pe.matmul(psum[:, 7 - 3 * g], M["b_rows"][:, g], M["xdte"][:, 512 * g:512 * g + 512],
                          start=True, stop=True).then_inc(S["st_made"], 1)
            pe.wait_ge(S["st_placed"], 2)

            def rows_out(n):
                pe.wait_ge(S["sg_diag"], n + 1)
                if n >= 2:
                    pe.wait_ge(S["sg_seg"], 2 * n - 2)
                    if n % 2:
                        pe.wait_ge(S["sg_e1"], (n - 1) // 2)
                pe.matmul(psum[:, 4 + n % 2], ones[0:16, :], M["diag"][0:16, n % 2],
                          start=True, stop=True).then_inc(S["sg_row"], 1)

            rows_out(0)
            for n in range(8):
                hb, c = divmod(n, 2)
                if n < 7:
                    rows_out(n + 1)
                pe.wait_ge(S["sg_g"], n + 1)
                if c:
                    pe.wait_ge(S["sg_cte"], hb + 1)
                elif hb >= 2:
                    pe.wait_ge(S["y_gated"], hb - 1)
                for k in range(4):
                    h = 4 * hb + k
                    e, p = h % 2, (h // 2) % 2
                    at = 256 * p + CH * c
                    out_ = psum[64 * e:64 * e + 64, 6 + hb % 2, at:at + CH]
                    mm = pe.matmul(out_, M["xdt"][:, c, 64 * h:64 * h + 64],
                                   M["gmat"][:, n % 2, CH * k:CH * k + CH], start=True, stop=not c)
                    if c:
                        mm = pe.matmul(out_, M["state0"][:, h // 8, 64 * (h % 8):64 * (h % 8) + 64],
                                       M["cte"][:, 1, CH * k:CH * k + CH], start=False, stop=True)
                mm.then_inc(S["sg_used"], 1)
            for g in range(2):
                pe.wait_ge(S["yn_sq"], g + 1)
                for k in range(4):
                    mm = pe.matmul(psum[:, 4 + g, 0:T1], ones[:], M["y_sq"][:, k],
                                   start=(k == 0), stop=(k == 3))
                mm.then_inc(S["yn_ss"], 1)
            u, g0 = stream.unit0["out1"], stream.group0["out1"]
            pe.wait_ge(S["mix_lo"], 2)
            with pe.Fori(0, 4) as i:
                out_units(u + 4 * i, g0 + 2 * i, TC1, T1, 0, g0 % 2)
            with pe.Fori(0, 4) as i:
                out_units(u + 4 * i + 16, g0 + 2 * i + 8, TC1, T1, 1, g0 % 2)

            def ffn(name, norm, T, tc):
                u, g0, n0 = stream.unit0[name], stream.group0[name], chunks_before[name]
                pair0 = g0 % 2

                def ups(v, g):
                    for j in range(4):
                        group(v + 4 * j, g + j, (pair0 + j) % 2, tc, T)

                def downs(v, g, i, hi_, lo_):
                    pe.wait_ge(S["ff_fflo"], i + (n0 + 1))
                    for d in range(8):
                        bank_free(g + d)
                        unit(v + d, d % 4, (pair0 + d) % 2, hi_, lo_, 0, T1, True, True)

                group(u, g0, pair0, tc, T, lambda j: norm_at(norm, "lo", 4 * j + 4))
                sum_over(norm, T)
                for j in range(1, 4):
                    group(u + 4 * j, g0 + j, (pair0 + j) % 2, tc, T)
                with pe.Fori(1, FCH) as i:
                    ups(u + 24 * i - 8, 12 * i - 8 + g0)
                    downs(u + 24 * i + 8, 12 * i - 4 + g0, i - 1, M["ff_hi"],
                          M["ff_lo"])
                downs(u + 24 * FCH - 8, g0 + 12 * FCH - 8, FCH - 1, M["last_hi"],
                      M["last_lo"])

            ffn("ffn1", "n1", T1, TC1)
            u, g0 = stream.unit0["in2"], stream.group0["in2"]
            group(u, g0, g0 % 2, TC2, T2, lambda j: norm_at("n2", "lo", 4 * j + 4), m=96, shift=96)
            sum_over("n2", T2)
            group(u + 4, g0 + 1, (g0 + 1) % 2, TC2, T2)
            with pe.Fori(0, IN2_RKV // 2) as i:
                for b in range(2):
                    group(u + 8 + 8 * i + 4 * b, g0 + 2 + 2 * i + b, (g0 + b) % 2, TC2, T2)
            low, t7, rk_a = M["low"], M["t7"], M["rk_a"]
            pe.wait_ge(S["low_landed"], 32)
            pe.wait_ge(S["low_act"], 1)
            for n in range(16):
                if n >= 4:
                    pe.wait_ge(S["low_out"], n - 3)
                j = n % 8
                pe.matmul(psum[:, 4 + n % 4, 0:T2], M["w_low"][0:96, n // 8, P * j:P * j + P],
                          low[0:96, n // 8, PAD:RT], start=True, stop=True) \
                    .then_inc(S["low_up"], 1)
            pe.wait_ge(S["kk_sq"], 1)
            for j in range(8):
                if j == 0:
                    pe.wait_ge(S["low_out"], 16)
                if j >= 4:
                    pe.wait_ge(S["kk_max"], j - 3)
                pe.matmul(psum[:, 4 + j % 4, 0:RT], halves[:], t7[:, j], start=True, stop=True) \
                    .then_inc(S["kk_ss"], 1)
            for j in range(8):
                pe.wait_ge(S["bo_scaled"], j + 1)
                if j >= 4:
                    pe.wait_ge(S["bo_made"], j - 3)
                pe.matmul(psum[:, 4 + j % 4, 0:T2], halves[:], t7[:, j, PAD:RT], start=True,
                          stop=True).then_inc(S["bo_sum"], 1)
            fs, uu, mt, st = M["fs"], M["uu"], M["mt"], M["state"]
            b_tok, kv, ru = M["b_tok"], M["kv_tok"], M["ru"]
            halfp = [slice(64 * e, 64 * e + 64) for e in range(2)]

            def each_head(lhs, rhs_, bank, wide=RB):
                for h in range(4):
                    mm = pe.matmul(psum[0:RB, bank, wide * h:wide * h + wide], lhs[0:RB, h],
                                   rhs_(h), start=True, stop=True)
                mm.then_inc(S["rw_tensor"], 1)

            uc, gc = u + 8 + 4 * IN2_RKV, g0 + 2 + IN2_RKV
            pe.wait_ge(S["bo_made"], 8)
            with pe.Fori(0, 4) as q:
                with pe.Fori(0, 3) as tt:
                    it = 3 * q + tt
                    n = it + 1
                    v, vg = uc + 12 * q + 4 * tt, gc + 3 * q + tt

                    def conv_rows(*ks):
                        for k in ks:
                            j, r = divmod(k, RK)
                            if r == 0:
                                pe.wait_ge(S["lo_done"], v + j + 1)
                            mm = unit_row(j, 0, act_hi, act_lo, 4 * j, T2, j == 0, j == 3, r)
                            if r == RK - 1:
                                mm.then_inc(S["unit_used"], 1)

                    pe.wait_ge(S["rw_end"], n)
                    pe.wait_ge(S["evicted"], vg)
                    pe.wait_ge(S["rw_still"], 3 * it + 3)
                    pe.wait_ge(S["rw_still_act"], 2 * it + 2)
                    for k, bank in ((2, 4), (3, 6)):
                        for p in range(2):
                            for e in range(2):
                                mm = pe.matmul(psum[0:RB, bank + e, 192 * p:192 * p + 192],
                                               fs[halfp[e], p, k], fs[halfp[e], p, 0:2],
                                               start=True, stop=True)
                        mm.then_inc(S["rw_tensor"], 1)
                    conv_rows(0, 1)
                    pe.wait_ge(*rw_dve.at("rbt", it))
                    for p in range(2):
                        for e in range(2):
                            mm = pe.matmul(psum[0:RB, 4 + e, RB * p:RB * p + RB],
                                           fs[halfp[e], p, 0], fs[halfp[e], p, 2],
                                           start=True, stop=True)
                    mm.then_inc(S["rw_tensor"], 1)
                    conv_rows(2)
                    pe.wait_ge(*rw_dve.at("rkt", it))
                    for ks, bank in (((0, 2), 6), ((3, 4), 7)):
                        for a, k in enumerate(ks):
                            for p in range(2):
                                at = P * (2 * a + p)
                                mm = pe.transpose(psum[0:RB, bank, at:at + P], fs[:, p, k],
                                                  ident[:])
                        mm.then_inc(S["rw_tensor"], 1)
                    conv_rows(3)
                    pe.wait_ge(*rw_dve.at("ld", it))
                    each_head(M["ldt"], lambda h: M["ld"][0:RB, h], 4)
                    each_head(M["ld"], lambda h: M["ldt"][0:RB, h], 5)
                    conv_rows(4)
                    pe.wait_ge(*rw_act.at("b_tok", it))
                    pe.wait_ge(*rw_act.at("kv", it))
                    each_head(M["akt"], lambda h: kv[0:RB, 1, 64 * h:64 * h + 64], 6, 64)
                    conv_rows(5)
                    pe.wait_ge(*rw_dve.at("l2_out", it))
                    pe.wait_ge(*rw_act.at("l2t_out", it))
                    pe.wait_ge(*rw_dve.at("p1", it))
                    each_head(M["l2t"], lambda h: M["l2"][0:RB, h], 4)
                    each_head(M["l2"], lambda h: M["l2t"][0:RB, h], 5)
                    each_head(M["l2"], lambda h: M["p1"][0:RB, h], 7)
                    conv_rows(6, 7)
                    pe.wait_ge(*rw_act.at("l4_out", it))
                    pe.wait_ge(*rw_dve.at("l4t_out", it))
                    each_head(l4t, lambda h: l4[0:RB, h], 4)
                    conv_rows(8)
                    pe.wait_ge(*rw_dve.at("p2", it))
                    pe.wait_ge(*rw_act.at("rhs_v", it))
                    each_head(l4, lambda h: p2[0:RB, h], 6)
                    conv_rows(9)
                    pe.wait_ge(*rw_act.at("l8_out", it))
                    pe.wait_ge(*rw_dve.at("p3", it))
                    each_head(l8, lambda h: p3[0:RB, h], 7)
                    conv_rows(10)
                    pe.wait_ge(*rw_dve.at("p4", it))
                    each_head(p4, lambda h: M["rhs"][0:RB, h], 4, P)
                    conv_rows(11)
                    pe.wait_ge(*rw_act.at("y1_out", it))
                    each_head(M["lot"], lambda h: M["y1"][0:RB, h], 5, P)
                    conv_rows(12)
                    pe.wait_ge(*rw_dve.at("z", it))
                    each_head(p4, lambda h: zz[0:RB, h], 6, P)
                    conv_rows(13)
                    pe.wait_ge(*rw_dve.at("u", it))
                    for p in range(2):
                        for e in range(2):
                            h = 2 * p + e
                            mm = pe.matmul(psum[halfp[e], 7, RB * p:RB * p + RB],
                                           uu[0:RB, 0, h], M["rbt"][0:RB, h],
                                           start=(p == 0), stop=True, skip_group_check=True)
                    mm.then_inc(S["rw_tensor"], 1)
                    for c in range(3):
                        rows32 = slice(RC * c, RC * c + RC)
                        for p in range(2):
                            mm = pe.matmul(psum[:, 4 + c, P * p:P * p + P],
                                           uu[rows32, 0, 2 * p:2 * p + 2].rearrange("p h k -> p (h k)"),
                                           b_tok[rows32, P * p:P * p + P],
                                           start=True, stop=True)
                    mm.then_inc(S["rw_tensor"], 1)
                    conv_rows(14)
                    pe.wait_ge(*rw_dve.at("ru", it))
                    for p in range(2):
                        for e in range(2):
                            h = 2 * p + e
                            o = psum[halfp[e], 7, 256 + RB * p:256 + RB * p + RB]
                            pe.matmul(o, uu[0:RB, 1, h], M["rbt"][0:RB, h], start=(p == 0),
                                      stop=False, skip_group_check=True)
                            pe.matmul(o, kv[0:RB, 1, 64 * h:64 * h + 64], M["rkt"][0:RB, h],
                                      start=False, stop=False, skip_group_check=True)
                    conv_rows(15)
                    pe.wait_ge(*rw_dve.at("mt1", it))
                    for c in range(3):
                        rows32 = slice(RC * c, RC * c + RC)
                        for p in range(2):
                            o = psum[:, 4 + c, P * p:P * p + P]
                            pe.matmul(o, b_tok[rows32, P * p:P * p + P],
                                      uu[rows32, 1, 2 * p:2 * p + 2], start=(p == 0),
                                      stop=False, skip_group_check=True)
                            pe.matmul(o, kv[rows32, 0, P * p:P * p + P],
                                      kv[rows32, 1, P * p:P * p + P], start=False, stop=False,
                                      skip_group_check=True)
                        pe.wait_ge(S["rw_s"], 19 * q + 1 + 6 * tt + 2 * c)
                        for p in range(2):
                            at = 256 + RB * p + RC * c
                            pe.matmul(psum[:, 7, at:at + RC], st[:, p],
                                      ru[:, p, RC * c:RC * c + RC], start=False, stop=True,
                                      skip_group_check=True)
                        for p in range(2):
                            mm = pe.matmul(psum[:, 4 + c, P * p:P * p + P], mt[:, c, p], st[:, p],
                                           start=False, stop=True, skip_group_check=True)
                        mm.then_inc(S["rw_tensor"], 1)
            t8 = M["t8"]
            u, g0 = stream.unit0["out2"], stream.group0["out2"]
            pe.wait_ge(S["rw_end"], 13)
            for j in range(8):
                if j >= 4:
                    pe.wait_ge(S["gn_centred"], j - 3)
                pe.matmul(psum[:, 4 + j % 4, 0:T2], halves[:], rk_a[:, j, PAD:RT], start=True,
                          stop=True).then_inc(S["gn_mean"], 1)
            pe.wait_ge(S["mix_lo"], 3)
            out_units(u, g0, TC3, T3, 0, g0 % 2)
            pe.wait_ge(S["gn_sq"], 1)
            for j in range(8):
                if j >= 4:
                    pe.wait_ge(S["gn_used"], j - 3)
                pe.matmul(psum[:, 4 + j % 4, 0:RT], halves[:], t8[:, j], start=True, stop=True) \
                    .then_inc(S["gn_ss"], 1)
            out_units(u + 4, g0 + 2, TC3, T3, 0, g0 % 2)
            out_units(u + 8, g0 + 4, TC3, T3, 0, g0 % 2)
            pe.wait_ge(S["gup_landed"], 16)
            for j in range(8):
                if j >= 4:
                    pe.wait_ge(S["gn_done"], j - 3)
                for k in range(2):
                    mm = pe.matmul(psum[:, 4 + j % 4, 0:T2], M["g_up"][:, k, P * j:P * j + P],
                                   low[:, 2 + k, PAD:RT], start=(k == 0), stop=(k == 1))
                mm.then_inc(S["gate_made"], 1)
            out_units(u + 12, g0 + 6, TC3, T3, 0, g0 % 2)
            pe.wait_ge(S["mix_lo"], 4)
            with pe.Fori(0, 4) as i:
                out_units(u + 4 * i + 16, g0 + 2 * i + 8, TC3, T3, 1, g0 % 2)
            sum_over("n3", T3)
            ffn("ffn2", "n4", T3, TC3)
            sum_over("n5", T1)
            for n in range(8):
                tt, g = divmod(n, 4)
                if n == 3:
                    pe.wait_ge(*norm_at("n5", "ms", 1))
                if n >= 4:
                    pe.wait_ge(S["out_copied"], n - 3)
                pe.wait_ge(S["post"], KD + 4 * g + 4)
                for k in range(4):
                    mm = pe.transpose(psum[:, 4 + n % 4, P * k:P * k + P],
                                      resid[:, 4 * g + k, T0 + P * tt:T0 + P * tt + P], ident[:])
                mm.then_inc(S["out_turned"], 1)


_INS = [
    "x", "norm1_w", "w_in", "q_norm_w", "k_norm_w", "ssm_conv_w", "ssm_conv_b", "dt_bias", "a_log",
    "d_skip", "ssm_norm_w", "w_out", "norm2_w", "w_up", "ffn_conv_w", "ffn_conv_b", "w_down",
    "meta_tokens_2", "g_pre_mix_2", "w_in_2", "conv_w_2", "mu_rwkv_2", "w_decay_up_2", "w0_2",
    "a_up_2", "a0_2", "g_up_2", "k_k_2", "k_a_2", "r_k_2", "ln_x_w_2", "ln_x_b_2", "w_out_2",
    "g_post_mix_2", "g_pre_ffn_2", "w_gate_up_2", "conv_ffn_2", "w_down_2", "g_post_ffn_2",
]


def kernel(**inputs):
    import numpy as np
    from concourse import bacc
    from concourse.bass_utils import run_bass_kernel_spmd

    nc = bacc.Bacc("TRN2", target_bir_lowering=False, num_devices=1)
    arrays, args = {}, []
    for name in _INS:
        a = np.ascontiguousarray(inputs[name])
        arrays[f"in_{name}"] = a
        args.append(nc.dram_tensor(f"in_{name}", a.shape, mybir.dt.from_np(a.dtype),
                                   kind="ExternalInput").ap())
    x = arrays["in_x"]
    out = nc.dram_tensor("out_x", x.shape, mybir.dt.from_np(x.dtype), kind="ExternalOutput").ap()
    two_blocks(nc, *args, out)
    got = run_bass_kernel_spmd(nc, [arrays], core_ids=[0])
    return got.results[0]["out_x"]
```

```python
import math
from contextlib import ExitStack

import concourse.bass as bass
from concourse import mybir

ALU = mybir.AluOpType
ACT = mybir.ActivationFunctionType
F32 = mybir.dt.float32
F32R = mybir.dt.float32r
AX_X = mybir.AxisListType.X

P = 128
BIG = 1.0e30


class Semaphores:

    def __init__(self, nc):
        self.nc, self.made = nc, {}

    def __getitem__(self, name):
        if name not in self.made:
            self.made[name] = self.nc.alloc_semaphore(name)
        return self.made[name]


class Tally:

    def __init__(self, sem, names, start=0):
        self.sem, self.names, self.start = sem, names.split(), start

    def at(self, name, again=0):
        return self.sem, again * len(self.names) + (self.start + self.names.index(name) + 1)


class Stream:

    def __init__(self):
        self.units = self.groups = 0
        self.unit0, self.group0 = {}, {}

    def phase(self, name, groups, units):
        self.unit0[name], self.group0[name] = self.units, self.groups
        self.units += units
        self.groups += groups


def two_blocks(
    nc, x, norm1_w, w_in, q_norm_w, k_norm_w, ssm_conv_w, ssm_conv_b, dt_bias, a_log, d_skip,
    ssm_norm_w, w_out, norm2_w, w_up, ffn_conv_w, ffn_conv_b, w_down, meta_tokens_2,
    g_pre_mix_2, w_in_2, conv_w_2, mu_rwkv_2, w_decay_up_2, w0_2, a_up_2, a0_2, g_up_2, k_k_2,
    k_a_2, r_k_2, ln_x_w_2, ln_x_b_2, w_out_2, g_post_mix_2, g_pre_ffn_2, w_gate_up_2,
    conv_ffn_2, w_down_2, g_post_ffn_2, out,
):
    _, SEQ, D = x.shape
    META = meta_tokens_2.shape[0]
    T1, T2 = SEQ, SEQ + META
    T0 = META
    LEAD = 2
    T3 = SEQ + LEAD
    TC1, TC2, TC3 = slice(T0, T2), slice(0, T2), slice(T0 - LEAD, T2)
    KD = D // P
    CH = 128
    DFF = w_down.shape[1]
    FCH = DFF // 512
    assert D == 2048 and SEQ == 256 and META == 16 and DFF == FCH * 512
    RK = 4
    NSLOT = 4
    RT = 288
    PAD = RT - T2
    RB = 96
    RC = 32
    RW = 8

    EPS = 1e-6
    GN_EPS = 64e-5
    DECAY = math.exp(-0.5)

    stream = Stream()
    G_IN1 = 22
    stream.phase("in1", G_IN1 + 1, 4 * (G_IN1 + 1))
    stream.phase("out1", 16, 32)
    stream.phase("ffn1", 4 * FCH + 8 * FCH, 24 * FCH)
    stream.phase("in2", 26, 104)
    stream.phase("out2", 16, 32)
    stream.phase("ffn2", 4 * FCH + 8 * FCH, 24 * FCH)

    chunks_before = {"ffn1": 0, "ffn2": FCH}

    S = Semaphores(nc)
    landed = [S[f"raw_landed_{j}"] for j in range(NSLOT)]

    rw_pe = Tally(S["rw_tensor"], "lt ak l tab tkv l2 l2t akv l4 l4t p2m l8 p3m p4m y1 zm xm rum "
                                  "mtm step0 step1 step2")
    rw_dve = Tally(S["rw_vector"], "ldt lot rbt akt rkt p1 ld l2_out l4t_out p2 p3 p4 z u ru mt0 "
                                   "mt1", start=3)
    rw_act = Tally(S["rw_scalar"], "rhs_a b_tok kv l2t_out rhs_v l4_out l8_out y1_out")
    ssd_pe = Tally(S["ssd_tensor"], "dt_turned cb_made b_turned")
    ssd_dve = Tally(S["ssd_vector"], "dt_w dt_rows cb_masked b_placed")
    MADE_CONSTS = 6
    MADE_CAUSAL = MADE_CONSTS + 3
    MADE_UPTO = MADE_CAUSAL + 2
    MADE_SCAN = MADE_UPTO + 2
    MADE_RWKV = MADE_SCAN + 5 + 2 + 2 + 2 + 2 + 4 + 1
    NORM_SIGNALS = dict(sq=4, add=5, ss=1, ms=1, inv=1, rstd=1, hi=16, lo=16)
    HI_NORMS = ("n0", "n1", "n2", "n4")

    def norm_at(name, what, n):
        before = HI_NORMS.index(name) if what in ("hi", "lo") else int(name[1])
        return S["norm_" + what], NORM_SIGNALS[what] * before + n

    def sb(name, shape, dtype=F32):
        return nc.alloc_sbuf_tensor(name, shape, dtype)

    raw = sb("raw", [P, NSLOT, RK * 256])
    w_hi = sb("w_hi", [P, NSLOT, RK * 256], F32R)
    w_lo = sb("w_lo", [P, NSLOT, RK * 256], F32R)
    resid = sb("resid", [P, KD, T2])
    act_hi = sb("act_hi", [P, KD, T2], F32R)
    act_lo = sb("act_lo", [P, KD, T2], F32R)
    ident = sb("ident", [P, P])
    ones = sb("ones", [P, P])
    halves = sb("halves", [P, P])
    rstd = sb("rstd", [P, T2])
    ss_part = sb("ss_part", [P, T2])
    head_par = sb("head_par", [P, 6])

    rows = []

    def rows_of(ap, n):
        at = sum(r[1] for r in rows)
        rows.append((ap, n, at))
        return at

    def flat(ap):
        return ap.rearrange("a d -> (a d)")

    def tiles(ap1, n):
        return ap1.rearrange("(k p) -> k p", p=P), n

    c_dskip = rows_of(None, 8)
    c_norm1 = rows_of(*tiles(flat(norm1_w), 16))
    c_qn = rows_of(q_norm_w, 1)
    rows_of(k_norm_w, 1)
    c_sconv = rows_of(ssm_conv_w.rearrange("a j (k p) -> (a j k) p", p=P), 48)
    c_sconvb = rows_of(*tiles(flat(ssm_conv_b), 12))
    c_snorm = rows_of(*tiles(flat(ssm_norm_w), 8))
    c_norm2 = rows_of(*tiles(flat(norm2_w), 16))
    fconv = ffn_conv_w.rearrange("a j (k p) -> (a j) k p", p=P)
    c_fconv = [rows_of(fconv[j], 88) for j in range(3)]
    c_fconvb = rows_of(*tiles(flat(ffn_conv_b), 88))
    c_premix = rows_of(*tiles(g_pre_mix_2, 16))
    c_conv2 = rows_of(conv_w_2.rearrange("j (k p) -> (j k) p", p=P), 24)
    c_mu = rows_of(mu_rwkv_2[0:3072].rearrange("(k p) -> k p", p=P), 24)
    c_mug = rows_of(mu_rwkv_2[3264:3520].rearrange("(k p) -> k p", p=P), 2)
    c_w0 = rows_of(*tiles(w0_2, 8))
    c_a0 = rows_of(*tiles(a0_2, 8))
    c_kk = rows_of(*tiles(k_k_2, 8))
    c_ka = rows_of(*tiles(k_a_2, 8))
    c_rk = rows_of(*tiles(flat(r_k_2), 8))
    c_lnw = rows_of(*tiles(ln_x_w_2, 8))
    c_lnb = rows_of(*tiles(ln_x_b_2, 8))
    c_postmix = rows_of(*tiles(g_post_mix_2, 16))
    c_preffn = rows_of(*tiles(g_pre_ffn_2, 16))
    gconv = conv_ffn_2.rearrange("j (k p) -> j k p", p=P)
    c_gconv = [rows_of(gconv[j], 44) for j in range(3)]
    c_postffn = rows_of(*tiles(g_post_ffn_2, 16))
    c_mulow = rows_of(None, 2)
    NROWS = sum(r[1] for r in rows)
    NPACK = -(-NROWS // P)
    par = sb("par", [P, NPACK * P])
    assert c_mulow // P == (c_mulow + 1) // P

    def col(c):
        return par[:, c:c + 1]

    def shared(shapes, keep=None):
        own = ExitStack()
        got = {n: own.enter_context(nc.sbuf_tensor(n, [P, *s], d)) for n, s, d in shapes}
        if keep is None:
            own.close()
        else:
            keep.enter_context(own)
        return got

    M = {}
    for names in (
        [("packs", [NPACK, P], F32), ("x_rows", [2, D], F32), ("meta_rows", [D], F32)],
        [
            ("proj", [45, T1], F32),
            ("squares1", [8, T2], F32),
            ("head_sq", [4, T1], F32), ("head_r", [4, T1], F32),
            ("q_still", [2, T1], F32), ("v_still", [2, T1], F32),
            ("causal", [384], F32), ("scores", [2, 384], F32), ("probs_t", [2, 384], F32),
            ("v_rows", [2, 2 * P], F32), ("soft", [2, 8], F32),
        ],
        [
            ("proj_ssd", [45, T1], F32), ("upto", [P], F32), ("conv_out", [4, T1], F32),
            ("step", [7, T1], F32), ("step_rows", [5, 16], F32), ("minus_a", [1], F32),
            ("cb", [4, P], F32), ("b_rows", [2, P], F32), ("xdt", [2, 1024], F32),
            ("xdte", [1024], F32), ("state0", [2, 512], F32), ("diag", [2, 512], F32),
            ("seg", [2, 512], F32), ("gmat", [2, 512], F32), ("cte", [2, 512], F32),
            ("y_r", [2, T1], F32),
        ],
        [
            ("up", [8, T3], F32), ("conv", [8, T1], F32), ("ff", [4, T1], F32),
            ("squares2", [8, T2], F32),
            ("ff_hi", [4, T1], F32R), ("ff_lo", [4, T1], F32R),
            ("last_hi", [4, T1], F32R), ("last_lo", [4, T1], F32R), ("out_rows", [2, D], F32),
        ],
    ):
        M.update(shared(names))
    both = ExitStack()
    M.update(shared([
        ("z2", [24, RT], F32),
        ("rk_a", [RW, RT], F32),
        ("rk_b", [RW, RT], F32),
        ("bonus", [RW, RT], F32), ("low", [4, RT], F32), ("wc", [RW, 9], F32),
    ], both))
    M.update(shared([("squares3", [8, T2], F32)]))
    M.update(shared([
        ("t5", [RW, RT], F32), ("t6", [RW, RT], F32), ("t7", [RW, RT], F32),
        ("w_low", [2, 1024], F32), ("scan_keep", [RT], F32), ("before", [2, T2], F32),
    ]))
    M.update(shared([
        ("fs", [2, 5, RB], F32),
        ("ldt", [4, RB], F32), ("lot", [4, RB], F32), ("rbt", [4, RB], F32),
        ("akt", [4, RB], F32), ("rkt", [4, RB], F32), ("ld", [4, RB], F32),
        ("p1", [4, RB], F32), ("l2", [4, RB], F32), ("l2t", [4, RB], F32),
        ("rhs", [4, P], F32), ("y1", [4, P], F32), ("uu", [2, 4, 64], F32),
        ("b_tok", [2 * P], F32), ("kv_tok", [2, 2 * P], F32), ("ru", [2, RB], F32),
        ("mt", [3, 2, P], F32), ("state", [2, P], F32),
        ("m_ldt", [RB], F32), ("m_lot", [RB], F32), ("m_r", [RB], F32), ("m_a", [RB], F32),
        ("m_ld", [RB], F32),
        ("gate_b", [2, T2], F32), ("gate_c", [2, T2], F32),
    ]))
    M.update(shared([("t8", [RW, RT], F32), ("g_up", [2, 1024], F32), ("mixed", [KD, T2], F32)]))
    both.close()

    proj = M["proj"]
    psum = nc.alloc_psum_tensor("psum", [P, 8, 512], F32)
    l8, p2, p3, p4 = M["l2"], M["ld"], M["p1"], M["ldt"]
    y_sq = M["diag"][:].rearrange("p a (b t) -> p (a b) t", t=T1)
    l4, l4t, zz = M["akt"], M["l2t"], M["rhs"]
    y_conv = M["z2"][:, 0:8, PAD:RT]

    def over(ap, axis, n):
        wide = ap.unsqueeze(axis)
        shape = list(wide.shape)
        shape[axis] = n
        return wide.to_broadcast(shape)

    def four(bank):
        return psum[0:RB, bank, 0:4 * RB].rearrange("p (h t) -> p h t", t=RB)

    def unit_rows(w):
        return w.rearrange("(j r p) n -> j p r n", r=RK, p=P)

    w_in1, w_out1, w_up1, w_dn1 = (unit_rows(w[0]) for w in (w_in, w_out, w_up, w_down))
    w_in2, w_out2, w_up2, w_dn2 = (unit_rows(w) for w in (w_in_2, w_out_2, w_gate_up_2, w_down_2))
    KRV_TILE = (8, 10, 12, 14, 0, 2, 4, 6, 16, 18, 20, 22)
    IN2_RKV = 12
    n_param_loads = {"first_params": 0, "params_landed": 0}

    with nc.Block() as block:

        @block.sync
        def _(sp):
            def load(u, slot, src, wide=256):
                if not isinstance(u, int) or u >= NSLOT:
                    sp.wait_ge(S["lo_done"], u - NSLOT + 1)
                dst = raw[:, slot].rearrange("p (r n) -> p r n", r=RK)[:, :, 0:wide]
                sp.dma_start(dst, src).then_inc(landed[slot], 16)

            def load_group(u, w, c0, wide=256):
                for j in range(4):
                    load(u + j, j, w[j][:, :, bass.ds(c0, wide)], wide)

            def half_loads(u, w):
                for half in range(2):
                    with sp.Fori(0, 4) as i:
                        for b in range(2):
                            for j in range(2):
                                load(u + 16 * half + 4 * i + 2 * b + j, 2 * b + j,
                                     w[2 * half + j][:, :, bass.ds(512 * i + 256 * b, 256)])

            sp.dma_start(M["x_rows"][:, 0], x[0, 0:P, :]).then_inc(S["x_landed"], 16)
            sp.dma_start(M["x_rows"][:, 1], x[0, P:2 * P, :]).then_inc(S["x_landed"], 16)
            sp.dma_start(M["meta_rows"][0:META], meta_tokens_2).then_inc(S["x_landed"], 16)
            sp.dma_start(head_par[0:8, 4:6], d_skip.rearrange("a (j b) -> (a j) b", b=2)) \
                .then_inc(S["d_landed"], 16)
            sp.wait_ge(S["packs_cleared"], 1)

            def load_params(first_pack):
                for ap, count, at in rows:
                    done = 0
                    while done < count and ap is not None:
                        pack, row = divmod(at + done, P)
                        k = min(count - done, P - row)
                        if (pack == 0) == first_pack:
                            sem = "first_params" if first_pack else "params_landed"
                            sp.dma_start(M["packs"][row:row + k, pack], ap[done:done + k]) \
                                .then_inc(S[sem], 16)
                            n_param_loads[sem] += 1
                        done += k

            load_params(True)
            u = stream.unit0["in1"]
            load_group(u, w_in1, 0)
            load_params(False)
            pack, row = divmod(c_mulow, P)
            assert pack > 0
            sp.dma_start(M["packs"][row:row + 2, pack, 0:96],
                         mu_rwkv_2[3072:3264].rearrange("(a b) -> a b", a=2)) \
                .then_inc(S["params_landed"], 16)
            n_param_loads["params_landed"] += 1
            sp.dma_start(head_par[0:16, 0:1], dt_bias.rearrange("a h -> h a")) \
                .then_inc(S["heads_landed"], 16)
            sp.dma_start(head_par[0:16, 1:2], a_log.rearrange("a h -> h a")) \
                .then_inc(S["heads_landed"], 16)
            with sp.Fori(1, G_IN1) as g:
                load_group(u + 4 * g, w_in1, 256 * g)
            load_group(u + 4 * G_IN1, w_in1, 256 * G_IN1, 16)
            half_loads(stream.unit0["out1"], w_out1)

            def ffn_loads(name, w_up, w_dn):
                u = stream.unit0[name]

                def ups(u, i):
                    for j, c0 in enumerate((0, 256, DFF, DFF + 256)):
                        load_group(u + 4 * j, w_up, c0 + 512 * i)

                def downs(u, i):
                    for d in range(8):
                        load(u + d, d % 4, w_dn[bass.ds(i, 1)][0][:, :, 256 * d:256 * d + 256])

                ups(u, 0)
                with sp.Fori(1, FCH) as i:
                    ups(u + 24 * i - 8, i)
                    downs(u + 24 * i + 8, i - 1)
                downs(u + 24 * FCH - 8, FCH - 1)

            ffn_loads("ffn1", w_up1, w_dn1)
            u = stream.unit0["in2"]
            load_group(u, w_in2, 6144, 192)
            load_group(u + 4, w_in2, 6336)
            for n, c0 in enumerate((4096, 3072, 5120)):
                with sp.Fori(0, 4) as g:
                    load_group(u + 8 + 16 * n + 4 * g, w_in2, c0 + 256 * g)
            u = u + 8 + 4 * IN2_RKV
            with sp.Fori(0, 4) as q:
                for j in range(3):
                    load_group(u + 12 * q + 4 * j, w_in2, 1024 * j + 256 * q)
            half_loads(stream.unit0["out2"], w_out2)
            ffn_loads("ffn2", w_up2, w_dn2)
            for n in range(8):
                g, tt = divmod(n, 2)
                sp.wait_ge(S["out_copied"], n + 1)
                cs = slice(512 * g, 512 * g + 512)
                sp.dma_start(out[0, tt * P:tt * P + P, cs], M["out_rows"][:, tt, cs]) \
                    .then_inc(S["stored"], 16)
            sp.wait_ge(S["stored"], 128)

        @block.gpsimd
        def _(pool):
            def select(out, in_, pattern, op, fill, base, mult):
                pool.wait_ge(S["made"], made[0])
                pool.affine_select(out=out, in_=in_, pattern=pattern, compare_op=op, fill=fill,
                                   base=base, channel_multiplier=mult).then_inc(S["made"], 1)
                made[0] += 1

            made = [0]
            for t, v in ((ones, 1.0), (ident, 1.0), (halves, 1.0)):
                pool.memset(t[:], v).then_inc(S["made"], 1)
            made[0] += 3
            select(ident[:], ident[:], [[-1, P]], ALU.is_equal, 0.0, 0, 1)
            h3 = halves[:].rearrange("p (b c) -> p b c", b=2)
            select(h3, h3, [[-64, 2], [0, 64]], ALU.is_ge, 0.0, 0, 1)
            select(h3, h3, [[64, 2], [0, 64]], ALU.is_ge, 0.0, 63, -1)

            def add_squares(name, sq, T, j):
                pool.wait_ge(*norm_at(name, "sq", j + 1))
                if j > 1:
                    pool.wait_ge(*norm_at(name, "add", j - 1))
                pool.tensor_tensor(sq[:, 0:4, 0:T], sq[:, 0:4, 0:T], sq[:, 4:8, 0:T], ALU.add) \
                    .then_inc(S["norm_add"], 1)

            def fold_squares(name, sq, T):
                pool.wait_ge(*norm_at(name, "add", 3))
                pool.tensor_tensor(sq[:, 0:2, 0:T], sq[:, 0:2, 0:T], sq[:, 2:4, 0:T], ALU.add) \
                    .then_inc(S["norm_add"], 1)
                pool.wait_ge(*norm_at(name, "add", 4))
                pool.tensor_tensor(ss_part[:, 0:T], sq[:, 0, 0:T], sq[:, 1, 0:T], ALU.add) \
                    .then_inc(S["norm_add"], 1)

            def sum_squares(name, sq, T):
                for j in range(1, 4):
                    add_squares(name, sq, T, j)
                fold_squares(name, sq, T)

            def add_post(before, tc, squares):
                for k in range(KD):
                    pool.wait_ge(S["post_scaled"], before + k + 1)
                    pool.tensor_tensor(resid[:, k, tc], resid[:, k, tc], M["mixed"][:, k, tc],
                                       ALU.add).then_inc(S["post"], 1)
                if squares:
                    sum_squares("n4", M["squares2"], T3)

            sum_squares("n0", M["squares1"], T1)
            pool.memset(M["causal"][:], 0.0).then_inc(S["made"], 1)
            made[0] += 1
            select(M["causal"][:, 0:P], M["causal"][:, 0:P], [[-1, P]], ALU.is_ge, -BIG, 0, 1)
            select(M["causal"][:, P:384], M["causal"][:, P:384], [[-1, 256]], ALU.is_ge, -BIG, P, 1)
            pool.wait_ge(S["qk_done"], 4)
            pool.wait_ge(S["evicted"], 12)
            with pool.Fori(0, 4) as i:
                for b in range(2):
                    pool.wait_ge(S["at_scored"], 2 * i + b + 1)
                    pool.wait_ge(S["at_v_turned"], 2 * i + b + 1)
                    pool.tensor_copy(M["q_still"][:, b], proj[:, bass.ds(2 * i + b, 1)][:, 0]) \
                        .then_inc(S["at_still"], 1)
                    pool.tensor_copy(M["v_still"][:, b], proj[:, bass.ds(2 * i + b + 16, 1)][:, 0]) \
                        .then_inc(S["at_still"], 1)
            pool.wait_ge(S["attention_over"], 1)
            pool.memset(M["upto"][:], 1.0).then_inc(S["made"], 1)
            made[0] += 1
            select(M["upto"][:], M["upto"][:], [[1, P]], ALU.is_ge, 0.0, 0, -1)
            sum_squares("n1", M["squares2"], T1)
            sum_squares("n2", M["squares3"], T2)
            pool.wait_ge(*norm_at("n2", "rstd", 1))
            sk = M["scan_keep"][:].rearrange("p (c t) -> p c t", t=RC)
            pool.memset(M["scan_keep"][:], 1.0).then_inc(S["made"], 1)
            made[0] += 1
            select(sk, sk, [[0, RT // RC], [1, RC]], ALU.is_gt, 0.0, 0, 0)
            pool.wait_ge(S["k_made"], 1)
            pool.tensor_tensor(M["rk_b"][:], M["rk_b"][:], M["rk_a"][:], ALU.mult) \
                .then_inc(S["b_made"], 1)
            pool.wait_ge(S["low_up"], 16)
            for n in ("m_ldt", "m_lot", "m_r", "m_a", "m_ld"):
                pool.memset(M[n][0:RB], 1.0).then_inc(S["made"], 1)
            made[0] += 5

            def same(name, w):
                m = M[name][0:RB].rearrange("p (b c) -> p b c", c=w)
                select(m, m, [[-w, RB // w], [0, w]], ALU.is_ge, 0.0, 0, 1)
                select(m, m, [[w, RB // w], [0, w]], ALU.is_ge, 0.0, w - 1, -1)

            def beyond(name, op, sign):
                m = M[name][0:RB]
                select(m, m, [[sign, RB]], op, 0.0, 0, -sign)

            same("m_ldt", 16)
            beyond("m_ldt", ALU.is_gt, 1)
            same("m_r", RC)
            beyond("m_r", ALU.is_ge, 1)
            same("m_a", RC)
            beyond("m_a", ALU.is_gt, 1)
            same("m_ld", 16)
            beyond("m_ld", ALU.is_gt, -1)
            pool.wait_ge(S["made"], made[0])
            pool.tensor_tensor(M["m_lot"][0:RB], M["m_a"][0:RB], M["m_ldt"][0:RB], ALU.subtract) \
                .then_inc(S["made"], 1)
            assert made[0] + 1 == MADE_RWKV
            with pool.Fori(0, 4) as q:
                with pool.Fori(0, 3) as tt:
                    pool.wait_ge(*rw_dve.at("ru", 3 * q + tt - 1))
                    for k, (src, t0) in enumerate((("rk_b", 0), ("z2", 8), ("z2", 16))):
                        pool.tensor_copy(
                            M["fs"][:, :, 2 + k],
                            M[src][:, bass.ds(2 * q + t0, 2), bass.ds(RB * tt, RB)],
                        ).then_inc(S["rw_still"], 1)
            pool.wait_ge(S["bo_made"], 8)
            b = M["bonus"][:, :, PAD:RT]
            pool.tensor_tensor(b, b, M["z2"][:, 16:24, PAD:RT], ALU.mult) \
                .then_inc(S["bonus_made"], 1)
            sum_squares("n3", M["squares2"], T3)
            add_post(0, TC3, True)
            sum_squares("n5", M["squares2"], T1)
            add_post(KD, TC1, False)

        @block.scalar
        def _(act):
            def hi(u, slot):
                act.wait_ge(landed[slot], 16 * (u // 4 + 1) if isinstance(u, int)
                            else landed_at(u, slot))
                if not isinstance(u, int) or u >= NSLOT:
                    act.wait_ge(S["unit_used"], u - NSLOT + 1)
                act.activation(w_hi[:, slot], raw[:, slot], ACT.Copy).then_inc(S["hi_done"], 1)

            def wait_apart(sem, value):
                act.wait_ge(sem, value)
                act.wait_ge(S["par_placed"], 3)

            def landed_at(u, slot):
                return (u - slot) * 4 + 16

            def hi_group(u):
                for j in range(4):
                    hi(u + j, j)

            def square(name, src, sq, j, tc):
                if j >= 2:
                    act.wait_ge(*norm_at(name, "add", j - 1))
                half = sq[:, 0:4] if j == 0 else sq[:, 4:8]
                act.activation(half[:, :, 0:tc.stop - tc.start], src[:, 4 * j:4 * j + 4, tc],
                               ACT.Square).then_inc(S["norm_sq"], 1)

            def norm_tiles(name, c, sq, d, tc):
                for k in (2 * d, 2 * d + 1):
                    act.activation(act_hi[:, k, tc], resid[:, k, tc], ACT.Identity,
                                   scale=col(c + k)).then_inc(S["norm_hi"], 1)
                if d % 2:
                    square(name, resid, sq, d // 2, tc)

            def rstd_root(name, T):
                act.wait_ge(*norm_at(name, "inv", 1))
                act.activation(rstd[:, 0:T], rstd[:, 0:T], ACT.Sqrt).then_inc(S["norm_rstd"], 1)

            hi_group(stream.unit0["in1"])
            act.wait_ge(S["x_placed"], 9)
            act.wait_ge(S["par_placed"], 1)
            for d in range(8):
                norm_tiles("n0", c_norm1, M["squares1"], d, TC1)
            u = stream.unit0["in1"]
            hi_group(u + 4)
            rstd_root("n0", T1)
            with act.Fori(2, 5) as g:
                hi_group(u + 4 * g)
            with act.Fori(0, 4) as n:
                wait_apart(S["qk_ss"], n + 1)
                wait_apart(S["evicted"], 2 * n + 2)
                act.activation(M["head_sq"][:], proj[:, bass.ds(4 * n, 4)], ACT.Square) \
                    .then_inc(S["qk_sq"], 1)
                hi_group(u + 20 + 8 * n)
                act.wait_ge(S["qk_inv"], n + 2)
                act.activation(M["head_r"][:], M["head_r"][:], ACT.Sqrt).then_inc(S["qk_rstd"], 1)
                hi_group(u + 24 + 8 * n)
            scale = 128.0 ** -0.5
            act.sem_inc(S["at_pt"], 2)
            with act.Fori(0, 4) as i:
                hi_group(u + 52 + 8 * i)
                for b in range(2):
                    act.wait_ge(S["at_v_turned"], 2 * i + b + 3)
                    act.wait_ge(S["at_out"], 2 * i + b + 1)
                    act.activation(M["v_rows"][:, b], psum[:, 6 + b, 0:256], ACT.Copy) \
                        .then_inc(S["at_v"], 1)
                for b in range(2):
                    act.wait_ge(S["at_shift"], 2 * i + b + 1)
                    for k, (lo, wide) in enumerate(((0, P), (P, 256))):
                        s = M["scores"][:, b, lo:lo + wide]
                        act.activation(s, s, ACT.Exp, bias=M["soft"][:, b, 2 + k:3 + k], scale=scale,
                                       accum_out=M["soft"][:, b, 4 + k:5 + k]) \
                            .then_inc(S["at_exp"], 1)
                hi_group(u + 56 + 8 * i)
                for b in range(2):
                    act.wait_ge(S["at_p_turned"], 2 * i + b + 3)
                    act.wait_ge(S["at_out"], 2 * i + b + 1)
                    act.activation(M["probs_t"][:, b], psum[:, 6 + b, 0:384], ACT.Copy) \
                        .then_inc(S["at_pt"], 1)
            for g in range(21, G_IN1 + 2):
                hi_group(u + 4 * g)
            act.wait_ge(S["attention_over"], 1)
            uo = stream.unit0["out1"]
            act.wait_ge(S["unit_used"], uo)
            act.activation(act_hi[:, 0:8, TC1], proj[:, 0:8], ACT.Copy).then_inc(S["mix_hi"], 1)
            step = M["step"]
            act.wait_ge(S["dt_abs"], 2)
            act.activation(step[0:16, 2], step[0:16, 1], ACT.Exp, scale=-1.0) \
                .then_inc(S["dt_exp"], 1)
            act.wait_ge(S["heads_landed"], 32)
            act.activation(head_par[0:16, 2:3], head_par[0:16, 1:2], ACT.Exp) \
                .then_inc(S["dt_exp"], 1)
            act.wait_ge(S["dt_exp"], 1)
            act.activation(step[0:16, 2], step[0:16, 2], ACT.Ln, bias=1.0).then_inc(S["dt_ln"], 1)
            for i in range(7):
                if i == 3:
                    act.wait_ge(S["dt_cum"], 2)
                    act.activation(step[0:16, 6, 0:P], step[0:16, 5, 0:P], ACT.Exp, scale=-1.0,
                                   bias=step[0:16, 5, P - 1:P]).then_inc(S["dt_end"], 1)
                if i < 6:
                    if i >= 2:
                        act.wait_ge(S["sc_silu"], 2 * i - 2)
                    for n in (2 * i, 2 * i + 1):
                        act.activation(M["conv_out"][:, n % 4], proj[:, 32 + n], ACT.Identity,
                                       bias=col(c_sconvb + n), scale=col(c_sconv + 36 + n)) \
                            .then_inc(S["sc_first"], 1)
                if i:
                    for b in range(2):
                        n = 2 * i - 2 + b
                        act.wait_ge(S["sc_taps"], 6 * i - 1 + b)
                        act.activation(proj[:, 32 + n], M["conv_out"][:, n % 4], ACT.Silu) \
                            .then_inc(S["sc_silu"], 1)
                if i in (3, 6):
                    hi_group(uo + 4 * (i // 3))
            act.activation(proj[:, 24:32], proj[:, 24:32], ACT.Silu).then_inc(S["z_silu"], 1)
            for n in range(8):
                if n % 2:
                    act.wait_ge(S["sg_row"], n + 1)
                    act.wait_ge(S["sg_seg"], 2 * n + 1)
                    if n > 2:
                        act.wait_ge(S["sg_cte"], (n - 1) // 2)
                    act.activation(M["cte"][:, 0], psum[:, 4 + n % 2], ACT.Exp) \
                        .then_inc(S["sg_e1"], 1)
                act.wait_ge(S["sg_seg"], 2 * n + 2)
                act.activation(M["seg"][:, n % 2], M["seg"][:, n % 2], ACT.Exp) \
                    .then_inc(S["sg_exp"], 1)
                if n % 2:
                    for k in range(2):
                        hi(uo + n + 11 + k, (n - 1) % 4 + k)
            for g in range(2):
                act.wait_ge(S["y_gated"], 2 * g + 2)
                if g:
                    act.wait_ge(S["yn_ss"], 1)
                act.activation(y_sq, proj[:, 32 + 4 * g:36 + 4 * g], ACT.Square) \
                    .then_inc(S["yn_sq"], 1)
            for g in range(2):
                act.wait_ge(S["yn_inv"], g + 1)
                act.activation(M["y_r"][:, g], M["y_r"][:, g], ACT.Sqrt).then_inc(S["yn_rstd"], 1)
            for g in range(2):
                act.wait_ge(S["yn_done"], 4 * g + 4)
                act.activation(act_hi[:, 8 + 4 * g:12 + 4 * g, TC1],
                               proj[:, 32 + 4 * g:36 + 4 * g], ACT.Copy).then_inc(S["mix_hi"], 1)
            u, g0 = stream.unit0["out1"], stream.group0["out1"]
            for d in range(8):
                for k in range(2):
                    hi(u + 20 + 2 * d + k, (2 * d + k) % 4)
                if d < 4:
                    act.wait_ge(S["evicted"], g0 + 9 + d)
                    norm_tiles("n1", c_norm2, M["squares2"], d, TC1)
            act.wait_ge(S["unit_used"], u + 32)
            for d in range(4, 8):
                act.wait_ge(S["evicted"], g0 + 9 + d)
                norm_tiles("n1", c_norm2, M["squares2"], d, TC1)

            def ffn(name, norm, lead, cc, cb, vals, last_step):
                u, g0, n0 = stream.unit0[name], stream.group0[name], chunks_before[name]
                nt = 8 if vals else 4
                K1 = len(cc) - 1

                def first_taps(i):
                    for t in range(nt):
                        c = (44 if t >= 4 else 0) + t % 4
                        how = dict(scale=par[:, bass.ds(4 * i + (c + cc[K1]), 1)])
                        if cb is not None:
                            how["bias"] = par[:, bass.ds(4 * i + (c + cb), 1)]
                        act.activation(M["conv"][:, t], M["up"][:, t, lead:lead + T1],
                                       ACT.Identity, **how).then_inc(S["ff_first"], 1)

                def silu(i):
                    act.wait_ge(S["ff_taps"], 2 * nt * i + (16 * n0 + 8))
                    act.activation(M["conv"][:, 0:4], M["conv"][:, 0:4], ACT.Silu) \
                        .then_inc(S["ff_silu"], 1)

                def product_hi(i, u_down, dst):
                    act.wait_ge(S["ff_ff"], i + (n0 + 1))
                    if u_down is not None:
                        act.wait_ge(S["unit_used"], u_down)
                    act.activation(dst[:], M["ff"][:], ACT.Copy).then_inc(S["ff_ffhi"], 1)

                def while_up(i, v):
                    hi_group(v)
                    wait_apart(S["evicted"], 12 * i - 8 + g0)
                    first_taps(i - 1)
                    hi_group(v + 4)
                    silu(i - 1)
                    hi_group(v + 8)
                    product_hi(i - 1, v, M["ff_hi"])
                    hi_group(v + 12)

                hi_group(u + 4)
                rstd_root(norm, T1 + lead)
                for j in range(2, 4):
                    hi_group(u + 4 * j)
                with act.Fori(1, FCH - 1) as i:
                    v = u + 24 * i - 8
                    while_up(i, v)
                    hi_group(v + 16)
                    hi_group(v + 20)
                i = FCH - 1
                w = u + 24 * i + 8
                while_up(i, w - 16)
                hi_group(w)
                act.wait_ge(S["evicted"], 12 * i - 4 + g0)
                first_taps(i)
                hi(w + 4, 0)
                hi(w + 5, 1)
                silu(i)
                for k in range(2, 5):
                    hi(w + 4 + k, k % 4)
                product_hi(i, None, M["last_hi"])
                for k in range(5, 8):
                    hi(w + 4 + k, k % 4)
                for d in range(8):
                    if d < 4 or w + 12 + d < stream.units:
                        hi(w + 12 + d, d % 4)
                    act.wait_ge(S["evicted"], g0 + 12 * FCH - 7 + d)
                    last_step(d)

            ffn("ffn1", "n1", 0, c_fconv, c_fconvb, True,
                lambda d: norm_tiles("n2", c_premix, M["squares3"], d, TC2))
            act.dma_start(M["w_low"][0:96, 0], w_decay_up_2).then_inc(S["low_landed"], 16)
            act.dma_start(M["w_low"][0:96, 1], a_up_2).then_inc(S["low_landed"], 16)
            u = stream.unit0["in2"]
            hi_group(u + 4)
            rstd_root("n2", T2)
            hi_group(u + 8)
            low, t5, t6, t7 = M["low"], M["t5"], M["t6"], M["t7"]
            rk_a, rk_b = M["rk_a"], M["rk_b"]

            def low_out(dst, c, n0):
                for j in range(8):
                    act.wait_ge(S["low_up"], n0 + j + 1)
                    act.activation(dst[:, j, PAD:RT], psum[:, 4 + j % 4, 0:T2], ACT.Sigmoid,
                                   bias=col(c + j)).then_inc(S["low_out"], 1)

            for j in range(12):
                hi_group(u + 12 + 4 * j)
                if j == 0:
                    act.wait_ge(S["low_shifted"], 4)
                    act.activation(low[0:96, 0], low[0:96, 0], ACT.Tanh).then_inc(S["low_act"], 1)
                    act.activation(low[:, 2:4], low[:, 2:4], ACT.Sigmoid) \
                        .then_inc(S["low_act"], 1)
                elif j == 1:
                    act.wait_ge(S["pads"], 4)
                    low_out(t5, c_w0, 0)
                elif j == 2:
                    low_out(rk_b, c_a0, 8)
                elif j == 3:
                    act.wait_ge(S["kk_scaled"], 8)
                    act.activation(t7[:], rk_a[:], ACT.Square).then_inc(S["kk_sq"], 1)
                elif j == 4:
                    act.wait_ge(S["kk_max"], 8)
                    act.activation(t7[:], t7[:], ACT.Ln).then_inc(S["kk_root"], 1)
                    act.wait_ge(S["kk_root"], 1)
                    act.activation(t7[:], t7[:], ACT.Exp, scale=-0.5).then_inc(S["kk_root"], 1)
                elif j == 7:
                    act.wait_ge(S["decay_prev"], 1)
                    act.activation(t5[:], t5[:], ACT.Exp, scale=-DECAY) \
                        .then_inc(S["decay_exp"], 1)
                elif j == 8:
                    act.wait_ge(S["a_made"], 1)
                    act.activation(t5[:], t6[:], ACT.Exp, scale=DECAY).then_inc(S["decay_exp"], 1)
                elif j == 10:
                    act.wait_ge(S["bk_made"], 2)
                    act.activation(t5[:], t6[:], ACT.Exp, scale=-DECAY) \
                        .then_inc(S["decay_exp"], 1)
                    for t in range(8):
                        act.wait_ge(S["bo_sum"], t + 1)
                        act.activation(M["bonus"][:, t, PAD:RT], psum[:, 4 + t % 4, 0:T2],
                                       ACT.Copy).then_inc(S["bo_made"], 1)
            act.wait_ge(S["rpre_over"], 1)
            fs = M["fs"]
            uc = u + 8 + 4 * IN2_RKV
            with act.Fori(0, 4) as q:
                with act.Fori(0, 3) as tt:
                    it = 3 * q + tt
                    wait_apart(*rw_dve.at("ru", it - 1))
                    for k, (src, t0) in enumerate((("rk_a", 0), ("z2", 0))):
                        act.activation(
                            fs[:, :, k], M[src][:, bass.ds(2 * q + t0, 2), bass.ds(RB * tt, RB)],
                            ACT.Copy).then_inc(S["rw_still_act"], 1)
                    act.wait_ge(*rw_pe.at("tab", it))
                    act.activation(M["rhs"][0:RB, :, 0:64],
                                   psum[0:RB, 6, 0:256].rearrange("p (h k) -> p h k", k=64),
                                   ACT.Copy).then_inc(S["rw_scalar"], 1)
                    act.activation(M["b_tok"][0:RB], psum[0:RB, 6, 256:512], ACT.Copy) \
                        .then_inc(S["rw_scalar"], 1)
                    act.wait_ge(*rw_pe.at("tkv", it))
                    act.activation(M["kv_tok"][0:RB].rearrange("p a b -> p (a b)"),
                                   psum[0:RB, 7, 0:512], ACT.Copy).then_inc(S["rw_scalar"], 1)
                    act.wait_ge(*rw_pe.at("l2t", it))
                    act.activation(M["l2t"][0:RB], four(5), ACT.Copy).then_inc(S["rw_scalar"], 1)
                    v = uc + 4 + 12 * q + 4 * tt
                    hi(v, 0)
                    act.wait_ge(*rw_pe.at("akv", it))
                    act.activation(M["rhs"][0:RB, :, 64:P],
                                   psum[0:RB, 6, 0:256].rearrange("p (h k) -> p h k", k=64),
                                   ACT.Copy).then_inc(S["rw_scalar"], 1)
                    act.wait_ge(*rw_pe.at("l4", it))
                    act.activation(l4[0:RB], four(4), ACT.Copy).then_inc(S["rw_scalar"], 1)
                    act.wait_ge(*rw_pe.at("l8", it))
                    act.activation(l8[0:RB], four(4), ACT.Copy).then_inc(S["rw_scalar"], 1)
                    hi(v + 1, 1)
                    act.wait_ge(*rw_pe.at("y1", it))
                    act.activation(M["y1"][0:RB].rearrange("p h k -> p (h k)"),
                                   psum[0:RB, 4, 0:512], ACT.Copy).then_inc(S["rw_scalar"], 1)
                    hi(v + 2, 2)
                    hi(v + 3, 3)
            act.wait_ge(S["rw_end"], 13)
            act.dma_start(M["g_up"][:], g_up_2.rearrange("(a p) n -> p a n", p=P)) \
                .then_inc(S["gup_landed"], 16)
            uo = stream.unit0["out2"]
            act.wait_ge(S["cv_done"], 5)
            act.wait_ge(S["unit_used"], uo)
            act.activation(act_hi[:, 0:8], y_conv, ACT.Copy).then_inc(S["mix_hi"], 1)
            t8 = M["t8"]
            hi_group(uo + 4)
            act.wait_ge(S["gn_centred"], 8)
            act.activation(t8[:], rk_a[:], ACT.Square).then_inc(S["gn_sq"], 1)
            act.wait_ge(S["gn_used"], 8)
            act.activation(t8[:], t8[:], ACT.Ln).then_inc(S["gn_root"], 1)
            act.wait_ge(S["gn_root"], 1)
            act.activation(t8[:], t8[:], ACT.Exp, scale=-0.5).then_inc(S["gn_root"], 1)
            hi(uo + 8, 0)
            hi(uo + 9, 1)
            hi(uo + 10, 2)
            hi(uo + 11, 3)
            hi_group(uo + 12)
            act.wait_ge(S["gn_done"], 8)
            act.activation(act_hi[:, 8:16], rk_a[:, :, PAD:RT], ACT.Copy).then_inc(S["mix_hi"], 1)
            go = stream.group0["out2"]
            hi_group(uo + 16)
            for d in range(8):
                for k in range(2):
                    hi(uo + 20 + 2 * d + k, (2 * d + k) % 4)
                if d % 2:
                    act.wait_ge(S["evicted"], go + 9 + d)
                    square("n3", M["mixed"], M["squares2"], d // 2, TC3)
            rstd_root("n3", T3)
            act.wait_ge(*norm_at("n3", "add", 5))
            for d in range(8):
                act.wait_ge(S["post"], 2 * d + 2)
                norm_tiles("n4", c_preffn, M["squares2"], d, TC3)
            def last_squares(d):
                if d % 2:
                    square("n5", M["mixed"], M["squares2"], d // 2, TC1)

            ffn("ffn2", "n4", LEAD, c_gconv, None, False, last_squares)
            rstd_root("n5", T1)

        @block.vector
        def _(dve):
            def lo(u, slot):
                dve.wait_ge(S["hi_done"], u + 1)
                dve.tensor_tensor(w_lo[:, slot], raw[:, slot], w_hi[:, slot].bitcast(F32),
                                  ALU.subtract).then_inc(S["lo_done"], 1)

            def lo_group(u):
                for j in range(4):
                    lo(u + j, j)

            def bank_pair(pair, T, rows_=P):
                return psum[0:rows_, 2 * pair:2 * pair + 2, 0:T]

            def leave(u_end, pair, dst, T, rows_=P, how="scaled", single=False):
                dve.wait_ge(S["unit_used"], u_end)
                src = bank_pair(pair, T, rows_)
                if single:
                    src = psum[0:rows_, 2 * pair, 0:T]
                if how == "scaled":
                    r = rstd[0:rows_, 0:T] if single else over(rstd[0:rows_, 0:T], 1, 2)
                    ins = dve.tensor_tensor(dst, src, r, ALU.mult)
                elif how == "added":
                    ins = dve.tensor_tensor(dst, src, dst, ALU.add)
                else:
                    ins = dve.tensor_copy(dst, src)
                ins.then_inc(S["evicted"], 1)

            def rstd_of(name, T, width, eps):
                dve.wait_ge(*norm_at(name, "ss", 1))
                dve.tensor_scalar(rstd[:, 0:T], psum[:, 7, 0:T], 1.0 / width, eps, ALU.mult,
                                  ALU.add).then_inc(S["norm_ms"], 1)
                dve.wait_ge(*norm_at(name, "ms", 1))
                dve.reciprocal(rstd[:, 0:T], rstd[:, 0:T]).then_inc(S["norm_inv"], 1)
                dve.wait_ge(*norm_at(name, "rstd", 1))

            def norm_lo(name, c, tc, tiles=range(KD)):
                for k in tiles:
                    dve.wait_ge(*norm_at(name, "hi", k + 1))
                    dve.scalar_tensor_tensor(
                        out=act_lo[:, k, tc], in0=resid[:, k, tc], scalar=col(c + k),
                        in1=act_hi[:, k, tc].bitcast(F32), op0=ALU.mult, op1=ALU.subtract,
                    ).then_inc(S["norm_lo"], 1)

            def norm_pair(name, c, tc, d):
                if d >= 0:
                    norm_lo(name, c, tc, (2 * d, 2 * d + 1))

            links = [0]

            def link(ins):
                links[0] += 1
                ins.then_inc(S["dve_links"], 1)
                dve.wait_ge(S["dve_links"], links[0])

            dve.memset(M["packs"][:], 0.0).then_inc(S["packs_cleared"], 1)
            dve.wait_ge(S["packs_cleared"], 1)
            dve.wait_ge(S["d_landed"], 16)
            assert c_dskip == 0
            dve.tensor_copy(M["packs"][0:8, 0].rearrange("p (b e) -> p b e", b=2),
                            over(head_par[0:8, 4:6], 2, 64)).then_inc(S["d_placed"], 1)
            for n in range(8):
                tt, g = divmod(n, 4)
                dve.wait_ge(S["x_turned"], n + 1)
                dve.tensor_copy(resid[:, 4 * g:4 * g + 4, T0 + P * tt:T0 + P * tt + P],
                                psum[:, 4 + n % 4].rearrange("p (k t) -> p k t", t=P)) \
                    .then_inc(S["x_placed"], 1)
            dve.wait_ge(S["x_turned"], 9)
            dve.tensor_copy(resid[:, :, 0:T0],
                            psum[:, 4, 0:KD * T0].rearrange("p (k t) -> p k t", t=T0)) \
                .then_inc(S["x_placed"], 1)
            dve.wait_ge(S["par_turned"], 1)
            dve.tensor_copy(par[:, 0:P], psum[:, 5, 0:P]).then_inc(S["par_placed"], 1)
            lo_group(stream.unit0["in1"])
            dve.wait_ge(S["par_placed"], 1)
            norm_lo("n0", c_norm1, TC1)
            u, g0 = stream.unit0["in1"], stream.group0["in1"]
            lo_group(u + 4)
            rstd_of("n0", T1, D, EPS)
            dve.wait_ge(S["par_turned"], 2)
            assert 5 < NPACK <= 8
            dve.tensor_copy(par[:, P:5 * P], psum[:, 6]).then_inc(S["par_placed"], 1)
            dve.tensor_copy(par[:, 5 * P:NPACK * P], psum[:, 5, P:(NPACK - 4) * P]) \
                .then_inc(S["par_placed"], 1)

            def in1_group(g, b):
                lo_group(u + 4 * g)
                leave(u + 4 * g, b, proj[:, bass.ds(2 * g - 2, 2)], T1)

            leave(u + 4, 0, proj[:, 0:2], T1)
            for g in range(2, 5):
                in1_group(g, (g - 1) % 2)
            hr = M["head_r"]
            dve.sem_inc(S["qk_inv"], 1)
            with dve.Fori(0, 2) as m:
                for e in range(2):
                    n = 2 * m + e
                    in1_group(2 * n + 5, 0)
                    dve.wait_ge(S["qk_ss"], n + 2)
                    dve.wait_ge(S["qk_done"], n)
                    dve.tensor_scalar(hr[:].rearrange("p (a b) t -> p a (b t)", a=2),
                                      psum[:, 4:6], 1.0 / 128, EPS, ALU.mult, ALU.add) \
                        .then_inc(S["qk_ms"], 1)
                    dve.wait_ge(S["qk_ms"], n + 1)
                    dve.reciprocal(hr[:], hr[:]).then_inc(S["qk_inv"], 1)
                    in1_group(2 * n + 6, 1)
                    dve.wait_ge(S["qk_rstd"], n + 1)
                    q4 = proj[:, bass.ds(4 * n, 4)]
                    dve.scalar_tensor_tensor(out=q4, in0=q4, scalar=par[:, bass.ds(m + c_qn, 1)],
                                             in1=hr[:], op0=ALU.mult, op1=ALU.mult) \
                        .then_inc(S["qk_done"], 1)
            dve.wait_ge(S["made"], MADE_CAUSAL)
            dve.sem_inc(S["at_done"], 2)
            scale = 128.0 ** -0.5
            with dve.Fori(0, 4) as i:
                in1_group(2 * i + 13, 0)
                for b in range(2):
                    sc, sf = M["scores"][:, b], M["soft"][:, b]
                    dve.wait_ge(S["at_scored"], 2 * i + b + 3)
                    dve.wait_ge(S["at_p_turned"], 2 * i + b + 1)
                    dve.tensor_tensor(sc, psum[:, 4 + b, 0:384], M["causal"][:], ALU.add) \
                        .then_inc(S["at_masked"], 1)
                    dve.wait_ge(S["at_masked"], 2 * i + b + 1)
                    dve.tensor_reduce(sf[:, 0:1], sc[:, 0:P], AX_X, ALU.max) \
                        .then_inc(S["at_max"], 1)
                    dve.tensor_reduce(sf[:, 1:2], sc[:, P:384], AX_X, ALU.max) \
                        .then_inc(S["at_max"], 1)
                    dve.wait_ge(S["at_max"], 4 * i + 2 * b + 2)
                    dve.tensor_scalar(sf[:, 2:4], sf[:, 0:2], -scale, None, ALU.mult) \
                        .then_inc(S["at_shift"], 1)
                for b in range(2):
                    sc, sf = M["scores"][:, b], M["soft"][:, b]
                    dve.wait_ge(S["at_exp"], 4 * i + 2 * b + 2)
                    dve.reciprocal(sf[:, 6:8], sf[:, 4:6]).then_inc(S["at_sum"], 1)
                    dve.wait_ge(S["at_sum"], 2 * i + b + 1)
                    for k, (at, wide) in enumerate(((0, P), (P, 256))):
                        dve.tensor_scalar(sc[:, at:at + wide], sc[:, at:at + wide],
                                          sf[:, 6 + k:7 + k], None, ALU.mult) \
                            .then_inc(S["at_probs"], 1)
                in1_group(2 * i + 14, 1)
                for b in range(2):
                    dve.wait_ge(S["at_out"], 2 * i + b + 3)
                    dve.tensor_copy(proj[:, bass.ds(2 * i + b, 1)][:, 0], psum[:, 4 + b, 0:256]) \
                        .then_inc(S["at_done"], 1)
            for g in range(21, G_IN1 + 1):
                in1_group(g, (g - 1) % 2)
            lo_group(stream.unit0["out1"])
            leave(u + 4 * G_IN1 + 4, G_IN1 % 2, proj[0:16, 44], T1, 16, single=True)
            dve.wait_ge(S["at_done"], 10)
            dve.sem_inc(S["attention_over"], 1)
            dve.wait_ge(S["mix_hi"], 1)
            dve.tensor_tensor(act_lo[:, 0:8, TC1], proj[:, 0:8], act_hi[:, 0:8, TC1].bitcast(F32),
                              ALU.subtract).then_inc(S["mix_lo"], 1)
            u, g0 = stream.unit0["out1"], stream.group0["out1"]

            def out1_half(u, b, tiles, next_units):
                leave(u, (g0 + b) % 2, resid[:, tiles, TC1], T1, how="added")
                for k in range(2):
                    lo(next_units + k, 2 * b + k)

            def upper_half(d):
                out1_half(u + 2 * d + 2, d % 2, slice(2 * d, 2 * d + 2), u + 2 * d + 4)

            step, srows = M["step"], M["step_rows"]
            s_ = [step[0:16, k] for k in range(7)]
            dve.wait_ge(S["evicted"], G_IN1 + 1)
            dve.wait_ge(S["heads_landed"], 32)
            dve.tensor_scalar(s_[0], proj[0:16, 44], head_par[0:16, 0:1], None, ALU.add) \
                .then_inc(S["dt_abs"], 1)
            dve.wait_ge(S["dt_abs"], 1)
            dve.scalar_tensor_tensor(out=s_[1], in0=s_[0], scalar=-1.0, in1=s_[0], op0=ALU.mult,
                                     op1=ALU.max).then_inc(S["dt_abs"], 1)
            for i in range(6):
                if i == 1:
                    dve.wait_ge(S["dt_ln"], 1)
                    link(dve.scalar_tensor_tensor(out=s_[3], in0=s_[0], scalar=0.0, in1=s_[2],
                                                  op0=ALU.max, op1=ALU.add))
                    dve.wait_ge(S["dt_exp"], 2)
                    link(dve.tensor_scalar(s_[4], s_[3], head_par[0:16, 2:3], -1.0, ALU.mult, ALU.mult))
                    for c in range(2):
                        cs = slice(c * CH, c * CH + CH)
                        dve.tensor_tensor_scan(s_[5][:, cs], ones[0:16, 0:CH], s_[4][:, cs], 0.0,
                                               ALU.mult, ALU.add).then_inc(S["dt_cum"], 1)
                elif i == 4:
                    dve.wait_ge(S["dt_end"], 1)
                    dve.tensor_tensor(s_[6][:, 0:P], s_[6][:, 0:P], s_[3][:, 0:P], ALU.mult) \
                        .then_inc(S["ssd_vector"], 1)
                for k in range(1, 4):
                    for n in (2 * i, 2 * i + 1):
                        if k == 1:
                            dve.wait_ge(S["sc_first"], n + 1)
                        else:
                            dve.wait_ge(S["sc_taps"], 6 * i + 2 * k - 3 + n % 2)
                        cv = M["conv_out"][:, n % 4, k:T1]
                        dve.scalar_tensor_tensor(
                            out=cv, in0=proj[:, 32 + n, 0:T1 - k],
                            scalar=col(c_sconv + 12 * (3 - k) + n), in1=cv, op0=ALU.mult,
                            op1=ALU.add).then_inc(S["sc_taps"], 1)
                if i in (2, 5):
                    upper_half(2 * (i // 3))
                    upper_half(2 * (i // 3) + 1)
            dve.wait_ge(*ssd_pe.at("dt_turned"))
            dve.tensor_copy(srows[:], psum[:, 4, 0:80].rearrange("p (k h) -> p k h", h=16)) \
                .then_inc(S["ssd_vector"], 1)
            dve.wait_ge(*ssd_pe.at("cb_made"))
            dve.wait_ge(S["made"], MADE_UPTO)
            dve.tensor_tensor(M["cb"][:], psum[:, 5].rearrange("p (k l) -> p k l", l=P),
                              over(M["upto"][:], 1, 4), ALU.mult).then_inc(S["ssd_vector"], 1)
            dve.wait_ge(*ssd_pe.at("b_turned"))
            dve.tensor_copy(M["b_rows"][:], psum[:, 6, 0:256].rearrange("p (k l) -> p k l", l=P)) \
                .then_inc(S["ssd_vector"], 1)
            dve.wait_ge(*ssd_dve.at("dt_rows"))
            for n in range(4):
                c, half = divmod(n, 2)
                dve.wait_ge(S["xs_turned"], n + 1)
                bank = (7, 4, 5, 6)[n]
                xt = psum[:, bank].rearrange("p (h k) -> p h k", k=64)
                hs = slice(8 * half, 8 * half + 8)
                dst = M["xdt"][:, c, 512 * half:512 * half + 512]
                dve.tensor_tensor(dst.rearrange("p (h k) -> p h k", k=64), xt,
                                  over(srows[:, 2 + c, hs], 2, 64), ALU.mult) \
                    .then_inc(S["xdt_made"], 1)
                if c == 0:
                    dst = M["xdte"][:, 512 * half:512 * half + 512]
                    dve.tensor_tensor(dst.rearrange("p (h k) -> p h k", k=64), xt,
                                      over(srows[:, 4, hs], 2, 64), ALU.mult) \
                        .then_inc(S["xdt_made"], 1)
            for g in range(2):
                dve.wait_ge(S["st_made"], g + 1)
                dve.tensor_copy(M["state0"][:, g], psum[:, 7 - 3 * g]).then_inc(S["st_placed"], 1)

            def gate(hb):
                dve.wait_ge(S["sg_used"], 2 * hb + 2)
                if hb == 0:
                    dve.wait_ge(S["z_silu"], 1)
                for p in range(2):
                    j = 2 * hb + p
                    link(dve.scalar_tensor_tensor(
                        out=proj[:, 32 + j], in0=proj[:, 32 + j], scalar=col(c_dskip + j),
                        in1=psum[:, 6 + hb % 2, 256 * p:256 * p + 256], op0=ALU.mult, op1=ALU.add))
                dve.tensor_tensor(proj[:, 32 + 2 * hb:34 + 2 * hb], proj[:, 32 + 2 * hb:34 + 2 * hb],
                                  proj[:, 24 + 2 * hb:26 + 2 * hb], ALU.mult) \
                    .then_inc(S["y_gated"], 1)

            def sums_diag(n):
                hb, c = divmod(n, 2)
                if n >= 2:
                    dve.wait_ge(S["sg_row"], n - 1)
                dg = M["diag"][0:16, n % 2].rearrange("p (h l) -> p h l", l=CH)
                dve.tensor_tensor(dg, over(s_[5][:, c * CH:c * CH + CH], 1, 4),
                                  over(ident[0:16, 4 * hb:4 * hb + 4], 2, CH), ALU.mult) \
                    .then_inc(S["sg_diag"], 1)

            def segments(n):
                hb, c = divmod(n, 2)
                seg = M["seg"][:, n % 2]
                dve.wait_ge(S["sg_row"], n + 1)
                if n >= 2:
                    dve.wait_ge(S["sg_g"], n - 1)
                dve.tensor_tensor(seg.rearrange("p (h l) -> p h l", l=CH),
                                  psum[:, 4 + n % 2].rearrange("p (h l) -> p h l", l=CH),
                                  over(srows[:, c, 4 * hb:4 * hb + 4], 2, CH), ALU.subtract) \
                    .then_inc(S["sg_seg"], 1)
                dve.wait_ge(S["sg_seg"], 2 * n + 1)
                dve.tensor_scalar(seg, seg, 0.0, None, ALU.min).then_inc(S["sg_seg"], 1)

            sums_diag(0)
            sums_diag(1)
            segments(0)
            for n in range(8):
                hb, c = divmod(n, 2)
                cs = slice(c * CH, c * CH + CH)
                seg3 = M["seg"][:, n % 2].rearrange("p (h l) -> p h l", l=CH)
                if n < 7:
                    segments(n + 1)
                if n < 6:
                    sums_diag(n + 2)
                if n >= 2:
                    dve.wait_ge(S["sg_used"], n - 1)
                if c:
                    dve.wait_ge(S["sg_e1"], (n + 1) // 2)
                    e3 = M["cte"][:, 0].rearrange("p (h l) -> p h l", l=CH)
                    c3 = M["cte"][:, 1].rearrange("p (h l) -> p h l", l=CH)
                    dve.tensor_tensor(c3, e3, over(proj[:, 42 + hb // 2, cs], 1, 4), ALU.mult) \
                        .then_inc(S["sg_cte"], 1)
                dve.wait_ge(S["sg_exp"], n + 1)
                dve.tensor_tensor(M["gmat"][:, n % 2].rearrange("p (h l) -> p h l", l=CH), seg3,
                                  over(M["cb"][:, 2 * (hb // 2) + c], 1, 4), ALU.mult) \
                    .then_inc(S["sg_g"], 1)
                if n % 2:
                    upper_half(4 + n // 2)
                if n in (3, 5, 7):
                    gate((n - 3) // 2)
            gate(3)
            for g in range(2):
                dve.wait_ge(S["yn_ss"], g + 1)
                link(dve.tensor_scalar(M["y_r"][:, g], psum[:, 4 + g, 0:T1], 1.0 / 512, EPS,
                                       ALU.mult, ALU.add))
                dve.reciprocal(M["y_r"][:, g], M["y_r"][:, g]).then_inc(S["yn_inv"], 1)
            for j in range(8):
                dve.wait_ge(S["yn_rstd"], j // 4 + 1)
                dve.scalar_tensor_tensor(out=proj[:, 32 + j], in0=proj[:, 32 + j],
                                         scalar=col(c_snorm + j), in1=M["y_r"][:, j // 4],
                                         op0=ALU.mult, op1=ALU.mult).then_inc(S["yn_done"], 1)
            for g in range(2):
                dve.wait_ge(S["mix_hi"], 2 + g)
                dve.tensor_tensor(act_lo[:, 8 + 4 * g:12 + 4 * g, TC1],
                                  proj[:, 32 + 4 * g:36 + 4 * g],
                                  act_hi[:, 8 + 4 * g:12 + 4 * g, TC1].bitcast(F32),
                                  ALU.subtract).then_inc(S["mix_lo"], 1)
            for d in range(8):
                out1_half(u + 18 + 2 * d, d % 2, slice(2 * d, 2 * d + 2), u + 20 + 2 * d)
                if 1 <= d <= 4:
                    norm_pair("n1", c_norm2, TC1, d - 1)
            for d in range(4, 8):
                norm_pair("n1", c_norm2, TC1, d)

            def ffn(name, norm, lead, cc, vals, acc, last_step):
                u, g0, n0 = stream.unit0[name], stream.group0[name], chunks_before[name]
                pair0 = g0 % 2
                nt = 8 if vals else 4
                T = T1 + lead
                up, conv, ff = M["up"], M["conv"], M["ff"]

                def taps(i, t0):
                    for t in range(t0, t0 + 4):
                        dve.wait_ge(S["ff_first"], nt * i + (8 * n0 + t + 1))
                        c = (44 if t >= 4 else 0) + t % 4
                        for k in (1, 2):
                            if k == 2:
                                dve.wait_ge(S["ff_taps"], 2 * nt * i + (16 * n0 + 2 * t + 1))
                            n = max(k - lead, 0)
                            cv = conv[:, t, n:T1]
                            dve.scalar_tensor_tensor(
                                out=cv, in0=up[:, t, lead - k + n:lead - k + T1],
                                scalar=par[:, bass.ds(4 * i + (c + cc[2 - k]), 1)],
                                in1=cv, op0=ALU.mult, op1=ALU.add) \
                                .then_inc(S["ff_taps"], 1)

                def product(i):
                    dve.wait_ge(S["ff_silu"], i + (n0 + 1))
                    dve.wait_ge(S["ff_taps"], 2 * nt * i + (16 * n0 + 2 * nt))
                    v = conv[:, 4:8] if vals else up[:, 4:8, lead:T]
                    dve.tensor_tensor(ff[:], conv[:, 0:4], v, ALU.mult) \
                        .then_inc(S["ff_ff"], 1)

                def product_lo(i, hi_, lo_):
                    dve.wait_ge(S["ff_ffhi"], i + (n0 + 1))
                    dve.tensor_tensor(lo_[:], ff[:], hi_[:].bitcast(F32), ALU.subtract) \
                        .then_inc(S["ff_fflo"], 1)

                def leave_up(v, j):
                    leave(v + 4 * j + 4, (pair0 + j) % 2, up[:, 2 * j:2 * j + 2, 0:T], T)

                def leave_down(v, d):
                    leave(v + d + 1, (pair0 + d) % 2, acc[:, 2 * d:2 * d + 2, TC1], T1,
                          how="added")

                def while_up(i, v):
                    taps(i - 1, 0)
                    lo_group(v + 4)
                    if vals:
                        taps(i - 1, 4)
                    leave_up(v, 0)
                    lo_group(v + 8)
                    product(i - 1)
                    leave_up(v, 1)
                    lo_group(v + 12)
                    product_lo(i - 1, M["ff_hi"], M["ff_lo"])
                    leave_up(v, 2)
                    lo_group(v + 16)
                    leave_up(v, 3)

                lo_group(u + 4)
                rstd_of(norm, T, D, EPS)
                leave_up(u, 0)
                for j in range(2, 4):
                    lo_group(u + 4 * j)
                    leave_up(u, j - 1)
                lo_group(u + 16)
                leave_up(u, 3)
                with dve.Fori(1, FCH - 1) as i:
                    v = u + 24 * i - 8
                    while_up(i, v)
                    for d in range(8):
                        leave_down(v + 16, d)
                        lo(v + 20 + d, d % 4)
                i = FCH - 1
                w = u + 24 * i + 8
                while_up(i, w - 16)
                for d in range(8):
                    leave_down(w, d)
                    lo(w + 4 + d, d % 4)
                    if d == 0:
                        taps(i, 0)
                    elif d == 1 and vals:
                        taps(i, 4)
                    elif d == 3:
                        product(i)
                    elif d == 4:
                        product_lo(i, M["last_hi"], M["last_lo"])
                for d in range(8):
                    leave_down(w + 8, d)
                    if d < 4 or w + 12 + d < stream.units:
                        lo(w + 12 + d, d % 4)
                    last_step(d)

            ffn("ffn1", "n1", 0, c_fconv, True, resid,
                lambda d: norm_pair("n2", c_premix, TC2, d - 1))
            norm_pair("n2", c_premix, TC2, 7)
            u, g0 = stream.unit0["in2"], stream.group0["in2"]
            z2, low = M["z2"], M["low"]
            rk_a, rk_b, bonus = M["rk_a"], M["rk_b"], M["bonus"]
            t5, t6, t7 = M["t5"], M["t6"], M["t7"]
            before = M["before"]
            link(dve.memset(z2[:, :, 0:PAD], 0.0))
            link(dve.memset(low[:, :, 0:PAD], 0.0))
            lo_group(u + 4)
            rstd_of("n2", T2, D, EPS)
            leave(u + 4, g0 % 2, low[0:96, 0:2, PAD:RT], T2, 96)
            lo_group(u + 8)
            leave(u + 8, (g0 + 1) % 2, low[:, 2:4, PAD:RT], T2)
            for t in (t5, rk_a, rk_b, bonus):
                dve.memset(t[:, :, 0:PAD], 0.0).then_inc(S["pads"], 1)

            def shift(t, cols_, rows_=P):
                cur, prev = t[0:rows_, :, PAD:RT], t[0:rows_, :, PAD - 1:RT - 1]
                link(dve.tensor_tensor(before[0:rows_], prev, cur, ALU.subtract))
                for j in range(2):
                    link(dve.scalar_tensor_tensor(
                        out=t[0:rows_, j, PAD:RT], in0=before[0:rows_, j],
                        scalar=par[0:rows_, cols_ + j:cols_ + j + 1], in1=t[0:rows_, j, PAD:RT],
                        op0=ALU.mult, op1=ALU.add))

            kz = z2[:, 8:16].rearrange("p a b -> p (a b)")
            f7, fa, f5 = (t[:].rearrange("p a b -> p (a b)") for t in (t7, rk_a, t5))
            for j in range(12):
                lo_group(u + 12 + 4 * j)
                at = KRV_TILE[j]
                leave(u + 12 + 4 * j, (g0 + j) % 2, z2[:, at:at + 2, PAD:RT], T2)
                dve.wait_ge(S["evicted"], g0 + j + 3)
                shift(z2[:, at:at + 2], c_mu + at)
                if j == 0:
                    shift(low[:, 0:2], c_mulow, 96)
                    shift(low[:, 2:4], c_mug)
                    dve.sem_inc(S["low_shifted"], 4)
                if j < 4:
                    for t in (2 * j, 2 * j + 1):
                        dve.tensor_scalar(rk_a[:, t], z2[:, 8 + t], col(c_kk + t), None,
                                          ALU.mult).then_inc(S["kk_scaled"], 1)
                if j == 2:
                    dve.wait_ge(S["low_out"], 8)
                    dve.wait_ge(S["made"], MADE_SCAN)
                    for t in range(8):
                        link(dve.tensor_tensor_scan(t6[:, t], M["scan_keep"][:], t5[:, t], 0.0,
                                                    ALU.mult, ALU.add))
                elif j == 4:
                    for t in range(8):
                        dve.wait_ge(S["kk_ss"], t + 1)
                        dve.tensor_scalar(t7[:, t], psum[:, 4 + t % 4, 0:RT], 1e-24, None,
                                          ALU.max).then_inc(S["kk_max"], 1)
                elif j == 5:
                    dve.wait_ge(S["kk_root"], 2)
                    link(dve.tensor_tensor(rk_a[:], rk_a[:], t7[:], ALU.mult))
                    dve.wait_ge(S["low_out"], 16)
                    for t in range(8):
                        link(dve.tensor_scalar(t7[:, t], rk_b[:, t], -1.0, col(c_ka + t), ALU.add,
                                               ALU.mult))
                elif j == 6:
                    dve.scalar_tensor_tensor(out=kz, in0=f7, scalar=1.0, in1=kz, op0=ALU.add,
                                             op1=ALU.mult).then_inc(S["k_made"], 1)
                    dve.wait_ge(S["k_made"], 1)
                elif j == 7:
                    dve.tensor_tensor(t5[:], t6[:], t5[:], ALU.subtract) \
                        .then_inc(S["decay_prev"], 1)
                elif j == 8:
                    link(dve.tensor_tensor(t7[:], z2[:, 0:8], z2[:, 8:16], ALU.mult))
                    dve.wait_ge(S["decay_exp"], 1)
                    dve.wait_ge(S["b_made"], 1)
                    dve.scalar_tensor_tensor(out=fa, in0=fa, scalar=-1.0, in1=f5, op0=ALU.mult,
                                             op1=ALU.mult).then_inc(S["a_made"], 1)
                elif j == 9:
                    for t in range(8):
                        dve.tensor_scalar(t7[:, t], t7[:, t], col(c_rk + t), None, ALU.mult) \
                            .then_inc(S["bo_scaled"], 1)
                    dve.wait_ge(S["decay_exp"], 2)
                    dve.tensor_tensor(rk_b[:], rk_b[:], t5[:], ALU.mult).then_inc(S["bk_made"], 1)
                    dve.tensor_tensor(z2[:, 8:16], z2[:, 8:16], t5[:], ALU.mult) \
                        .then_inc(S["bk_made"], 1)
                elif j == 10:
                    dve.wait_ge(S["decay_exp"], 3)
                    link(dve.tensor_copy(M["wc"][:], t5[:].rearrange("p a (c t) -> p a c t", t=RC)
                                         [:, :, :, RC - 1]))
                    link(dve.tensor_tensor(z2[:, 0:8], z2[:, 0:8], t5[:], ALU.mult))
            dve.wait_ge(S["bo_made"], 8)
            dve.sem_inc(S["rpre_over"], 1)
            fs, mt, st, ru = M["fs"], M["mt"], M["state"], M["ru"]
            dve.wait_ge(S["rpre_over"], 1)
            link(dve.memset(mt[:], 0.0))
            dve.wait_ge(S["made"], MADE_RWKV)

            def heads4(name):
                return M[name][0:RB].rearrange("s (p e) t -> s e p t", e=2)

            def mask4(name):
                m = M[name][0:RB]
                return over(over(m, 1, 2), 1, 2)

            def masked(dst, banks, at, wide, mask):
                src = psum[0:RB, banks:banks + 2, 0:2 * wide] \
                    .rearrange("s e (p w) -> s e p w", p=2)[:, :, :, at:at + RB]
                dve.tensor_tensor(heads4(dst), src, mask4(mask), ALU.mult) \
                    .then_inc(S["rw_vector"], 1)

            dve.sem_inc(S["rw_end"], 1)
            dve.sem_inc(S["rw_vector"], rw_dve.start)
            uc = u + 8 + 4 * IN2_RKV
            gate_b, gate_c = M["gate_b"], M["gate_c"]
            gc = g0 + 2 + IN2_RKV

            def conv_tail(v, q):
                dve.wait_ge(S["unit_used"], v)
                dve.wait_ge(S["cv_step"], 7 * q + 1)
                dve.tensor_tensor(gate_c[:], bank_pair(0, T2), gate_c[:], ALU.mult) \
                    .then_inc(S["evicted"], 1)
                dve.wait_ge(S["evicted"], 3 * q + (gc + 3))
                y = y_conv[:, bass.ds(2 * q, 2)]
                for k in range(3):
                    for p in range(2):
                        c = par[:, bass.ds(2 * q + (p + c_conv2 + 8 * (2 - k)), 1)]
                        yp = y_conv[:, bass.ds(2 * q + p, 1)][:, 0]
                        if k == 0:
                            dve.tensor_scalar(yp, gate_c[:, p], c, None, ALU.mult) \
                                .then_inc(S["cv_step"], 1)
                            continue
                        dve.wait_ge(S["cv_step"], 7 * q + 2 * k + p)
                        dve.scalar_tensor_tensor(out=yp[:, k:T2], in0=gate_c[:, p, 0:T2 - k],
                                                 scalar=c, in1=yp[:, k:T2], op0=ALU.mult,
                                                 op1=ALU.add).then_inc(S["cv_step"], 1)
                dve.wait_ge(S["cv_step"], 7 * q + 7)
                dve.tensor_tensor(y, y, gate_b[:], ALU.mult).then_inc(S["cv_done"], 1)

            dve.sem_inc(S["cv_done"], 1)
            with dve.Fori(0, 4) as q:
                dve.wait_ge(S["rw_end"], 3 * q + 1)
                dve.memset(st[:], 0.0).then_inc(S["rw_s"], 1)
                for tt in range(3):
                    it = 3 * q + tt
                    dve.wait_ge(*rw_pe.at("lt", it))
                    masked("ldt", 4, 0, 192, "m_ldt")
                    masked("lot", 4, 0, 192, "m_lot")
                    masked("rbt", 4, RB, 192, "m_r")
                    dve.wait_ge(*rw_pe.at("ak", it))
                    masked("akt", 6, 0, 192, "m_a")
                    masked("rkt", 6, RB, 192, "m_r")
                    dve.wait_ge(*rw_dve.at("ldt", it))
                    dve.tensor_tensor(M["p1"][0:RB], M["ldt"][0:RB], over(ident[0:RB, 0:RB], 1, 4),
                                      ALU.add).then_inc(S["rw_vector"], 1)
                    dve.wait_ge(*rw_pe.at("l", it))
                    masked("ld", 4, 0, RB, "m_ld")
                    dve.wait_ge(*rw_pe.at("l2", it))
                    dve.tensor_copy(M["l2"][0:RB], four(4)).then_inc(S["rw_vector"], 1)
                    dve.wait_ge(*rw_pe.at("l4t", it))
                    dve.tensor_copy(l4t[0:RB], four(5)).then_inc(S["rw_vector"], 1)
                    v = uc + 4 + 12 * q + 4 * tt
                    lo(v, 0)
                    dve.wait_ge(*rw_pe.at("p2m", it))
                    dve.tensor_tensor(p2[0:RB], four(7), M["p1"][0:RB], ALU.add) \
                        .then_inc(S["rw_vector"], 1)
                    dve.wait_ge(*rw_pe.at("p3m", it))
                    dve.wait_ge(*rw_dve.at("p2", it))
                    dve.tensor_tensor(p3[0:RB], four(6), p2[0:RB], ALU.add) \
                        .then_inc(S["rw_vector"], 1)
                    dve.wait_ge(*rw_pe.at("p4m", it))
                    dve.wait_ge(*rw_dve.at("p3", it))
                    dve.tensor_tensor(p4[0:RB], four(7), p3[0:RB], ALU.add) \
                        .then_inc(S["rw_vector"], 1)
                    lo(v + 1, 1)
                    dve.wait_ge(*rw_pe.at("zm", it))
                    dve.tensor_copy(zz[0:RB].rearrange("p h k -> p (h k)"),
                                    psum[0:RB, 5, 0:512]).then_inc(S["rw_vector"], 1)
                    dve.wait_ge(*rw_pe.at("xm", it))
                    dve.tensor_tensor(M["uu"][0:RB].rearrange("p a h k -> p h a k"),
                                      psum[0:RB, 6, 0:512].rearrange("p (h a k) -> p h a k", h=4,
                                                                     a=2),
                                      M["y1"][0:RB].rearrange("p h (a k) -> p h a k", a=2),
                                      ALU.add) \
                        .then_inc(S["rw_vector"], 1)
                    dve.wait_ge(*rw_pe.at("rum", it))
                    dve.tensor_tensor(ru[:], psum[:, 7, 0:192].rearrange("p (a t) -> p a t", a=2),
                                      fs[:, :, 1], ALU.add).then_inc(S["rw_vector"], 1)
                    dve.wait_ge(*rw_pe.at("mtm", it))
                    for e in range(2):
                        h = slice(64 * e, 64 * e + 64)
                        src = psum[h, 4:7, 0:256].rearrange("p c (a k) -> p c a k", a=2)[:, :, :, h]
                        dve.tensor_tensor(mt[h, :, :, h], src,
                                          over(over(ident[h, h], 1, 2), 1, 3), ALU.add) \
                            .then_inc(S["rw_vector"], 1)
                    for c in range(3):
                        dve.wait_ge(*rw_pe.at(f"step{c}", it))
                        for e in range(2):
                            h = slice(64 * e, 64 * e + 64)
                            src = psum[h, 4 + c, 0:256].rearrange("p (a k) -> p a k", a=2)[:, :, h]
                            w = M["wc"][h, bass.ds(2 * q, 2), 3 * tt + c:3 * tt + c + 1]
                            dve.tensor_tensor(st[h, :, h], src, w.to_broadcast([64, 2, 64]),
                                              ALU.mult).then_inc(S["rw_s"], 1)
                    dve.tensor_copy(rk_a[:, bass.ds(2 * q, 2), RB * tt:RB * tt + RB],
                                    psum[:, 7, 256:448].rearrange("p (a t) -> p a t", a=2)) \
                        .then_inc(S["rw_end"], 1)
                    lo(v + 2, 2)
                    lo(v + 3, 3)
                    if tt == 0:
                        dve.wait_ge(S["cv_done"], q + 1)
                        leave(v, 0, gate_b[:], T2)
                    elif tt == 1:
                        leave(v, 0, gate_c[:], T2)
                        dve.wait_ge(S["evicted"], gc + 3 * q + 2)
                        dve.tensor_tensor(gate_c[:], gate_c[:], over(rstd[:], 1, 2), ALU.mult) \
                            .then_inc(S["cv_step"], 1)
                    else:
                        conv_tail(v, q)
            t8, mixed = M["t8"], M["mixed"]
            u, g0 = stream.unit0["out2"], stream.group0["out2"]
            dve.wait_ge(S["mix_hi"], 4)
            dve.tensor_tensor(act_lo[:, 0:8], y_conv, act_hi[:, 0:8].bitcast(F32),
                              ALU.subtract).then_inc(S["mix_lo"], 1)
            dve.wait_ge(S["rw_end"], 13)
            for j in range(8):
                dve.wait_ge(S["gn_mean"], j + 1)
                ya = rk_a[:, j, PAD:RT]
                dve.scalar_tensor_tensor(out=ya, in0=psum[:, 4 + j % 4, 0:T2], scalar=-1.0 / 64,
                                         in1=ya, op0=ALU.mult, op1=ALU.add) \
                    .then_inc(S["gn_centred"], 1)

            def out_half(n, next_units, how):
                leave(u + 2 * n + 2, (g0 + n) % 2, mixed[:, 2 * (n % 8):2 * (n % 8) + 2, TC3],
                      T3, how=how)
                for k in range(2):
                    lo(next_units + k, 2 * (n % 2) + k)

            out_half(0, u + 4, "copied")
            out_half(1, u + 6, "copied")
            for j in range(8):
                dve.wait_ge(S["gn_ss"], j + 1)
                dve.tensor_scalar(t8[:, j], psum[:, 4 + j % 4, 0:RT], 1.0 / 64, GN_EPS, ALU.mult,
                                  ALU.add).then_inc(S["gn_used"], 1)
            dve.wait_ge(S["gn_used"], 8)
            out_half(2, u + 8, "copied")
            out_half(3, u + 10, "copied")
            dve.wait_ge(S["gn_root"], 2)
            link(dve.tensor_tensor(rk_a[:], rk_a[:], t8[:], ALU.mult))
            out_half(4, u + 12, "copied")
            for j in range(8):
                link(dve.tensor_scalar(rk_a[:, j], rk_a[:, j], col(c_lnw + j), col(c_lnb + j),
                                       ALU.mult, ALU.add))
            out_half(5, u + 14, "copied")
            dve.wait_ge(S["bonus_made"], 1)
            link(dve.tensor_tensor(rk_a[:], rk_a[:], bonus[:], ALU.add))
            for j in range(8):
                dve.wait_ge(S["gate_made"], j + 1)
                dve.tensor_tensor(rk_a[:, j, PAD:RT], rk_a[:, j, PAD:RT],
                                  psum[:, 4 + j % 4, 0:T2], ALU.mult).then_inc(S["gn_done"], 1)
            dve.wait_ge(S["gn_done"], 8)
            dve.wait_ge(S["mix_hi"], 5)
            dve.tensor_tensor(act_lo[:, 8:16], rk_a[:, :, PAD:RT], act_hi[:, 8:16].bitcast(F32),
                              ALU.subtract).then_inc(S["mix_lo"], 1)
            out_half(6, u + 16, "copied")
            out_half(7, u + 18, "copied")
            with dve.Fori(0, 3) as i:
                for b in range(2):
                    leave(u + 4 * i + (18 + 2 * b), (g0 + b) % 2,
                          mixed[:, bass.ds(4 * i + 2 * b, 2), TC3], T3, how="added")
                    for k in range(2):
                        lo(u + 4 * i + (20 + 2 * b + k), 2 * b + k)
            for b in range(2):
                leave(u + 30 + 2 * b, (g0 + b) % 2, mixed[:, 12 + 2 * b:14 + 2 * b, TC3], T3,
                      how="added")
                for k in range(2):
                    lo(stream.unit0["ffn2"] + 2 * b + k, 2 * b + k)

            def post(c, tc, k):
                m = mixed[:, k, tc]
                dve.scalar_tensor_tensor(out=m, in0=m, scalar=col(c + k),
                                         in1=rstd[:, 0:tc.stop - tc.start], op0=ALU.mult,
                                         op1=ALU.mult).then_inc(S["post_scaled"], 1)

            rstd_of("n3", T3, D, EPS)
            dve.wait_ge(S["evicted"], stream.group0["ffn2"])
            for k in range(KD + 3):
                if k < KD:
                    post(c_postmix, TC3, k)
                if k >= 3:
                    norm_lo("n4", c_preffn, TC3, (k - 3,))
            dve.wait_ge(S["post"], KD)
            link(dve.memset(mixed[:], 0.0))
            ffn("ffn2", "n4", LEAD, c_gconv, False, mixed, lambda d: None)
            rstd_of("n5", T1, D, EPS)
            dve.wait_ge(S["evicted"], stream.groups)
            for k in range(KD):
                post(c_postffn, TC1, k)
            for n in range(8):
                g, tt = divmod(n, 2)
                dve.wait_ge(S["out_turned"], n + 1)
                dve.tensor_copy(M["out_rows"][:, tt, 512 * g:512 * g + 512], psum[:, 4 + n % 4]) \
                    .then_inc(S["out_copied"], 1)

        @block.tensor
        def _(pe):
            def unit(u, slot, pair, hi_, lo_, k0, T, first, last, m=P, ncol=2, shift=P):
                pe.wait_ge(S["lo_done"], u + 1)
                for r in range(RK):
                    mm = unit_row(slot, pair, hi_, lo_, k0, T, first, last, r, m, ncol, shift)
                mm.then_inc(S["unit_used"], 1)

            def unit_row(slot, pair, hi_, lo_, k0, T, first, last, r, m=P, ncol=2, shift=P):
                for c in range(ncol):
                    out_ = psum[0:m, 2 * pair + c, 0:T]
                    at = 256 * r + shift * c
                    wh, wl = w_hi[:, slot, at:at + m], w_lo[:, slot, at:at + m]
                    xh, xl = hi_[:, k0 + r], lo_[:, k0 + r]
                    pe.matmul(out_, wh, xh, start=first and r == 0, stop=False)
                    pe.matmul(out_, wh, xl, start=False, stop=False)
                    mm = pe.matmul(out_, wl, xh, start=False, stop=last and r == RK - 1)
                return mm

            def bank_free(g):
                if not isinstance(g, int) or g >= 2:
                    pe.wait_ge(S["evicted"], g - 1)

            def out_units(u, g, tc, T, half, out_pair0):
                for b in range(2):
                    half_group(u + 2 * b, g + b, b, tc, T, half, out_pair0)

            def half_group(u, g, b, tc, T, half, out_pair0):
                bank_free(g)
                for j in range(2):
                    unit(u + j, 2 * b + j, (out_pair0 + b) % 2, act_hi[:, :, tc],
                         act_lo[:, :, tc], 8 * half + 4 * j, T, j == 0, j == 1)

            def group(u, g, pair, tc, T, ready=None, **how):
                bank_free(g)
                for j in range(4):
                    if ready:
                        pe.wait_ge(*ready(j))
                    unit(u + j, j, pair, act_hi[:, :, tc], act_lo[:, :, tc], 4 * j, T,
                         j == 0, j == 3, **how)

            def group_with_sum(name, u, g, pair, tc, T, **how):
                bank_free(g)
                for j in range(4):
                    if j == 2:
                        sum_over(name, T)
                    unit(u + j, j, pair, act_hi[:, :, tc], act_lo[:, :, tc], 4 * j, T,
                         j == 0, j == 3, **how)

            def sum_over(name, T):
                pe.wait_ge(*norm_at(name, "add", 5))
                pe.matmul(psum[:, 7, 0:T], ones[:], ss_part[:, 0:T], start=True, stop=True) \
                    .then_inc(S["norm_ss"], 1)

            pe.wait_ge(S["made"], MADE_CONSTS)
            pe.wait_ge(S["x_landed"], 48)
            for n in range(8):
                tt, g = divmod(n, 4)
                if n >= 4:
                    pe.wait_ge(S["x_placed"], n - 3)
                for k in range(4):
                    c = P * (4 * g + k)
                    mm = pe.transpose(psum[:, 4 + n % 4, P * k:P * k + P],
                                      M["x_rows"][:, tt, c:c + P], ident[:])
                mm.then_inc(S["x_turned"], 1)
            pe.wait_ge(S["x_placed"], 5)
            for k in range(KD):
                mm = pe.transpose(psum[:, 4, T0 * k:T0 * k + T0],
                                  M["meta_rows"][0:T0, P * k:P * k + P], ident[0:T0, 0:T0])
            mm.then_inc(S["x_turned"], 1)
            pe.wait_ge(S["x_placed"], 7)
            pe.wait_ge(S["first_params"], 16 * n_param_loads["first_params"])
            pe.wait_ge(S["d_placed"], 1)
            pe.transpose(psum[:, 5, 0:P], M["packs"][:, 0], ident[:]) \
                .then_inc(S["par_turned"], 1)
            u = stream.unit0["in1"]
            group(u, 0, 0, TC1, T1, lambda j: norm_at("n0", "lo", 4 * j + 4))
            pe.wait_ge(S["par_placed"], 1)
            pe.wait_ge(S["params_landed"], 16 * n_param_loads["params_landed"])
            for n in range(1, NPACK):
                mm = pe.transpose(psum[:, 6, P * (n - 1):P * n] if n < 5 else
                                  psum[:, 5, P * (n - 4):P * (n - 3)], M["packs"][:, n], ident[:])
            mm.then_inc(S["par_turned"], 1)
            group_with_sum("n0", u + 4, 1, 1, TC1, T1)
            for g in range(2, 5):
                group(u + 4 * g, g, g % 2, TC1, T1)
            pe.sem_inc(S["qk_ss"], 1)
            with pe.Fori(0, 4) as n:
                pe.wait_ge(S["qk_sq"], n + 1)
                pe.wait_ge(S["qk_inv"], n + 1)
                for k in range(2):
                    mm = pe.matmul(psum[:, 4 + k], ones[:],
                                   M["head_sq"][:, 2 * k:2 * k + 2].rearrange("p a t -> p (a t)"),
                                   start=True, stop=True)
                mm.then_inc(S["qk_ss"], 1)
                group(u + 20 + 8 * n, 2 * n + 5, 1, TC1, T1)
                group(u + 24 + 8 * n, 2 * n + 6, 0, TC1, T1)
            pe.sem_inc(S["at_scored"], 2)
            pe.sem_inc(S["at_v_turned"], 2)
            pe.sem_inc(S["at_p_turned"], 2)
            pe.sem_inc(S["at_out"], 2)
            pe.wait_ge(S["qk_done"], 4)
            with pe.Fori(0, 4) as i:
                for b in range(2):
                    h = 2 * i + b
                    qs, vs = M["q_still"][:, b], M["v_still"][:, b]
                    pe.wait_ge(S["at_still"], 2 * h + 2)
                    pe.wait_ge(S["at_done"], h + 1)
                    kt = proj[:, bass.ds(h + 8, 1)][:, 0]
                    pe.matmul(psum[:, 4 + b, 0:P], qs[:, 0:P], kt[:, 0:P], start=True, stop=True)
                    pe.matmul(psum[:, 4 + b, P:384], qs[:, P:256], kt, start=True, stop=True) \
                        .then_inc(S["at_scored"], 1)
                    pe.wait_ge(S["at_pt"], h + 1)
                    pe.transpose(psum[:, 6 + b, 0:P], vs[:, 0:P], ident[:])
                    pe.transpose(psum[:, 6 + b, P:256], vs[:, P:256], ident[:]) \
                        .then_inc(S["at_v_turned"], 1)
                group(u + 52 + 8 * i, 2 * i + 13, 1, TC1, T1)
                for b in range(2):
                    h = 2 * i + b
                    pe.wait_ge(S["at_probs"], 2 * h + 2)
                    pe.wait_ge(S["at_v"], h + 1)
                    for k in range(3):
                        mm = pe.transpose(psum[:, 6 + b, P * k:P * k + P],
                                          M["scores"][:, b, P * k:P * k + P], ident[:])
                    mm.then_inc(S["at_p_turned"], 1)
                bank_free(2 * i + 14)
                in_units = [(u + 56 + 8 * i + j, j, 0, act_hi[:, :, TC1], act_lo[:, :, TC1], 4 * j,
                             T1, j == 0, j == 3) for j in range(4)]
                unit(*in_units[0])
                unit(*in_units[1])
                for b in range(2):
                    h = 2 * i + b
                    pe.wait_ge(S["at_pt"], h + 3)
                    vr, pt = M["v_rows"][:, b], M["probs_t"][:, b]
                    pe.matmul(psum[:, 4 + b, 0:P], vr[:, 0:P], pt[:, 0:P], start=True, stop=True)
                    pe.matmul(psum[:, 4 + b, P:256], vr[:, 0:P], pt[:, P:256],
                              start=True, stop=False)
                    pe.matmul(psum[:, 4 + b, P:256], vr[:, P:256], pt[:, 256:384],
                              start=False, stop=True) \
                        .then_inc(S["at_out"], 1)
                unit(*in_units[2])
                unit(*in_units[3])
            group(u + 84, 21, 1, TC1, T1)
            group(u + 4 * G_IN1, G_IN1, G_IN1 % 2, TC1, T1, ncol=1)
            step = M["step"]
            uo, go = stream.unit0["out1"], stream.group0["out1"]
            pe.wait_ge(S["mix_lo"], 1)
            for j in range(2):
                out_units(uo + 4 * j, go + 2 * j, TC1, T1, 0, go % 2)
            pe.wait_ge(S["attention_over"], 1)
            pe.wait_ge(S["dt_cum"], 2)
            pe.wait_ge(*ssd_dve.at("dt_w"))
            for k, (row, at) in enumerate(((5, 0), (5, P), (3, 0), (3, P), (6, 0))):
                mm = pe.transpose(psum[:, 4, 16 * k:16 * k + 16], step[0:16, row, at:at + P],
                                  ident[0:16, 0:16])
            mm.then_inc(S["ssd_tensor"], 1)
            pe.wait_ge(S["sc_silu"], 12)
            for g in range(2):
                for c in range(2):
                    cs = slice(c * CH, c * CH + CH)
                    mm = pe.matmul(psum[:, 5, P * (2 * g + c):P * (2 * g + c) + P],
                                   proj[:, 40 + g, cs], proj[:, 42 + g, cs], start=True, stop=True)
            mm.then_inc(S["ssd_tensor"], 1)
            for g in range(2):
                mm = pe.transpose(psum[:, 6, P * g:P * g + P], proj[:, 40 + g, 0:P], ident[:])
            mm.then_inc(S["ssd_tensor"], 1)
            for n in range(4):
                c, half = divmod(n, 2)
                bank = (7, 4, 5, 6)[n]
                if n:
                    pe.wait_ge(*ssd_dve.at(("dt_rows", "cb_masked", "b_placed")[n - 1]))
                for k in range(4):
                    mm = pe.transpose(psum[:, bank, P * k:P * k + P],
                                      proj[:, 32 + 4 * half + k, c * CH:c * CH + CH], ident[:])
                mm.then_inc(S["xs_turned"], 1)
            pe.wait_ge(*ssd_dve.at("b_placed"))
            pe.wait_ge(S["xdt_made"], 6)
            for g in range(2):
                pe.matmul(psum[:, 7 - 3 * g], M["b_rows"][:, g], M["xdte"][:, 512 * g:512 * g + 512],
                          start=True, stop=True).then_inc(S["st_made"], 1)
            pe.wait_ge(S["st_placed"], 2)

            def rows_out(n):
                pe.wait_ge(S["sg_diag"], n + 1)
                if n >= 2:
                    pe.wait_ge(S["sg_seg"], 2 * n - 2)
                    if n % 2:
                        pe.wait_ge(S["sg_e1"], (n - 1) // 2)
                pe.matmul(psum[:, 4 + n % 2], ones[0:16, :], M["diag"][0:16, n % 2],
                          start=True, stop=True).then_inc(S["sg_row"], 1)

            rows_out(0)
            for n in range(8):
                hb, c = divmod(n, 2)
                if n % 2:
                    half_group(uo + n + 7, go + 4 + n // 2, n // 2 % 2, TC1, T1, 0, go % 2)
                if n < 7:
                    rows_out(n + 1)
                pe.wait_ge(S["sg_g"], n + 1)
                if c:
                    pe.wait_ge(S["sg_cte"], hb + 1)
                elif hb >= 2:
                    pe.wait_ge(S["y_gated"], hb - 1)
                for k in range(4):
                    h = 4 * hb + k
                    e, p = h % 2, (h // 2) % 2
                    at = 256 * p + CH * c
                    out_ = psum[64 * e:64 * e + 64, 6 + hb % 2, at:at + CH]
                    mm = pe.matmul(out_, M["xdt"][:, c, 64 * h:64 * h + 64],
                                   M["gmat"][:, n % 2, CH * k:CH * k + CH], start=True, stop=not c)
                    if c:
                        mm = pe.matmul(out_, M["state0"][:, h // 8, 64 * (h % 8):64 * (h % 8) + 64],
                                       M["cte"][:, 1, CH * k:CH * k + CH], start=False, stop=True)
                mm.then_inc(S["sg_used"], 1)
            for g in range(2):
                pe.wait_ge(S["yn_sq"], g + 1)
                for k in range(4):
                    mm = pe.matmul(psum[:, 4 + g, 0:T1], ones[:], y_sq[:, k],
                                   start=(k == 0), stop=(k == 3))
                mm.then_inc(S["yn_ss"], 1)
            u, g0 = stream.unit0["out1"], stream.group0["out1"]
            pe.wait_ge(S["mix_lo"], 3)
            with pe.Fori(0, 4) as i:
                out_units(u + 4 * i + 16, g0 + 2 * i + 8, TC1, T1, 1, g0 % 2)

            def ffn(name, norm, T, tc):
                u, g0, n0 = stream.unit0[name], stream.group0[name], chunks_before[name]
                pair0 = g0 % 2

                def ups(v, g):
                    for j in range(4):
                        group(v + 4 * j, g + j, (pair0 + j) % 2, tc, T)

                def downs(v, g, i, hi_, lo_):
                    pe.wait_ge(S["ff_fflo"], i + (n0 + 1))
                    for d in range(8):
                        bank_free(g + d)
                        unit(v + d, d % 4, (pair0 + d) % 2, hi_, lo_, 0, T1, True, True)

                group(u, g0, pair0, tc, T, lambda j: norm_at(norm, "lo", 4 * j + 4))
                group_with_sum(norm, u + 4, g0 + 1, (pair0 + 1) % 2, tc, T)
                for j in range(2, 4):
                    group(u + 4 * j, g0 + j, (pair0 + j) % 2, tc, T)
                with pe.Fori(1, FCH) as i:
                    ups(u + 24 * i - 8, 12 * i - 8 + g0)
                    downs(u + 24 * i + 8, 12 * i - 4 + g0, i - 1, M["ff_hi"],
                          M["ff_lo"])
                downs(u + 24 * FCH - 8, g0 + 12 * FCH - 8, FCH - 1, M["last_hi"],
                      M["last_lo"])

            ffn("ffn1", "n1", T1, TC1)
            u, g0 = stream.unit0["in2"], stream.group0["in2"]
            group(u, g0, g0 % 2, TC2, T2, lambda j: norm_at("n2", "lo", 4 * j + 4), m=96, shift=96)
            group_with_sum("n2", u + 4, g0 + 1, (g0 + 1) % 2, TC2, T2)
            low, t7, rk_a = M["low"], M["t7"], M["rk_a"]

            def low_up(n0):
                for n in range(n0, n0 + 8):
                    if n >= 4:
                        pe.wait_ge(S["low_out"], n - 3)
                    j = n % 8
                    pe.matmul(psum[:, 4 + n % 4, 0:T2], M["w_low"][0:96, n // 8, P * j:P * j + P],
                              low[0:96, n // 8, PAD:RT], start=True, stop=True) \
                        .then_inc(S["low_up"], 1)

            for j in range(12):
                group(u + 8 + 4 * j, g0 + 2 + j, (g0 + j) % 2, TC2, T2)
                if j == 1:
                    pe.wait_ge(S["low_landed"], 32)
                    pe.wait_ge(S["low_act"], 1)
                    low_up(0)
                elif j == 2:
                    low_up(8)
                elif j == 4:
                    pe.wait_ge(S["kk_sq"], 1)
                    pe.wait_ge(S["low_out"], 16)
                    for t in range(8):
                        if t >= 4:
                            pe.wait_ge(S["kk_max"], t - 3)
                        pe.matmul(psum[:, 4 + t % 4, 0:RT], halves[:], t7[:, t], start=True,
                                  stop=True).then_inc(S["kk_ss"], 1)
                elif j == 10:
                    pe.wait_ge(S["kk_max"], 8)
                    for t in range(8):
                        pe.wait_ge(S["bo_scaled"], t + 1)
                        if t >= 4:
                            pe.wait_ge(S["bo_made"], t - 3)
                        pe.matmul(psum[:, 4 + t % 4, 0:T2], halves[:], t7[:, t, PAD:RT],
                                  start=True, stop=True).then_inc(S["bo_sum"], 1)
            fs, uu, mt, st = M["fs"], M["uu"], M["mt"], M["state"]
            b_tok, kv, ru = M["b_tok"], M["kv_tok"], M["ru"]
            halfp = [slice(64 * e, 64 * e + 64) for e in range(2)]

            def each_head(lhs, rhs_, bank, wide=RB):
                for h in range(4):
                    mm = pe.matmul(psum[0:RB, bank, wide * h:wide * h + wide], lhs[0:RB, h],
                                   rhs_(h), start=True, stop=True)
                mm.then_inc(S["rw_tensor"], 1)

            uc, gc = u + 8 + 4 * IN2_RKV, g0 + 2 + IN2_RKV
            pe.wait_ge(S["bo_made"], 8)
            with pe.Fori(0, 4) as q:
                with pe.Fori(0, 3) as tt:
                    it = 3 * q + tt
                    n = it + 1
                    v, vg = uc + 12 * q + 4 * tt, gc + 3 * q + tt

                    def conv_rows(*ks):
                        for k in ks:
                            j, r = divmod(k, RK)
                            if r == 0:
                                pe.wait_ge(S["lo_done"], v + j + 1)
                            mm = unit_row(j, 0, act_hi, act_lo, 4 * j, T2, j == 0, j == 3, r)
                            if r == RK - 1:
                                mm.then_inc(S["unit_used"], 1)

                    pe.wait_ge(S["rw_end"], n)
                    pe.wait_ge(S["rw_still"], 3 * it + 3)
                    pe.wait_ge(S["rw_still_act"], 2 * it + 2)
                    for k, bank in ((2, 4), (3, 6)):
                        for p in range(2):
                            for e in range(2):
                                mm = pe.matmul(psum[0:RB, bank + e, 192 * p:192 * p + 192],
                                               fs[halfp[e], p, k], fs[halfp[e], p, 0:2],
                                               start=True, stop=True)
                        mm.then_inc(S["rw_tensor"], 1)
                    pe.wait_ge(S["evicted"], vg)
                    conv_rows(0, 1)
                    pe.wait_ge(*rw_dve.at("rbt", it))
                    for p in range(2):
                        for e in range(2):
                            mm = pe.matmul(psum[0:RB, 4 + e, RB * p:RB * p + RB],
                                           fs[halfp[e], p, 0], fs[halfp[e], p, 2],
                                           start=True, stop=True)
                    mm.then_inc(S["rw_tensor"], 1)
                    conv_rows(2)
                    pe.wait_ge(*rw_dve.at("rkt", it))
                    for ks, bank in (((0, 2), 6), ((3, 4), 7)):
                        for a, k in enumerate(ks):
                            for p in range(2):
                                at = P * (2 * a + p)
                                mm = pe.transpose(psum[0:RB, bank, at:at + P], fs[:, p, k],
                                                  ident[:])
                        mm.then_inc(S["rw_tensor"], 1)
                    conv_rows(3)
                    pe.wait_ge(*rw_dve.at("ld", it))
                    each_head(M["ldt"], lambda h: M["ld"][0:RB, h], 4)
                    each_head(M["ld"], lambda h: M["ldt"][0:RB, h], 5)
                    conv_rows(4)
                    pe.wait_ge(*rw_act.at("b_tok", it))
                    pe.wait_ge(*rw_act.at("kv", it))
                    each_head(M["akt"], lambda h: kv[0:RB, 1, 64 * h:64 * h + 64], 6, 64)
                    conv_rows(5)
                    pe.wait_ge(*rw_dve.at("l2_out", it))
                    pe.wait_ge(*rw_act.at("l2t_out", it))
                    pe.wait_ge(*rw_dve.at("p1", it))
                    each_head(M["l2t"], lambda h: M["l2"][0:RB, h], 4)
                    each_head(M["l2"], lambda h: M["l2t"][0:RB, h], 5)
                    each_head(M["l2"], lambda h: M["p1"][0:RB, h], 7)
                    conv_rows(6, 7)
                    pe.wait_ge(*rw_act.at("l4_out", it))
                    pe.wait_ge(*rw_dve.at("l4t_out", it))
                    each_head(l4t, lambda h: l4[0:RB, h], 4)
                    conv_rows(8)
                    pe.wait_ge(*rw_dve.at("p2", it))
                    pe.wait_ge(*rw_act.at("rhs_v", it))
                    each_head(l4, lambda h: p2[0:RB, h], 6)
                    conv_rows(9)
                    pe.wait_ge(*rw_act.at("l8_out", it))
                    pe.wait_ge(*rw_dve.at("p3", it))
                    each_head(l8, lambda h: p3[0:RB, h], 7)
                    conv_rows(10)
                    pe.wait_ge(*rw_dve.at("p4", it))
                    each_head(p4, lambda h: M["rhs"][0:RB, h], 4, P)
                    conv_rows(11)
                    pe.wait_ge(*rw_act.at("y1_out", it))
                    each_head(M["lot"], lambda h: M["y1"][0:RB, h], 5, P)
                    conv_rows(12)
                    pe.wait_ge(*rw_dve.at("z", it))
                    each_head(p4, lambda h: zz[0:RB, h], 6, P)
                    conv_rows(13)
                    pe.wait_ge(*rw_dve.at("u", it))
                    for p in range(2):
                        for e in range(2):
                            h = 2 * p + e
                            mm = pe.matmul(psum[halfp[e], 7, RB * p:RB * p + RB],
                                           uu[0:RB, 0, h], M["rbt"][0:RB, h],
                                           start=(p == 0), stop=True, skip_group_check=True)
                    mm.then_inc(S["rw_tensor"], 1)
                    for c in range(3):
                        rows32 = slice(RC * c, RC * c + RC)
                        for p in range(2):
                            mm = pe.matmul(psum[:, 4 + c, P * p:P * p + P],
                                           uu[rows32, 0, 2 * p:2 * p + 2].rearrange("p h k -> p (h k)"),
                                           b_tok[rows32, P * p:P * p + P],
                                           start=True, stop=True)
                    mm.then_inc(S["rw_tensor"], 1)
                    conv_rows(14)
                    pe.wait_ge(*rw_dve.at("ru", it))
                    for p in range(2):
                        for e in range(2):
                            h = 2 * p + e
                            o = psum[halfp[e], 7, 256 + RB * p:256 + RB * p + RB]
                            pe.matmul(o, uu[0:RB, 1, h], M["rbt"][0:RB, h], start=(p == 0),
                                      stop=False, skip_group_check=True)
                            pe.matmul(o, kv[0:RB, 1, 64 * h:64 * h + 64], M["rkt"][0:RB, h],
                                      start=False, stop=False, skip_group_check=True)
                    conv_rows(15)
                    pe.wait_ge(*rw_dve.at("mt1", it))
                    for c in range(3):
                        rows32 = slice(RC * c, RC * c + RC)
                        for p in range(2):
                            o = psum[:, 4 + c, P * p:P * p + P]
                            pe.matmul(o, b_tok[rows32, P * p:P * p + P],
                                      uu[rows32, 1, 2 * p:2 * p + 2], start=(p == 0),
                                      stop=False, skip_group_check=True)
                            pe.matmul(o, kv[rows32, 0, P * p:P * p + P],
                                      kv[rows32, 1, P * p:P * p + P], start=False, stop=False,
                                      skip_group_check=True)
                        pe.wait_ge(S["rw_s"], 19 * q + 1 + 6 * tt + 2 * c)
                        for p in range(2):
                            at = 256 + RB * p + RC * c
                            pe.matmul(psum[:, 7, at:at + RC], st[:, p],
                                      ru[:, p, RC * c:RC * c + RC], start=False, stop=True,
                                      skip_group_check=True)
                        for p in range(2):
                            mm = pe.matmul(psum[:, 4 + c, P * p:P * p + P], mt[:, c, p], st[:, p],
                                           start=False, stop=True, skip_group_check=True)
                        mm.then_inc(S["rw_tensor"], 1)
            t8 = M["t8"]
            u, g0 = stream.unit0["out2"], stream.group0["out2"]
            pe.wait_ge(S["rw_end"], 13)
            for j in range(8):
                if j >= 4:
                    pe.wait_ge(S["gn_centred"], j - 3)
                pe.matmul(psum[:, 4 + j % 4, 0:T2], halves[:], rk_a[:, j, PAD:RT], start=True,
                          stop=True).then_inc(S["gn_mean"], 1)
            pe.wait_ge(S["mix_lo"], 4)
            out_units(u, g0, TC3, T3, 0, g0 % 2)
            pe.wait_ge(S["gn_sq"], 1)
            for j in range(8):
                if j >= 4:
                    pe.wait_ge(S["gn_used"], j - 3)
                pe.matmul(psum[:, 4 + j % 4, 0:RT], halves[:], t8[:, j], start=True, stop=True) \
                    .then_inc(S["gn_ss"], 1)
            out_units(u + 4, g0 + 2, TC3, T3, 0, g0 % 2)
            out_units(u + 8, g0 + 4, TC3, T3, 0, g0 % 2)
            pe.wait_ge(S["gup_landed"], 16)
            for j in range(8):
                if j >= 4:
                    pe.wait_ge(S["gn_done"], j - 3)
                for k in range(2):
                    mm = pe.matmul(psum[:, 4 + j % 4, 0:T2], M["g_up"][:, k, P * j:P * j + P],
                                   low[:, 2 + k, PAD:RT], start=(k == 0), stop=(k == 1))
                mm.then_inc(S["gate_made"], 1)
            out_units(u + 12, g0 + 6, TC3, T3, 0, g0 % 2)
            pe.wait_ge(S["mix_lo"], 5)
            with pe.Fori(0, 4) as i:
                out_units(u + 4 * i + 16, g0 + 2 * i + 8, TC3, T3, 1, g0 % 2)
            sum_over("n3", T3)
            ffn("ffn2", "n4", T3, TC3)
            sum_over("n5", T1)
            for n in range(8):
                g, tt = divmod(n, 2)
                if n == 3:
                    pe.wait_ge(*norm_at("n5", "ms", 1))
                if n >= 4:
                    pe.wait_ge(S["out_copied"], n - 3)
                pe.wait_ge(S["post"], KD + 4 * g + 4)
                for k in range(4):
                    mm = pe.transpose(psum[:, 4 + n % 4, P * k:P * k + P],
                                      resid[:, 4 * g + k, T0 + P * tt:T0 + P * tt + P], ident[:])
                mm.then_inc(S["out_turned"], 1)


_INS = [
    "x", "norm1_w", "w_in", "q_norm_w", "k_norm_w", "ssm_conv_w", "ssm_conv_b", "dt_bias", "a_log",
    "d_skip", "ssm_norm_w", "w_out", "norm2_w", "w_up", "ffn_conv_w", "ffn_conv_b", "w_down",
    "meta_tokens_2", "g_pre_mix_2", "w_in_2", "conv_w_2", "mu_rwkv_2", "w_decay_up_2", "w0_2",
    "a_up_2", "a0_2", "g_up_2", "k_k_2", "k_a_2", "r_k_2", "ln_x_w_2", "ln_x_b_2", "w_out_2",
    "g_post_mix_2", "g_pre_ffn_2", "w_gate_up_2", "conv_ffn_2", "w_down_2", "g_post_ffn_2",
]


def kernel(**inputs):
    import numpy as np
    from concourse import bacc
    from concourse.bass_utils import run_bass_kernel_spmd

    nc = bacc.Bacc("TRN2", target_bir_lowering=False, num_devices=1)
    arrays, args = {}, []
    for name in _INS:
        a = np.ascontiguousarray(inputs[name])
        arrays[f"in_{name}"] = a
        args.append(nc.dram_tensor(f"in_{name}", a.shape, mybir.dt.from_np(a.dtype),
                                   kind="ExternalInput").ap())
    x = arrays["in_x"]
    out = nc.dram_tensor("out_x", x.shape, mybir.dt.from_np(x.dtype), kind="ExternalOutput").ap()
    two_blocks(nc, *args, out)
    got = run_bass_kernel_spmd(nc, [arrays], core_ids=[0])
    return got.results[0]["out_x"]
```
